# Optimizing a Trainium2 kernel written in Bass

```python
import jax
import jax.numpy as jnp
from jax import lax
import numpy as np

D_MODEL = 1024
BATCH = 1
SEQ = 1024
DEPTH = 1
DEC_BATCH = 8
DEC_SEQ = 4
PAST_LEN = 8192
PAGE_SIZE = 128

NORM_EPS = 1e-5
HEAD_DIM = 64
N_Q_HEADS = 8
N_KV_HEADS = 2
Q_PER_KV = N_Q_HEADS // N_KV_HEADS
ATTN_WIDTH = N_Q_HEADS * HEAD_DIM
KV_WIDTH = N_KV_HEADS * HEAD_DIM
WINDOW = 128
ATTN_BLOCK = WINDOW
ROT_DIM = HEAD_DIM // 4
ROPE_THETA = 500000.0
ATTN_SCALE = HEAD_DIM ** -0.5
RWKV_HEADS = 8
RWKV_HEAD_DIM = 64
RWKV_WIDTH = RWKV_HEADS * RWKV_HEAD_DIM
DECAY_LORA = 32
AAA_LORA = 32
GATE_LORA = 96
GN_EPS = 64e-5
RWKV_COLS = 3 * RWKV_WIDTH + DECAY_LORA + AAA_LORA + GATE_LORA
RWKV_SPLITS = (RWKV_WIDTH, 2 * RWKV_WIDTH, 3 * RWKV_WIDTH, 3 * RWKV_WIDTH + DECAY_LORA,
               3 * RWKV_WIDTH + DECAY_LORA + AAA_LORA)
OFF_Q = 0
OFF_K = OFF_Q + ATTN_WIDTH
OFF_V = OFF_K + KV_WIDTH
OFF_B = OFF_V + KV_WIDTH
OFF_GATE = OFF_B + RWKV_COLS
IN_WIDTH = OFF_GATE + 2 * D_MODEL
N_KEYS = 128
N_EXPERTS = N_KEYS * N_KEYS
PEER_HEADS = 8
PEER_TOPK = 16
D_KEY = 256
D_KEY_HALF = D_KEY // 2
PEER_BLOCK = 128

kernel_name = "hybrid_swa_rwkv7_peer_step"

def rms_norm(x, g):
    xf = x.astype(jnp.float32)
    y = xf * lax.rsqrt(jnp.mean(xf * xf, axis=-1, keepdims=True) + NORM_EPS)
    return (y * g.astype(jnp.float32)).astype(x.dtype)

def rope_partial(x, pos):
    half = ROT_DIM // 2
    inv_freq = ROPE_THETA ** (-jnp.arange(half, dtype=jnp.float32) / half)
    ang = pos.astype(jnp.float32)[:, None] * inv_freq[None, :]
    cos = jnp.cos(ang)[:, None, :]
    sin = jnp.sin(ang)[:, None, :]
    xf = x.astype(jnp.float32)
    x1, x2, rest = xf[..., :half], xf[..., half:ROT_DIM], xf[..., ROT_DIM:]
    out = jnp.concatenate([x1 * cos - x2 * sin, x2 * cos + x1 * sin, rest], axis=-1)
    return out.astype(x.dtype)

def sink_softmax(s, sinks, mask):
    s = jnp.where(mask, s, -jnp.inf)
    sink_col = jnp.broadcast_to(sinks.astype(jnp.float32)[:, :, None, None], s.shape[:-1] + (1,))
    p = jax.nn.softmax(jnp.concatenate([s, sink_col], axis=-1), axis=-1)
    return p[..., :-1]

def window_attn_prompt(q, k, v, sinks):
    b, t = q.shape[:2]
    nb = t // ATTN_BLOCK
    qb = q.reshape(b, nb, ATTN_BLOCK, N_KV_HEADS, Q_PER_KV, HEAD_DIM)

    def band(z):
        zb = z.reshape(b, nb, ATTN_BLOCK, N_KV_HEADS, HEAD_DIM)
        prev = jnp.pad(zb, ((0, 0), (1, 0), (0, 0), (0, 0), (0, 0)))[:, :-1]
        return jnp.concatenate([prev, zb], axis=2)

    kb, vb = band(k), band(v)
    s = jnp.einsum("bnqkgd,bnskd->bnkgqs", qb, kb).astype(jnp.float32) * ATTN_SCALE
    i = jnp.arange(ATTN_BLOCK)[:, None]
    j = jnp.arange(2 * ATTN_BLOCK)[None, :]
    diff = ATTN_BLOCK + i - j
    blk = jnp.arange(nb)[:, None, None]
    mask = (diff >= 0) & (diff < WINDOW) & ((blk > 0) | (j >= ATTN_BLOCK))
    p = sink_softmax(s, sinks, mask[:, None, None])
    o = jnp.einsum("bnkgqs,bnskd->bnqkgd", p.astype(vb.dtype), vb)
    return o.reshape(b, t, ATTN_WIDTH)

def window_attn_sample(q, k, v, cache_k, cache_v, sinks):
    b, t = q.shape[:2]
    n_past = cache_k.shape[1]
    keys = jnp.concatenate([cache_k.astype(k.dtype), k], axis=1)
    vals = jnp.concatenate([cache_v.astype(v.dtype), v], axis=1)
    s = jnp.einsum("bqkgd,bskd->bkgqs", q, keys).astype(jnp.float32) * ATTN_SCALE
    i = jnp.arange(t)[:, None]
    j = jnp.arange(n_past + t)[None, :]
    diff = n_past + i - j
    mask = (diff >= 0) & (diff < WINDOW)
    p = sink_softmax(s, sinks, mask)
    o = jnp.einsum("bkgqs,bskd->bqkgd", p.astype(vals.dtype), vals).reshape(b, t, ATTN_WIDTH)
    return o, keys[:, t:], vals[:, t:]

def _wkv_step(S, inp):
    r, w, k, v, kk, bb = inp
    sa = jnp.einsum("bhij,bhj->bhi", S, kk)
    S = S * w[:, :, None, :] - sa[..., None] * bb[:, :, None, :] + v[..., None] * k[:, :, None, :]
    return S, jnp.einsum("bhij,bhj->bhi", S, r)

def rwkv7_time_mix(p, wkv0, shift0, lp):
    f32 = jnp.float32
    b, t, _ = p.shape
    prev = jnp.concatenate([shift0[:, None].astype(p.dtype), p[:, :-1]], axis=1)
    xm = p + lp["shift_mu"] * (prev - p)
    r, k, v, wl, al, gl = jnp.split(xm, RWKV_SPLITS, axis=-1)
    w_log = -jax.nn.softplus(-(lp["w0"] + jnp.tanh(wl) @ lp["w2"]).astype(f32)) - 0.5
    a = jax.nn.sigmoid((lp["a0"] + al @ lp["a2"]).astype(f32))
    g = jax.nn.sigmoid(gl) @ lp["g2"]

    def heads(z):
        return z.astype(f32).reshape(z.shape[:-1] + (RWKV_HEADS, RWKV_HEAD_DIM))

    r, k, v, a = heads(r), heads(k), heads(v), heads(a)
    decay = heads(jnp.exp(-jnp.exp(w_log)))
    kk = k * heads(lp["k_k"])
    kk = kk * lax.rsqrt(jnp.maximum(jnp.sum(kk * kk, axis=-1, keepdims=True), 1e-24))
    k = k * (1.0 + (a - 1.0) * heads(lp["k_a"]))
    xs = tuple(jnp.moveaxis(z, 1, 0) for z in (r, decay, k, v, kk, kk * a))
    wkv_t, y = lax.scan(_wkv_step, wkv0.astype(f32), xs)
    y = jnp.moveaxis(y, 0, 1)
    mean = jnp.mean(y, axis=-1, keepdims=True)
    var = jnp.mean(jnp.square(y - mean), axis=-1, keepdims=True)
    y = (y - mean) * lax.rsqrt(var + GN_EPS) * heads(lp["ln_x_w"]) + heads(lp["ln_x_b"])
    y = y + jnp.sum(r * k * lp["r_k"].astype(f32), axis=-1, keepdims=True) * v
    y = y.reshape(b, t, RWKV_WIDTH) * g.astype(f32)
    return y.astype(p.dtype), wkv_t, p[:, -1]

def peer_ffn(x, w_query, sub_keys, expert_u, expert_v):
    m = x.shape[0]
    pad = (-m) % PEER_BLOCK
    xb = jnp.pad(x, ((0, pad), (0, 0))).reshape(-1, PEER_BLOCK, D_MODEL)
    n_cand = PEER_TOPK * PEER_TOPK

    def block(xt):
        q = (xt @ w_query).reshape(PEER_BLOCK, PEER_HEADS, 2, D_KEY_HALF)
        s = jnp.einsum("thcd,hcnd->thcn", q, sub_keys).astype(jnp.float32)
        sv, si = lax.top_k(s, PEER_TOPK)
        cand_s = (sv[:, :, 0, :, None] + sv[:, :, 1, None, :]).reshape(PEER_BLOCK, PEER_HEADS, n_cand)
        cand_i = (si[:, :, 0, :, None] * N_KEYS + si[:, :, 1, None, :]).reshape(PEER_BLOCK, PEER_HEADS, n_cand)
        best_s, best_pos = lax.top_k(cand_s, PEER_TOPK)
        idx = jnp.take_along_axis(cand_i, best_pos, axis=-1)
        gate = jax.nn.softmax(best_s, axis=-1)
        u = expert_u[idx]
        v = expert_v[idx]
        act = jax.nn.gelu(jnp.einsum("thkd,td->thk", u, xt).astype(jnp.float32), approximate=False)
        return jnp.einsum("thk,thkd->td", (gate * act).astype(v.dtype), v)

    y = lax.map(block, xb)
    return y.reshape(-1, D_MODEL)[:m].astype(x.dtype)

def hybrid_layer(x, pos, lp, win_k, win_v, wkv0, shift0):
    b, t, _ = x.shape
    h = rms_norm(x, lp["norm1_g"])
    proj = h @ lp["w_in"] + lp["b_in"]
    q = rope_partial(proj[..., OFF_Q:OFF_K].reshape(b, t, N_Q_HEADS, HEAD_DIM), pos)
    k = rope_partial(proj[..., OFF_K:OFF_V].reshape(b, t, N_KV_HEADS, HEAD_DIM), pos)
    v = proj[..., OFF_V:OFF_B].reshape(b, t, N_KV_HEADS, HEAD_DIM)
    q = q.reshape(b, t, N_KV_HEADS, Q_PER_KV, HEAD_DIM)
    sinks = lp["attn_sinks"].reshape(N_KV_HEADS, Q_PER_KV)
    if win_k is None:
        att = window_attn_prompt(q, k, v, sinks)
        keep = min(WINDOW, t)
        new_k, new_v = k[:, t - keep:], v[:, t - keep:]
    else:
        att, new_k, new_v = window_attn_sample(q, k, v, win_k, win_v, sinks)
    rw, wkv_t, shift_t = rwkv7_time_mix(proj[..., OFF_B:OFF_GATE], wkv0, shift0, lp)
    gate_a = jax.nn.sigmoid(proj[..., OFF_GATE:OFF_GATE + D_MODEL])
    gate_b = jax.nn.sigmoid(proj[..., OFF_GATE + D_MODEL:])
    merged = gate_a * (att @ lp["w_up_a"]) + gate_b * (rw @ lp["w_up_b"])
    x = x + merged @ lp["w_o"]
    h2 = rms_norm(x, lp["norm2_g"]).reshape(b * t, D_MODEL)
    x = x + peer_ffn(h2, lp["w_query"], lp["sub_keys"], lp["expert_u"], lp["expert_v"]).reshape(b, t, D_MODEL)
    return x, new_k.astype(x.dtype), new_v.astype(x.dtype), wkv_t.astype(x.dtype), shift_t

def setup_inputs(seed: int = 0) -> dict:
    key = jax.random.key(seed)
    ks = iter(jax.random.split(key, 32))
    f32 = jnp.float32

    def nrm(shape, scale):
        return jax.random.normal(next(ks), shape, f32) * scale

    L = DEPTH
    win = min(WINDOW, PAST_LEN)
    return {
        "x_prompt": nrm((BATCH, SEQ, D_MODEL), 1.0),
        "x_sample": nrm((DEC_BATCH, DEC_SEQ, D_MODEL), 1.0),
        "cache_win_k": nrm((L, DEC_BATCH, win, N_KV_HEADS, HEAD_DIM), 1.0),
        "cache_win_v": nrm((L, DEC_BATCH, win, N_KV_HEADS, HEAD_DIM), 1.0),
        "state_wkv": nrm((L, DEC_BATCH, RWKV_HEADS, RWKV_HEAD_DIM, RWKV_HEAD_DIM), 0.3),
        "state_shift": nrm((L, DEC_BATCH, RWKV_COLS), 1.0),
        "norm1_g": 1.0 + nrm((L, D_MODEL), 0.05),
        "w_in": nrm((L, D_MODEL, IN_WIDTH), D_MODEL ** -0.5),
        "b_in": nrm((L, IN_WIDTH), 0.02),
        "attn_sinks": nrm((L, N_Q_HEADS), 0.5),
        "shift_mu": jax.random.uniform(next(ks), (L, RWKV_COLS), f32),
        "w0": nrm((L, RWKV_WIDTH), 0.5) - 0.5,
        "w2": nrm((L, DECAY_LORA, RWKV_WIDTH), 0.1 * DECAY_LORA ** -0.5),
        "a0": nrm((L, RWKV_WIDTH), 0.3),
        "a2": nrm((L, AAA_LORA, RWKV_WIDTH), 0.1 * AAA_LORA ** -0.5),
        "g2": nrm((L, GATE_LORA, RWKV_WIDTH), GATE_LORA ** -0.5),
        "k_k": 0.85 + nrm((L, RWKV_WIDTH), 0.05),
        "k_a": 1.0 + nrm((L, RWKV_WIDTH), 0.05),
        "r_k": nrm((L, RWKV_HEADS, RWKV_HEAD_DIM), 0.1),
        "ln_x_w": 1.0 + nrm((L, RWKV_WIDTH), 0.05),
        "ln_x_b": nrm((L, RWKV_WIDTH), 0.02),
        "w_up_a": nrm((L, ATTN_WIDTH, D_MODEL), ATTN_WIDTH ** -0.5),
        "w_up_b": nrm((L, RWKV_WIDTH, D_MODEL), RWKV_WIDTH ** -0.5),
        "w_o": nrm((L, D_MODEL, D_MODEL), D_MODEL ** -0.5),
        "norm2_g": 1.0 + nrm((L, D_MODEL), 0.05),
        "w_query": nrm((L, D_MODEL, PEER_HEADS * D_KEY), D_MODEL ** -0.5),
        "sub_keys": nrm((L, PEER_HEADS, 2, N_KEYS, D_KEY_HALF), D_KEY_HALF ** -0.5),
        "expert_u": nrm((L, N_EXPERTS, D_MODEL), D_MODEL ** -0.5),
        "expert_v": nrm((L, N_EXPERTS, D_MODEL), (PEER_HEADS * PEER_TOPK) ** -0.5),
        "final_norm_g": 1.0 + nrm((D_MODEL,), 0.05),
    }

def reference(x_prompt, x_sample, cache_win_k, cache_win_v, state_wkv, state_shift, norm1_g, w_in, b_in,
              attn_sinks, shift_mu, w0, w2, a0, a2, g2, k_k, k_a, r_k, ln_x_w, ln_x_b, w_up_a, w_up_b, w_o,
              norm2_g, w_query, sub_keys, expert_u, expert_v, final_norm_g):
    pos_p = jnp.arange(x_prompt.shape[1])
    pos_s = PAST_LEN + jnp.arange(x_sample.shape[1])
    hp, hs = x_prompt, x_sample
    pk, pv, pw, psh, sk, sv, sw, ssh = [], [], [], [], [], [], [], []
    for l in range(DEPTH):
        lp = dict(norm1_g=norm1_g[l], w_in=w_in[l], b_in=b_in[l], attn_sinks=attn_sinks[l],
                  shift_mu=shift_mu[l], w0=w0[l], w2=w2[l], a0=a0[l], a2=a2[l], g2=g2[l], k_k=k_k[l],
                  k_a=k_a[l], r_k=r_k[l], ln_x_w=ln_x_w[l], ln_x_b=ln_x_b[l], w_up_a=w_up_a[l],
                  w_up_b=w_up_b[l], w_o=w_o[l], norm2_g=norm2_g[l], w_query=w_query[l],
                  sub_keys=sub_keys[l], expert_u=expert_u[l], expert_v=expert_v[l])
        wkv0 = jnp.zeros((x_prompt.shape[0], RWKV_HEADS, RWKV_HEAD_DIM, RWKV_HEAD_DIM), jnp.float32)
        shift0 = jnp.zeros((x_prompt.shape[0], RWKV_COLS), x_prompt.dtype)
        hp, k_, v_, w_, s_ = hybrid_layer(hp, pos_p, lp, None, None, wkv0, shift0)
        pk.append(k_)
        pv.append(v_)
        pw.append(w_)
        psh.append(s_)
        hs, k_, v_, w_, s_ = hybrid_layer(hs, pos_s, lp, cache_win_k[l], cache_win_v[l], state_wkv[l],
                                          state_shift[l])
        sk.append(k_)
        sv.append(v_)
        sw.append(w_)
        ssh.append(s_)
    y_prompt = rms_norm(hp, final_norm_g)
    y_sample = rms_norm(hs, final_norm_g)
    prompt_win_k = jnp.stack(pk)
    prompt_win_v = jnp.stack(pv)
    prompt_wkv = jnp.stack(pw)
    prompt_shift = jnp.stack(psh)
    sample_win_k = jnp.stack(sk)
    sample_win_v = jnp.stack(sv)
    sample_wkv = jnp.stack(sw)
    sample_shift = jnp.stack(ssh)
    return (y_prompt, y_sample, prompt_win_k, prompt_win_v, prompt_wkv, prompt_shift, sample_win_k, sample_win_v, sample_wkv, sample_shift)


_drawn_inputs = setup_inputs


def setup_inputs(seed=0):
    import zlib

    import numpy as np

    out = dict(_drawn_inputs(seed))
    spreads = {}
    factors = {'attn_sinks': 8.0,
     'w2': 4.709,
     'k_k': 4.762,
     'ln_x_w': 3.909,
     'ln_x_b': 8.0,
     'norm2_g': 5.527}
    for name, (base, spread) in spreads.items():
        noise = np.random.default_rng([zlib.crc32(name.encode()), seed]).standard_normal(out[name].shape)
        drawn = base * np.exp(spread * noise) if base else spread * noise
        out[name] = jnp.asarray(drawn.astype(out[name].dtype))
    for name, factor in factors.items():
        out[name] = (out[name] * factor).astype(out[name].dtype)
    return out
```

```python
from contextlib import ExitStack, contextmanager

import numpy as np
import concourse.bass as bass
from concourse import mybir

ALU = mybir.AluOpType
ACT = mybir.ActivationFunctionType
AX = mybir.AxisListType
F32 = mybir.dt.float32
U32 = mybir.dt.uint32
ds = bass.ds

P = 128
D = 1024
KT = D // P
TP = 1024
NB, NS = 8, 4
TS = NB * NS
T = TP + TS
TT = (T + P - 1) // P
NC = 3
CW = T // NC
HD = 64
NQ, NKV = 8, 2
QW, KW = NQ * HD, NKV * HD
QKV = QW + 2 * KW
ROT = HD // 4
RH = ROT // 2
WIN = 128
NBLK = TP // WIN
RW = 512
NPAIR = RW // P
LW, LA, LG = 32, 32, 96
NMAIN = 3 * RW // P
OFF_B = QKV
OFF_G = OFF_B + 3 * RW + LW + LA + LG
CH = 64
LANES = 4
NQUAD = TP // CH // LANES
LEVELS = 6
PH, NKEY, TOPK = 8, 128, 16
NHALF = 2 * PH
NSLOT = PH * TOPK
WORK = (17 + LEVELS - 1) * LANES * P + LANES * CH + LANES + 6 * P
NEG = -1.0e30
EPS = 1e-5
GN_EPS = 64e-5
SCALE = HD ** -0.5


def tokens_in(tile):
    return P if tile < TP // P else TS


class Chain:

    def __init__(self, eng, sem, base=0):
        self.eng, self.sem, self.base, self.n = eng, sem, base, 0

    def __call__(self, ins):
        ins.then_inc(self.sem, 1)
        self.n += 1
        return ins

    def settle(self):
        self.eng.wait_ge(self.sem, self.base + self.n)


class Carver:

    def __init__(self, buffer):
        self.buffer, self.at = buffer, 0

    def __call__(self, *shape):
        n = int(np.prod(shape))
        part = self.buffer[:, self.at:self.at + n]
        self.at += n
        if len(shape) == 2:
            return part.rearrange("p (a b) -> p a b", a=shape[0])
        if len(shape) == 3:
            return part.rearrange("p (a b c) -> p a b c", a=shape[0], b=shape[1])
        return part


class Program:

    def __init__(self, nc, i, o):
        self.nc, self.i, self.o = nc, i, o
        self.life = ExitStack()

    def sb(self, ctx, name, shape, dt=F32):
        return ctx.enter_context(self.nc.sbuf_tensor(name, shape, dt))

    def ps(self, ctx, name, shape, dt=F32):
        return ctx.enter_context(self.nc.psum_tensor(name, shape, dt))

    def sems(self, *names):
        new = [self.held.enter_context(self.nc.semaphore(n)) for n in names]
        self.owned += new
        return new

    @contextmanager
    def stage(self):
        nc = self.nc
        with ExitStack() as self.held:
            self.owned = []
            with nc.Block() as block, ExitStack() as c:
                yield c, block
            numbers = sorted(s.num for s in self.owned)
            first = numbers[0]
            for a, b in zip(numbers, numbers[1:] + [None]):
                if b != a + 1:
                    nc.gpsimd.sem_clear(range(first, a + 1))
                    first = b
            nc.all_engine_barrier()

    def build(self, until=99):
        nc = self.nc
        dr = lambda n, s: nc.dram_tensor(n, s, F32).ap()
        self.x1_d = dr("x1_rows", [T, D])
        self.h2_d = dr("h2_rows", [T, D])
        self.s_d = dr("scores_by_unit", [TT + 1, PH, P, 2 * NKEY])
        with ExitStack() as c:
            self.ident = self.sb(c, "ident", [P, P])
            self.headones = self.sb(c, "headones", [P, P])
            self.ones = self.sb(c, "ones", [P, P])
            with ExitStack() as c1:
                self.hT = self.sb(c1, "hT", [P, KT, T])
                self.attT = self.sb(c1, "attT", [P, QW // P, T])
                with ExitStack() as c2:
                    self.mixed = self.sb(c2, "mixed", [P, NMAIN, T])
                    self.lw = self.sb(c2, "lw", [LW, T])
                    self.la = self.sb(c2, "la", [LA, T])
                    self.lg = self.sb(c2, "lg", [LG, T])
                    with ExitStack() as c3:
                        self.norm_in()
                        self.project_rwkv()
                    with ExitStack() as c3:
                        self.qkv = self.sb(c3, "qkv", [P, TT, QKV])
                        self.project_qkv()
                        if until > 1:
                            self.attention()
                    if until > 2:
                        self.rwkv()
                    if until > 3:
                        self.merge()
                    if until > 4:
                        self.output_projection()
                if until > 5:
                    self.scores()
            if until > 6:
                self.experts(0, TT - 1, P)
                self.experts(TT - 1, 1, TS)

    def norm_in(self):
        nc, i = self.nc, self.i
        with self.stage() as (c, block):
            rstd = self.sb(c, "rstd", [P, T])
            sq = self.sb(c, "sq", [P, 2, T])
            g = self.sb(c, "g1", [P, KT])
            epsc = self.sb(c, "epsc", [P, 1])
            ms = self.ps(c, "ms", [P, NC, 512])
            consts_in, g_in, eps_set, x_sq, sq_used, root, inv, normed = self.sems(
                "consts_in", "g_in", "eps_set", "x_sq", "sq_used", "root", "inv", "normed")
            x_in = self.sems(*[f"x_in{k}" for k in range(KT)])
            hT = self.hT

            @block.sync
            def _(e):
                e.dma_start(self.ones[:, :], i["ones"]).then_inc(consts_in, 16)
                e.dma_start(self.ident[:, :], i["ident"]).then_inc(consts_in, 16)
                e.dma_start(self.headones[:, :], i["headones"]).then_inc(consts_in, 16)
                for k in range(KT):
                    e.dma_start(hT[:, k, :], i["xT"][k * P:(k + 1) * P, :]).then_inc(x_in[k], 16)
                e.dma_start(g[:, :], i["norm1_g"]).then_inc(g_in, 16)

            @block.scalar
            def _(e):
                for k in range(KT):
                    e.wait_ge(x_in[k], 16)
                    if k >= 2:
                        e.wait_ge(sq_used, k - 1)
                    e.activation(sq[:, k % 2, :], hT[:, k, :], ACT.Square).then_inc(x_sq, 1)
                e.wait_ge(sq_used, KT)
                e.wait_ge(eps_set, 1)
                for n in range(NC):
                    e.activation(rstd[:, n * CW:(n + 1) * CW], ms[:, n, 0:CW], ACT.Sqrt,
                                 bias=epsc[:, 0:1], scale=1.0 / D).then_inc(root, 1)

            @block.tensor
            def _(e):
                e.wait_ge(consts_in, 48)
                for k in range(KT):
                    e.wait_ge(x_sq, k + 1)
                    for n in range(NC):
                        mm = e.matmul(ms[:, n, 0:CW], self.ones[:, :], sq[:, k % 2, n * CW:(n + 1) * CW],
                                      start=(k == 0), stop=(k == KT - 1))
                    mm.then_inc(sq_used, 1)

            @block.vector
            def _(e):
                e.memset(epsc[:, :], EPS).then_inc(eps_set, 1)
                e.wait_ge(root, NC)
                e.reciprocal(rstd[:, :], rstd[:, :]).then_inc(inv, 1)
                e.wait_ge(inv, 1)
                e.wait_ge(g_in, 16)
                for k in range(KT):
                    e.scalar_tensor_tensor(out=hT[:, k, :], in0=hT[:, k, :], scalar=g[:, k:k + 1],
                                           in1=rstd[:, :], op0=ALU.mult, op1=ALU.mult).then_inc(normed, 1)
                e.wait_ge(normed, KT)

    def project_rwkv(self):
        nc, i, o = self.nc, self.i, self.o
        hT = self.hT
        with self.stage() as (c, block):
            w = self.sb(c, "w_main", [P, 2, KT, P])
            wl = self.sb(c, "w_lora", [P, KT, LW + LA + LG])
            bias = self.sb(c, "b_main", [P, NMAIN])
            mu = self.sb(c, "mu_main", [P, NMAIN])
            sh = self.sb(c, "shift_main", [P, NMAIN, NB])
            lb = self.sb(c, "lora_bias", [LG, 3])
            lmu = self.sb(c, "lora_mu", [LG, 3])
            lsh = self.sb(c, "lora_shift", [LG, 3, NB])
            praw = self.sb(c, "praw", [P, 2, 1 + T])
            dif = self.sb(c, "dif", [P, 2, T])
            prevs = self.sb(c, "prevs", [P, 2, NB, NS])
            last = self.sb(c, "last", [P, NMAIN + 3, 1 + NB])
            lrow = self.sb(c, "lrow", [1 + NB, 3 * RW + LW + LA + LG])
            pp = [self.ps(c, f"pp{s}", [P, NC, 512]) for s in range(2)]
            pt = self.ps(c, "pt", [1 + NB, 512])
            par_in, lora_in, zeroed, prod, evac, mixstep, laststep, lrow_t, lrow_c, out_s = self.sems(
                "par_in", "lora_in", "zeroed", "prod", "evac", "mixstep", "laststep", "lrow_t", "lrow_c",
                "out_s")
            w_in = self.sems("w_in0", "w_in1")
            LORAS = [(0, LW, self.lw), (LW, LA, self.la), (LW + LA, LG, self.lg)]
            MIX = 6
            LASTS = 2

            @block.sync
            def _(e):
                for a, b in ((bias, "b_main"), (mu, "mu_main"), (sh, "shift_main"), (lb, "lora_b"),
                             (lmu, "lora_mu"), (lsh, "lora_shift")):
                    e.dma_start(a[:], i[b]).then_inc(par_in, 16)
                e.dma_start(wl[:, :, :], i["w_lora"]).then_inc(lora_in, 16)
                with e.Fori(0, NMAIN // 2) as t:
                    for s in range(2):
                        e.wait_ge(prod, 2 * t + s)
                        e.dma_start(w[:, s, :, :], i["w_main"][ds(2 * t + s, 1)].rearrange("o p k f -> (o p) k f")
                                    ).then_inc(w_in[s], 16)
                e.wait_ge(lrow_c, 1)
                e.dma_start(o["shift"], lrow[:, :]).then_inc(out_s, 16)
                e.wait_ge(out_s, 16)

            @block.tensor
            def _(e):
                e.sem_inc(prod, 1)
                with e.Fori(0, NMAIN // 2) as t:
                    for s in range(2):
                        e.wait_ge(w_in[s], 16 * (t + 1))
                        e.wait_ge(evac, NC * (2 * t + s))
                        for k in range(KT):
                            for n in range(NC):
                                mm = e.matmul(pp[s][:, n, 0:CW], w[:, s, k, :], hT[:, k, n * CW:(n + 1) * CW],
                                              start=(k == 0), stop=(k == KT - 1))
                        mm.then_inc(prod, 1)
                e.wait_ge(lora_in, 16)
                for m, (off, width, _) in enumerate(LORAS):
                    s = m % 2
                    e.wait_ge(evac, NC * (NMAIN + m))
                    for k in range(KT):
                        for n in range(NC):
                            mm = e.matmul(pp[s][0:width, n, 0:CW], wl[:, k, off:off + width],
                                          hT[:, k, n * CW:(n + 1) * CW], start=(k == 0), stop=(k == KT - 1))
                    mm.then_inc(prod, 1)
                e.wait_ge(laststep, NMAIN + 3 + 1)
                for m in range(NMAIN + 3):
                    width = P if m < NMAIN else LORAS[m - NMAIN][1]
                    off = m * P if m < NMAIN else NMAIN * P + LORAS[m - NMAIN][0]
                    if m:
                        e.wait_ge(lrow_t, m)
                    e.transpose(pt[:, 0:width], last[0:width, m, :], self.ident[0:width, 0:width]
                                ).then_inc(mixstep, 1)

            def evacuate(e, s, rows, b):
                for n in range(NC):
                    e.activation(praw[0:rows, s, 1 + n * CW:1 + (n + 1) * CW], pp[s][0:rows, n, 0:CW],
                                 ACT.Identity, bias=b).then_inc(evac, 1)

            bcol = self.sb(c, "bcol", [P, 2, 1])
            bstep, = self.sems("bstep")

            @block.scalar
            def _(e):
                e.sem_inc(evac, NC)
                e.wait_ge(par_in, 96)
                with e.Fori(0, NMAIN // 2) as t:
                    for s in range(2):
                        e.copy(bcol[:, s, :], bias[:, ds(2 * t + s, 1)]).then_inc(bstep, 1)
                        e.wait_ge(bstep, 2 * t + s + 1)
                        e.wait_ge(prod, 2 * t + s + 2)
                        e.wait_ge(laststep, 2 * t + s)
                        evacuate(e, s, P, bcol[:, s, :])
                for m in range(3):
                    s = m % 2
                    e.wait_ge(prod, NMAIN + m + 2)
                    e.wait_ge(laststep, NMAIN + m)
                    evacuate(e, s, LORAS[m][1], lb[0:LORAS[m][1], m:m + 1])

            mstep, = self.sems("mstep")

            def mix(e, ch, s, rows, shift, muc, out, lastout):
                p = praw[0:rows, s, :]
                ch(e.tensor_copy(prevs[0:rows, s, :, 0], shift))
                ch(e.tensor_copy(prevs[0:rows, s, :, 1:NS],
                                 p[:, 1 + TP:1 + T].rearrange("p (b n) -> p b n", b=NB)[:, :, 0:NS - 1]))
                ch(e.tensor_tensor(dif[0:rows, s, 0:TP], p[:, 0:TP], p[:, 1:1 + TP], ALU.subtract))
                ch.settle()
                ch(e.tensor_tensor(dif[0:rows, s, TP:T], prevs[0:rows, s, :, :].rearrange("p b n -> p (b n)"),
                                   p[:, 1 + TP:1 + T], ALU.subtract))
                ch(e.tensor_copy(lastout[:, 1:1 + NB],
                                 p[:, 1 + TP:1 + T].rearrange("p (b n) -> p b n", b=NB)[:, :, NS - 1]))
                ch(e.tensor_copy(lastout[:, 0:1], p[:, TP:TP + 1]))
                ch.settle()
                ch(e.scalar_tensor_tensor(out=out, in0=dif[0:rows, s, :], scalar=muc, in1=p[:, 1:1 + T],
                                          op0=ALU.mult, op1=ALU.add))
                ch.settle()

            mucol = self.sb(c, "mucol", [P, 2, 1])

            @block.vector
            def _(e):
                e.memset(praw[:, :, 0:1], 0.0).then_inc(zeroed, 1)
                e.wait_ge(zeroed, 1)
                e.wait_ge(par_in, 96)
                e.sem_inc(laststep, 1)
                with e.Fori(0, NMAIN // 2) as t:
                    for s in range(2):
                        ch = Chain(e, mstep, (2 * t + s) * 8)
                        ch(e.tensor_copy(mucol[:, s, :], mu[:, ds(2 * t + s, 1)]))
                        e.wait_ge(evac, NC * (2 * t + s + 2))
                        mix(e, ch, s, P, sh[:, ds(2 * t + s, 1), :].rearrange("p o b -> p (o b)"), mucol[:, s, :],
                            self.mixed[:, ds(2 * t + s, 1), :].rearrange("p o t -> p (o t)"),
                            last[:, ds(2 * t + s, 1), :].rearrange("p o b -> p (o b)"))
                        assert ch.n == 8
                        e.sem_inc(laststep, 1)
                ch = Chain(e, mstep, NMAIN * 8)
                for m, (off, width, out) in enumerate(LORAS):
                    e.wait_ge(evac, NC * (NMAIN + m + 2))
                    mix(e, ch, m % 2, width, lsh[0:width, m, :], lmu[0:width, m:m + 1], out[:, :],
                        last[0:width, NMAIN + m, :])
                    e.sem_inc(laststep, 1)
                for m in range(NMAIN + 3):
                    width = P if m < NMAIN else LORAS[m - NMAIN][1]
                    off = m * P if m < NMAIN else NMAIN * P + LORAS[m - NMAIN][0]
                    e.wait_ge(mixstep, m + 1)
                    e.tensor_copy(lrow[:, off:off + width], pt[:, 0:width]).then_inc(lrow_t, 1)
                e.wait_ge(lrow_t, NMAIN + 3)
                e.sem_inc(lrow_c, 1)

    def project_qkv(self):
        nc, i = self.nc, self.i
        hT, qkv = self.hT, self.qkv
        with self.stage() as (c, block):
            w = self.sb(c, "w_qkv", [P, KT, QKV])
            bb = self.sb(c, "b_qkv", [P, QKV])
            pq = [self.ps(c, f"pq{s}", [P, 2, 512]) for s in range(2)]
            prod, evac = self.sems("qkv_prod", "qkv_evac")
            w_in = self.sems(*[f"wq_in{k}" for k in range(KT)])
            b_in, = self.sems("bq_in")

            @block.sync
            def _(e):
                for k in range(KT):
                    e.dma_start(w[:, k, :], i["w_in"][k * P:(k + 1) * P, 0:QKV]).then_inc(w_in[k], 16)
                e.dma_start(bb[:, :], i["b_qkv"].to_broadcast([P, QKV])).then_inc(b_in, 16)

            @block.tensor
            def _(e):
                for m in range(TT):
                    n = tokens_in(m)
                    if m >= 2:
                        e.wait_ge(evac, m - 1)
                    for k in range(KT):
                        if m == 0:
                            e.wait_ge(w_in[k], 16)
                        lhsT = hT[:, k, m * P:m * P + n]
                        e.matmul(pq[m % 2][0:n, 0, :], lhsT, w[:, k, 0:QW], start=(k == 0), stop=(k == KT - 1))
                        mm = e.matmul(pq[m % 2][0:n, 1, 0:2 * KW], lhsT, w[:, k, QW:QKV],
                                      start=(k == 0), stop=(k == KT - 1))
                    mm.then_inc(prod, 1)

            @block.vector
            def _(e):
                e.wait_ge(b_in, 16)
                for m in range(TT):
                    n = tokens_in(m)
                    e.wait_ge(prod, m + 1)
                    e.tensor_tensor(qkv[0:n, m, :], pq[m % 2][0:n, :, :].rearrange("p a b -> p (a b)")[:, 0:QKV],
                                    bb[0:n, :], ALU.add).then_inc(evac, 1)
                e.wait_ge(evac, TT)


    def rope(self):
        nc, i = self.nc, self.i
        NH = NQ + NKV
        with self.stage() as (c, block):
            cs = self.sb(c, "rope_cos", [P, TT, RH])
            sn = self.sb(c, "rope_sin", [P, TT, RH])
            tmp = [self.sb(c, f"rope_t{n}", [P, TT, NH, RH]) for n in range(4)]
            tab_in, step, = self.sems("tab_in", "rope_step")

            @block.sync
            def _(e):
                e.dma_start(cs[:], i["cos"]).then_inc(tab_in, 16)
                e.dma_start(sn[:], i["sin"]).then_inc(tab_in, 16)

            @block.vector
            def _(e):
                e.wait_ge(tab_in, 32)
                ch = Chain(e, step)
                for rows, a, b in ((P, 0, TT - 1), (TS, TT - 1, TT)):
                    heads = self.qkv[0:rows, a:b, 0:NH * HD].rearrange("p m (h d) -> p m h d", h=NH)
                    x1, x2 = heads[:, :, :, 0:RH], heads[:, :, :, RH:ROT]
                    n = b - a
                    co = cs[0:rows, a:b, :].unsqueeze(2).to_broadcast([rows, n, NH, RH])
                    si = sn[0:rows, a:b, :].unsqueeze(2).to_broadcast([rows, n, NH, RH])
                    t = [z[0:rows, a:b] for z in tmp]
                    ch(e.tensor_tensor(t[0], x1, co, ALU.mult))
                    ch(e.tensor_tensor(t[1], x2, si, ALU.mult))
                    ch(e.tensor_tensor(t[2], x2, co, ALU.mult))
                    ch(e.tensor_tensor(t[3], x1, si, ALU.mult))
                    ch.settle()
                    ch(e.tensor_tensor(x1, t[0], t[1], ALU.subtract))
                    ch(e.tensor_tensor(x2, t[2], t[3], ALU.add))
                ch.settle()

    def attention(self):
        nc, i, o = self.nc, self.i, self.o
        qkv, attT, ident = self.qkv, self.attT, self.ident
        self.rope()
        G = NQ // NKV
        with self.stage() as (c, block):
            mask = self.sb(c, "band", [P, 2 * WIN])
            mcur = self.sb(c, "band_now", [P, 2 * WIN])
            sink = self.sb(c, "sinks", [P, NQ])
            qT = self.sb(c, "qT", [P, QW // P, P])
            kT = self.sb(c, "kT", [P, 2, NKV, P])
            rows = self.sb(c, "qkv_ring", [P, 2, QKV])
            sc = self.sb(c, "sc", [P, G, 2 * WIN])
            pr = self.sb(c, "probs", [P, 2, G, 2 * WIN])
            pT = self.sb(c, "probsT", [P, 4, 4 * P])
            mx = self.sb(c, "mx", [P, 2, G])
            nmx = self.sb(c, "nmx", [P, 2, G])
            sx = self.sb(c, "sx", [P, 2, G])
            es = self.sb(c, "es", [P, 2, G])
            den = self.sb(c, "den", [P, 2, G])
            att = self.sb(c, "att", [P, QW])
            psq = self.ps(c, "psq", [P, 4, P])
            psk = self.ps(c, "psk", [P, 4, P])
            pss = self.ps(c, "pss", [P, G, 2 * WIN])
            pst = [self.ps(c, f"pst{n}", [P, 4 * P]) for n in range(2)]
            pso = self.ps(c, "pso", [P, 2, G, HD])
            names = ("consts2", "kv_out", "ring0", "qk_t", "qk_c", "s_done", "s_taken", "neg", "expd", "recip",
                     "p_t", "p_c", "o_done", "o_taken", "a_t", "a_c", "vstep")
            (consts2, kv_out, ring0, qk_t, qk_c, s_done, s_taken, neg, expd, recip, p_t, p_c, o_done, o_taken,
             a_t, a_c, vstep) = self.sems(*names)
            rung, = self.sems("rung")
            NP = 2 * G // 4
            VS = 8

            @block.sync
            def _(e):
                e.dma_start(mask[:], i["band"]).then_inc(consts2, 16)
                e.dma_start(mcur[:], i["band_first"]).then_inc(consts2, 16)
                e.dma_start(sink[:], i["sinks"].to_broadcast([P, NQ])).then_inc(consts2, 16)
                e.dma_start(o["prompt_win_k"], qkv[:, TT - 2, QW:QW + KW]).then_inc(kv_out, 16)
                e.dma_start(o["prompt_win_v"], qkv[:, TT - 2, QW + KW:QKV]).then_inc(kv_out, 16)
                for name, cache, off in (("sample_win_k", "cache_k", QW), ("sample_win_v", "cache_v", QW + KW)):
                    e.dma_start(o[name][:, 0:WIN - NS, :], i[cache][:, NS:WIN, :]).then_inc(kv_out, 16)
                    for b in range(NB):
                        e.dma_start(o[name][b, WIN - NS:WIN, :], qkv[b * NS:(b + 1) * NS, TT - 1, off:off + KW]
                                    ).then_inc(kv_out, 16)
                e.wait_ge(kv_out, 16 * (4 + 2 * NB))

            @block.gpsimd
            def _(e):
                e.wait_ge(ring0, 3)
                with e.Fori(0, NBLK // 2) as t:
                    for s in range(2):
                        u = 2 * t + s
                        e.wait_ge(a_c, u)
                        e.tensor_copy(rows[:, s, :], qkv[:, ds(u, 1), :].rearrange("p o f -> p (o f)")
                                      ).then_inc(rung, 1)

            @block.tensor
            def _(e):
                e.wait_ge(ring0, 3)
                with e.Fori(0, NBLK // 2) as t:
                    for s in range(2):
                        u = 2 * t + s
                        e.wait_ge(qk_c, 2 * u)
                        e.wait_ge(s_done, 2 * u)
                        e.wait_ge(rung, u + 1)
                        row = rows[:, s, :]
                        for j in range(4):
                            e.transpose(psq[:, j, :], row[:, j * P:(j + 1) * P], ident[:, :])
                        for g in range(NKV):
                            for d in range(2):
                                mm = e.matmul(psk[d * HD:(d + 1) * HD, g, :],
                                              row[:, QW + g * HD:QW + (g + 1) * HD], ident[:, :],
                                              start=True, stop=True)
                        mm.then_inc(qk_t, 1)
                        e.wait_ge(qk_c, 2 * (u + 1))
                        for g in range(NKV):
                            w = 2 * u + g
                            e.wait_ge(s_taken, w)
                            for z in range(G):
                                h = 2 * (z % 2) + z // 2
                                q0 = (h % 2) * HD
                                lhsT = qT[q0:q0 + HD, (g * G + h) // 2, :]
                                e.matmul(pss[:, z, 0:WIN], lhsT, kT[q0:q0 + HD, 1 - s, g, :], start=True, stop=True)
                                mm = e.matmul(pss[:, z, WIN:2 * WIN], lhsT, kT[q0:q0 + HD, s, g, :],
                                              start=True, stop=True)
                            mm.then_inc(s_done, 1)
                            e.wait_ge(expd, (G + 1) * (w + 1))
                            e.wait_ge(o_taken, w)
                            for n in range(NP):
                                e.wait_ge(p_c, NP * w + n - 1) if n > 1 else None
                                for q in range(4):
                                    h, half = 2 * n + q // 2, q % 2
                                    mm = e.transpose(pst[n % 2][:, q * P:(q + 1) * P],
                                                     pr[:, g, h, half * WIN:(half + 1) * WIN], ident[:, :])
                                mm.then_inc(p_t, 1)
                            e.wait_ge(p_c, NP * (w + 1))
                            for h in range(G):
                                n = h // 2
                                q = 2 * (h % 2)
                                e.matmul(pso[:, g, h, :], pT[:, 2 * g + n, q * P:(q + 1) * P],
                                         rows[:, 1 - s, QW + KW + g * HD:QW + KW + (g + 1) * HD], start=True, stop=False)
                                mm = e.matmul(pso[:, g, h, :], pT[:, 2 * g + n, (q + 1) * P:(q + 2) * P],
                                              rows[:, s, QW + KW + g * HD:QW + KW + (g + 1) * HD], start=False, stop=True)
                            mm.then_inc(o_done, 1)
                        e.wait_ge(o_taken, 2 * (u + 1))
                        for j in range(4):
                            mm = e.transpose(psq[:, j, :], att[:, j * P:(j + 1) * P], ident[:, :])
                        mm.then_inc(a_t, 1)
                        e.wait_ge(a_c, u + 1)

            @block.scalar
            def _(e):
                with e.Fori(0, NBLK // 2) as t:
                    for s in range(2):
                        u = 2 * t + s
                        e.wait_ge(qk_t, u + 1)
                        e.copy(qT[:], psq[:]).then_inc(qk_c, 1)
                        e.copy(kT[:, s, :, :], psk[:, 0:NKV, :]).then_inc(qk_c, 1)
                        for g in range(NKV):
                            w = 2 * u + g
                            e.wait_ge(neg, w + 1)
                            for h in range(G):
                                e.activation(pr[:, g, h, :], sc[:, h, :], ACT.Exp, bias=nmx[:, g, h:h + 1],
                                             accum_out=den[:, g, h:h + 1]).then_inc(expd, 1)
                            e.activation(es[:, g, :], sx[:, g, :], ACT.Exp).then_inc(expd, 1)
                            for n in range(NP):
                                e.wait_ge(p_t, NP * w + n + 1)
                                e.copy(pT[:, 2 * g + n, :], pst[n % 2][:, :]).then_inc(p_c, 1)
                        e.wait_ge(a_t, u + 1)
                        e.copy(attT[:, :, ds(u * P, P)], psq[:]).then_inc(a_c, 1)
                e.wait_ge(a_c, NBLK)

            @block.vector
            def _(e):
                e.memset(kT[:, 1, :, :], 0.0).then_inc(ring0, 1)
                e.memset(rows[:, 1, QW + KW:QKV], 0.0).then_inc(ring0, 1)
                e.wait_ge(consts2, 48)
                e.memset(att[:, 0:1], 0.0).then_inc(ring0, 1)
                with e.Fori(0, NBLK // 2) as t:
                    for s in range(2):
                        u = 2 * t + s
                        for g in range(NKV):
                            w = 2 * u + g
                            ch = Chain(e, vstep, VS * w)
                            e.wait_ge(s_done, w + 1)
                            e.wait_ge(expd, (G + 1) * w)
                            ch(e.scalar_tensor_tensor(out=sc[:], in0=pss[:], scalar=SCALE,
                                                      in1=mcur[:].unsqueeze(1).to_broadcast([P, G, 2 * WIN]),
                                                      op0=ALU.mult, op1=ALU.add))
                            ch.settle()
                            e.sem_inc(s_taken, 1)
                            ch(e.tensor_reduce(mx[:, g, :], sc[:], AX.X, ALU.max))
                            ch.settle()
                            ch(e.tensor_tensor(mx[:, g, :], mx[:, g, :], sink[:, g * G:(g + 1) * G], ALU.max))
                            ch.settle()
                            ch(e.tensor_scalar(nmx[:, g, :], mx[:, g, :], -1.0, None, ALU.mult))
                            ch(e.tensor_tensor(sx[:, g, :], sink[:, g * G:(g + 1) * G], mx[:, g, :], ALU.subtract))
                            ch.settle()
                            e.sem_inc(neg, 1)
                            e.wait_ge(expd, (G + 1) * (w + 1))
                            ch(e.tensor_tensor(den[:, g, :], den[:, g, :], es[:, g, :], ALU.add))
                            ch.settle()
                            ch(e.reciprocal(den[:, g, :], den[:, g, :]))
                            ch.settle()
                            e.wait_ge(o_done, w + 1)
                            e.wait_ge(a_c, u)
                            ch(e.tensor_tensor(
                                att[:, g * G * HD:(g + 1) * G * HD].rearrange("p (b a d) -> p a b d", a=2, b=2),
                                pso[:, g, :, :].rearrange("p (a b) d -> p a b d", a=2),
                                den[:, g, :].rearrange("p (a b) -> p a b", a=2).unsqueeze(3).to_broadcast([P, 2, 2, HD]),
                                ALU.mult))
                            ch.settle()
                            e.sem_inc(o_taken, 1)
                            assert ch.n == VS
                        if s == 0:
                            e.tensor_copy(mcur[:], mask[:]).then_inc(recip, 1)
                            e.wait_ge(recip, t + 1)
        self.attention_decode()

    def attention_decode(self):
        nc, i = self.nc, self.i
        qkv, attT, ident = self.qkv, self.attT, self.ident
        G = NQ // NKV
        NKC = NB * WIN
        with self.stage() as (c, block):
            ck = self.sb(c, "ck", [P, NB, KW])
            cv = self.sb(c, "cv", [P, NB, KW])
            mask = self.sb(c, "dmask", [P, T])
            sink = self.sb(c, "dsink", [P, NKV])
            kT = self.sb(c, "dkT", [P, T])
            qT = self.sb(c, "dqT", [P, NKV, P])
            sc = self.sb(c, "dsc", [P, T])
            pr = self.sb(c, "dpr", [P, T])
            pT = self.sb(c, "dpT", [P, TT, P])
            col = self.sb(c, "dcol", [P, 8])
            pss = self.ps(c, "dpss", [P, NC, 512])
            psa = self.ps(c, "dpsa", [P, 4, P])
            psb = self.ps(c, "dpsb", [P, 4, P])
            pso = self.ps(c, "dpso", [P, P])
            dk_in, kt, kc, qt, qc, sdone, vst, ex, ptt, ptc, od, oc = self.sems(
                "dk_in", "dkt", "dkc", "dqt", "dqc", "dsdone", "dvst", "dex", "dptt", "dptc", "dod", "doc")

            @block.sync
            def _(e):
                e.dma_start(ck[:], i["cache_k"].rearrange("b s f -> s b f")).then_inc(dk_in, 16)
                e.dma_start(cv[:], i["cache_v"].rearrange("b s f -> s b f")).then_inc(dk_in, 16)
                e.dma_start(mask[:], i["dmask"]).then_inc(dk_in, 16)
                e.dma_start(sink[:], i["dsink"]).then_inc(dk_in, 16)

            @block.tensor
            def _(e):
                e.wait_ge(dk_in, 64)
                for q in range(3):
                    ps = (psa, psb, psa)[q]
                    if q == 2:
                        e.wait_ge(kc, 1)
                        mm = e.transpose(ps[:, 0, 0:TS], qkv[0:TS, TT - 1, QW:QW + KW], ident[0:TS, 0:TS])
                    else:
                        for b in range(4):
                            mm = e.transpose(ps[:, b, :], ck[:, 4 * q + b, :], ident[:, :])
                    mm.then_inc(kt, 1)
                e.wait_ge(kc, 2)
                for g in range(NKV):
                    for h in range(G):
                        a = (g * G + h) * HD
                        mm = e.matmul(psb[g * HD:(g + 1) * HD, g, h * TS:(h + 1) * TS],
                                      qkv[0:TS, TT - 1, a:a + HD], ident[0:TS, 0:TS], start=True, stop=True)
                mm.then_inc(qt, 1)
                e.wait_ge(qc, 2)
                e.wait_ge(kc, 3)
                for g in range(NKV):
                    rows = slice(g * HD, (g + 1) * HD)
                    if g:
                        e.wait_ge(vst, 1)
                    for n in range(NC):
                        mm = e.matmul(pss[:, n, 0:CW], qT[rows, g, :], kT[rows, n * CW:(n + 1) * CW],
                                      start=True, stop=True)
                    mm.then_inc(sdone, 1)
                    e.wait_ge(vst, 7 * g + 7)
                    for q in range(3):
                        if q or g:
                            e.wait_ge(ptc, 3 * g + q)
                        ps = (psa, psb, psa)[q]
                        if q == 2:
                            mm = e.transpose(ps[0:TS, 0, :], pr[:, NKC:T], ident[:, :])
                        else:
                            for b in range(4):
                                mm = e.transpose(ps[:, b, :], pr[:, (4 * q + b) * P:(4 * q + b + 1) * P], ident[:, :])
                        mm.then_inc(ptt, 1)
                    e.wait_ge(ptc, 3 * g + 3)
                    if g:
                        e.wait_ge(oc, 4)
                    for b in range(NB):
                        e.matmul(pso[0:HD, :], cv[:, b, g * HD:(g + 1) * HD], pT[:, b, :], start=(b == 0), stop=False)
                    a = QW + KW + g * HD
                    e.matmul(pso[0:HD, :], qkv[0:TS, TT - 1, a:a + HD], pT[0:TS, NB, :], start=False, stop=True
                             ).then_inc(od, 1)

            @block.scalar
            def _(e):
                for q in range(3):
                    e.wait_ge(kt, q + 1)
                    ps = (psa, psb, psa)[q]
                    if q == 2:
                        e.copy(kT[:, NKC:T], ps[:, 0, 0:TS]).then_inc(kc, 1)
                    else:
                        e.copy(kT[:, q * 512:(q + 1) * 512], ps[:].rearrange("p a b -> p (a b)")).then_inc(kc, 1)
                e.wait_ge(qt, 1)
                for g in range(NKV):
                    rows = slice(g * HD, (g + 1) * HD)
                    e.copy(qT[rows, g, :], psb[rows, g, :]).then_inc(qc, 1)
                for g in range(NKV):
                    e.wait_ge(vst, 7 * g + 4)
                    e.activation(pr[:, :], sc[:, :], ACT.Exp, bias=col[:, 1:2], accum_out=col[:, 2:3]).then_inc(ex, 1)
                    e.activation(col[:, 3:4], sink[:, g:g + 1], ACT.Exp, bias=col[:, 1:2]).then_inc(ex, 1)
                    for q in range(3):
                        e.wait_ge(ptt, 3 * g + q + 1)
                        ps = (psa, psb, psa)[q]
                        if q == 2:
                            e.copy(pT[0:TS, NB, :], ps[0:TS, 0, :]).then_inc(ptc, 1)
                        else:
                            e.copy(pT[:, 4 * q:4 * q + 4, :], ps[:]).then_inc(ptc, 1)

            @block.vector
            def _(e):
                for g in range(NKV):
                    ch = Chain(e, vst, 7 * g)
                    e.wait_ge(sdone, g + 1)
                    e.wait_ge(ptt, 3 * g)
                    ch(e.scalar_tensor_tensor(out=sc[:].rearrange("p (n w) -> p n w", n=NC), in0=pss[:, :, 0:CW],
                                              scalar=SCALE, in1=mask[:].rearrange("p (n w) -> p n w", n=NC),
                                              op0=ALU.mult, op1=ALU.add))
                    ch.settle()
                    ch(e.tensor_reduce(col[:, 0:1], sc[:], AX.X, ALU.max))
                    ch.settle()
                    ch(e.tensor_tensor(col[:, 0:1], col[:, 0:1], sink[:, g:g + 1], ALU.max))
                    ch.settle()
                    ch(e.tensor_scalar(col[:, 1:2], col[:, 0:1], -1.0, None, ALU.mult))
                    e.wait_ge(ex, 2 * g + 2)
                    ch(e.tensor_tensor(col[:, 4:5], col[:, 2:3], col[:, 3:4], ALU.add))
                    ch.settle()
                    ch(e.reciprocal(col[:, 5:6], col[:, 4:5]))
                    ch.settle()
                    ch(e.tensor_scalar(pr[:, :], pr[:, :], col[:, 5:6], None, ALU.mult))
                    e.wait_ge(od, g + 1)
                    for h in range(G):
                        hh = g * G + h
                        e.tensor_copy(attT[(hh % 2) * HD:(hh % 2 + 1) * HD, hh // 2, TP:T],
                                      pso[0:HD, h * TS:(h + 1) * TS]).then_inc(oc, 1)
                e.wait_ge(oc, NQ)


    def rwkv(self):
        nc, i, o = self.nc, self.i, self.o
        with ExitStack() as c:
            self.dv = {n: self.sb(c, "dec_" + n, [P, NPAIR, TS]) for n in ("alpha", "beta", "kappa", "rho", "v")}
            self.dcum = self.sb(c, "dec_cum", [P, NPAIR, NB])
            self.lmask = self.sb(c, "level_masks", [P, LEVELS, P])
            self.low0 = self.sb(c, "low0", [P, P])
            self.before = self.sb(c, "before", [P, P])
            self.upto = self.sb(c, "upto", [P, 2, CH])
            with ExitStack() as c2:
                al, be, ka, rh, cu = (self.sb(c2, n, [P, T]) for n in ("alpha", "beta", "kappa", "rho", "cum"))
                self.al, self.be, self.ka, self.rh, self.cu = al, be, ka, rh, cu
                self.w2, self.a2 = self.sb(c2, "w2", [LW, P]), self.sb(c2, "a2", [LA, P])
                self.g2 = self.sb(c2, "g2", [LG, P])
                self.par = self.sb(c2, "pair_par", [P, 5])
                self.omka = self.sb(c2, "omka", [P, 1])
                self.work = self.sb(c2, "work", [P, WORK])
                self.banks = self.ps(c2, "banks", [P, 8, 512])
                self.lora_inputs()
                with nc.Fori(0, NPAIR) as j:
                    self.rwkv_elementwise(j)
                    self.rwkv_chunks(j)
            self.rwkv_decode()
        self.rwkv_out()

    def lora_inputs(self):
        nc, i = self.nc, self.i
        with self.stage() as (c, block):
            m_in, done = self.sems("m_in", "lora_done")

            @block.sync
            def _(e):
                e.dma_start(self.lmask[:], i["level_masks"]).then_inc(m_in, 16)
                e.dma_start(self.low0[:], i["low0"]).then_inc(m_in, 16)
                e.dma_start(self.before[:], i["before"]).then_inc(m_in, 16)
                e.dma_start(self.upto[:], i["upto"]).then_inc(m_in, 16)
                e.wait_ge(m_in, 64)

            @block.scalar
            def _(e):
                e.activation(self.lw[:], self.lw[:], ACT.Tanh).then_inc(done, 1)
                e.activation(self.lg[:], self.lg[:], ACT.Sigmoid).then_inc(done, 1)
                e.wait_ge(done, 2)

    def rwkv_elementwise(self, j):
        nc, i = self.nc, self.i
        al, be, ka, rh, cu = self.al, self.be, self.ka, self.rh, self.cu
        plane = lambda n: self.mixed[:, ds(j + n, 1), :].rearrange("p o t -> p (o t)")
        r, k, v = plane(0), plane(NPAIR), plane(2 * NPAIR)
        with self.stage() as (c, block):
            w2, a2, g2, par, omka = self.w2, self.a2, self.g2, self.par, self.omka
            carve = Carver(self.work)
            dec, a, kk, t0, t1 = (carve(T) for _ in range(5))
            pa, pb = self.banks[:, 0:NC, :], self.banks[:, NC:2 * NC, :]
            par_in, pz, az, va, pv, vz = self.sems("par_in2", "pz", "az", "va", "pv", "vz")
            split = lambda x: x.rearrange("p (n w) -> p n w", n=NC)
            used = lambda p: p[:, :, 0:CW]
            starts = lambda x: (x[:, 0:TP].rearrange("p (n w) -> p n w", w=CH)[:, :, 0],
                                x[:, TP:T].rearrange("p (n w) -> p n w", w=NS)[:, :, 0])

            @block.sync
            def _(e):
                for a_, b_ in ((w2, "w2"), (a2, "a2"), (g2, "g2"), (par, "pair_par")):
                    e.dma_start(a_[:], i[b_][ds(j, 1)].rearrange("o p f -> (o p) f")).then_inc(par_in, 16)

            @block.tensor
            def _(e):
                def product(ps, lhsT, rhs):
                    for n in range(NC):
                        mm = e.matmul(ps[:, n, 0:CW], lhsT, rhs[:, n * CW:(n + 1) * CW], start=True, stop=True)
                    mm.then_inc(pz, 1)
                e.wait_ge(par_in, 64)
                product(pa, w2[:], self.lw[:])
                product(pb, a2[:], self.la[:])
                e.wait_ge(az, 1)
                product(pa, g2[:], self.lg[:])
                e.wait_ge(az, 2)
                e.wait_ge(pv, 1)
                product(pb, self.headones[:], t0[:])
                e.wait_ge(az, 4)
                e.wait_ge(va, 14)
                product(pa, self.headones[:], t1[:])

            @block.scalar
            def _(e):
                e.wait_ge(pz, 1)
                e.activation(split(dec[:]), used(pa), ACT.Sigmoid, bias=par[:, 0:1]).then_inc(az, 1)
                e.wait_ge(pz, 2)
                e.activation(split(a[:]), used(pb), ACT.Sigmoid, bias=par[:, 1:2]).then_inc(az, 1)
                e.wait_ge(az, 1)
                e.activation(dec[:], dec[:], ACT.Exp, scale=-float(np.exp(-0.5))).then_inc(az, 1)
                e.wait_ge(pz, 3)
                e.wait_ge(va, 9)
                e.copy(split(k), used(pa)).then_inc(az, 1)
                e.wait_ge(va, 10)
                e.activation(t0[:], t0[:], ACT.Sqrt).then_inc(az, 1)

            @block.gpsimd
            def _(e):
                e.wait_ge(va, 2)
                e.tensor_tensor(t0[:], kk[:], kk[:], ALU.mult).then_inc(pv, 1)

            @block.vector
            def _(e):
                ch = Chain(e, va)
                e.wait_ge(par_in, 64)
                ch(e.tensor_scalar(omka[:], par[:, 3:4], -1.0, 1.0, ALU.mult, ALU.add))
                ch(e.tensor_scalar(kk[:], k, par[:, 2:3], None, ALU.mult))
                e.wait_ge(az, 3)
                ch(e.tensor_copy(al[:], dec[:]))
                ch(e.memset(be[:], 0.0))
                ch.settle()
                for n, (x, y) in enumerate(zip(starts(be[:]), starts(dec[:]))):
                    ch(e.tensor_copy(x, y))
                for x in starts(al[:]):
                    e.memset(x, 0.0).then_inc(vz, 1)
                e.wait_ge(vz, 2)
                ch.settle()
                ch(e.tensor_tensor_scan(cu[:], al[:], be[:], 0.0, ALU.mult, ALU.add))
                ch(e.tensor_scalar(t1[:], a[:], par[:, 3:4], omka[:, 0:1], ALU.mult, ALU.add))
                ch.settle()
                ch(e.tensor_tensor(ka[:], t1[:], k, ALU.mult))
                e.wait_ge(pz, 4)
                ch(e.tensor_scalar(split(t0[:]), used(pb), 1e-24, None, ALU.max))
                ch.settle()
                ch(e.scalar_tensor_tensor(out=t1[:], in0=ka[:], scalar=par[:, 4:5], in1=r, op0=ALU.mult,
                                          op1=ALU.mult))
                ch(e.tensor_tensor(rh[:], cu[:], r, ALU.mult))
                ch(e.reciprocal(be[:], cu[:]))
                ch.settle()
                ch(e.tensor_tensor(ka[:], ka[:], be[:], ALU.mult))
                e.wait_ge(az, 5)
                ch(e.reciprocal(t0[:], t0[:]))
                ch.settle()
                ch(e.tensor_tensor(kk[:], kk[:], t0[:], ALU.mult))
                ch(e.tensor_copy(dec[:, 1:T], cu[:, 0:T - 1]))
                ch.settle()
                for x in starts(dec[:]):
                    ch(e.memset(x, 1.0))
                ch(e.tensor_tensor(a[:], a[:], kk[:], ALU.mult))
                ch.settle()
                ch(e.tensor_tensor(al[:], dec[:], kk[:], ALU.mult))
                ch(e.tensor_tensor(be[:], be[:], a[:], ALU.mult))
                e.wait_ge(pz, 5)
                ch(e.tensor_tensor(split(r), used(pa), split(v), ALU.mult))
                ch.settle()
                for n, x in (("alpha", al), ("beta", be), ("kappa", ka), ("rho", rh)):
                    ch(e.tensor_copy(self.dv[n][:, ds(j, 1), :].rearrange("p o t -> p (o t)"), x[:, TP:T]))
                ch(e.tensor_copy(self.dv["v"][:, ds(j, 1), :].rearrange("p o t -> p (o t)"), v[:, TP:T]))
                ch(e.tensor_copy(self.dcum[:, ds(j, 1), :].rearrange("p o t -> p (o t)"),
                                 cu[:, TP:T].rearrange("p (b n) -> p b n", n=NS)[:, :, NS - 1]))
                ch.settle()

    def rwkv_chunks(self, j):
        nc, i, o = self.nc, self.i, self.o
        ident = self.ident
        v = self.mixed[:, ds(j + 2 * NPAIR, 1), :].rearrange("p o t -> p (o t)")
        L = LANES
        with self.stage() as (c, block):
            carve = Carver(self.work)
            big = lambda n: carve(L, P)
            ab, bb, kb, vb = (big(n) for n in ("alpha_bd", "beta_bd", "kappa_bd", "v_bd"))
            rq = carve(L, CH)
            cq = carve(L)
            araw = big("a_raw")
            alv = carve(LEVELS - 1, L, P)
            X, Y, Pm = big("inv_x"), big("inv_y"), big("inv_p")
            bt = big("b_masked")
            brk = carve(L, 2, CH)
            at, bT, kT, vT = (big(n) for n in ("alpha_t", "beta_t", "kappa_t", "v_t"))
            r1, wv, apt = big("r1"), big("w_v"), big("a_alpha")
            st, sc, nsa = carve(2, P), carve(2, P), carve(2, P)
            b = [self.banks[:, n, :].rearrange("p (l w) -> p l w", l=L) for n in range(8)]
            names = ("built", "gram", "tposed", "araw_c", "t_c", "lvl", "g_v", "p_d", "p_cc", "xy_d", "xy_v", "r1_d",
                     "r1_c", "wa_d", "wa_c", "sa_d", "nsa_v", "u_d", "sc_c", "st_v", "y_c", "zset")
            (built, gram, tposed, araw_c, t_c, lvl, g_v, p_d, p_cc, xy_d, xy_v, r1_d, r1_c, wa_d, wa_c, sa_d,
             nsa_v, u_d, sc_c, st_v, y_c, zset) = self.sems(*names)
            NL = LEVELS - 1
            bc = lambda m: m.unsqueeze(1).to_broadcast([P, L, P])

            @block.gpsimd
            def _(e):
                with e.Fori(0, NQUAD) as q:
                    at_q = q * (L * CH)
                    e.wait_ge(y_c, q)
                    for src, dst in ((self.al[:], ab), (self.be[:], bb), (self.ka[:], kb), (v, vb)):
                        for h in range(2):
                            mine = self.headones[:, h * HD:(h + 1) * HD].unsqueeze(1).to_broadcast([P, L, CH])
                            e.tensor_tensor(dst[:, :, h * CH:(h + 1) * CH],
                                            src[:, ds(at_q, L * CH)].rearrange("p (l w) -> p l w", l=L),
                                            mine, ALU.mult).then_inc(built, 1)
                    e.tensor_copy(rq[:].rearrange("p l w -> p (l w)"), self.rh[:, ds(at_q, L * CH)]).then_inc(built, 1)
                    e.tensor_copy(cq[:], self.cu[:, ds(at_q, L * CH)].rearrange("p (l w) -> p l w", l=L)[:, :, CH - 1]
                                  ).then_inc(built, 1)
                    e.wait_ge(araw_c, q + 1)
                    for l in range(NL):
                        e.tensor_tensor(alv[:, l, :, :], araw[:], bc(self.lmask[:, l + 1, :]), ALU.mult
                                        ).then_inc(lvl, 1)

            @block.tensor
            def _(e):
                with e.Fori(0, NQUAD) as q:
                    e.wait_ge(built, 10 * (q + 1))
                    e.wait_ge(y_c, q)
                    for l in range(L):
                        e.matmul(b[0][:, l, :], bb[:, l, :], ab[:, l, :], start=True, stop=True)
                    for l in range(L):
                        mm = e.matmul(b[1][:, l, :], ab[:, l, :], bb[:, l, :], start=True, stop=True)
                    mm.then_inc(gram, 1)
                    for l in range(L):
                        e.matmul(b[2][:, l, :], kb[:, l, :], ab[:, l, :], start=True, stop=True)
                    for l in range(L):
                        e.matmul(b[3][:, l, 0:CH], bb[:, l, :], rq[:, l, :], start=True, stop=True)
                        mm = e.matmul(b[3][:, l, CH:P], kb[:, l, :], rq[:, l, :], start=True, stop=True)
                    mm.then_inc(gram, 1)
                    for n, m in enumerate((ab, bb, kb, vb)):
                        for l in range(L):
                            mm = e.transpose(b[4 + n][:, l, :], m[:, l, :], ident[:])
                        mm.then_inc(tposed, 1)
                    for n in range(NL):
                        e.wait_ge(lvl, NL * q + n + 1)
                        if n == 0:
                            e.wait_ge(g_v, 6 * (q + 1))
                        else:
                            e.wait_ge(xy_v, 2 * (NL * q + n))
                        for l in range(L):
                            mm = e.matmul(b[0][:, l, :], alv[:, n, l, :], X[:, l, :], start=True, stop=True)
                        mm.then_inc(p_d, 1)
                        e.wait_ge(p_cc, NL * q + n + 1)
                        for l in range(L):
                            e.matmul(b[1][:, l, :], Y[:, l, :], Pm[:, l, :], start=True, stop=True)
                            mm = e.matmul(b[2][:, l, :], Pm[:, l, :], Y[:, l, :], start=True, stop=True)
                        mm.then_inc(xy_d, 1)
                    e.wait_ge(t_c, 4 * (q + 1))
                    for l in range(L):
                        mm = e.matmul(b[3][:, l, :], bt[:, l, :], vT[:, l, :], start=True, stop=True)
                    mm.then_inc(r1_d, 1)
                    e.wait_ge(xy_v, 2 * NL * (q + 1))
                    for l in range(L):
                        mm = e.matmul(b[5][:, l, :], at[:, l, :], Y[:, l, :], start=True, stop=True)
                    mm.then_inc(wa_d, 1)
                    e.wait_ge(r1_c, q + 1)
                    for l in range(L):
                        mm = e.matmul(b[4][:, l, :], Y[:, l, :], r1[:, l, :], start=True, stop=True)
                    mm.then_inc(wa_d, 1)
                    e.wait_ge(wa_c, 2 * (q + 1))
                    for l in range(L):
                        s = l % 2
                        e.wait_ge(st_v, L * q + l + 1)
                        e.matmul(b[6][:, l, :], apt[:, l, :], st[:, s, :], start=True, stop=True).then_inc(sa_d, 1)
                        y = b[0][:].rearrange("p l w -> p (l w)")[:, l * CH:(l + 1) * CH]
                        e.matmul(y, st[:, s, :], rq[:, l, :], start=True, stop=False)
                        e.matmul(y, vT[:, l, :], brk[:, l, 1, :], start=False, stop=False)
                        e.wait_ge(nsa_v, L * q + l + 1)
                        e.matmul(y, nsa[:, s, :], brk[:, l, 0, :], start=False, stop=True)
                        e.matmul(b[7][:, l, :], kT[:, l, :], vT[:, l, :], start=True, stop=False)
                        e.matmul(b[7][:, l, :], bT[:, l, :], nsa[:, s, :], start=False, stop=True).then_inc(u_d, 1)

            @block.scalar
            def _(e):
                with e.Fori(0, NQUAD) as q:
                    e.wait_ge(gram, 2 * q + 1)
                    e.wait_ge(lvl, NL * q)
                    e.wait_ge(g_v, 6 * q)
                    e.copy(araw[:], b[0][:]).then_inc(araw_c, 1)
                    for n, m in enumerate((at, bT, kT, vT)):
                        e.wait_ge(tposed, 4 * q + n + 1)
                        e.copy(m[:], b[4 + n][:]).then_inc(t_c, 1)
                    for n in range(NL):
                        e.wait_ge(p_d, NL * q + n + 1)
                        e.copy(Pm[:], b[0][:]).then_inc(p_cc, 1)
                    e.wait_ge(r1_d, q + 1)
                    e.copy(r1[:], b[3][:]).then_inc(r1_c, 1)
                    e.wait_ge(wa_d, 2 * q + 1)
                    e.copy(apt[:], b[5][:]).then_inc(wa_c, 1)
                    e.wait_ge(wa_d, 2 * q + 2)
                    e.copy(wv[:], b[4][:]).then_inc(wa_c, 1)
                    for l in range(L):
                        e.wait_ge(st_v, L * q + l + 1)
                        e.mul(sc[:, l % 2, :], st[:, l % 2, :], cq[:, l:l + 1]).then_inc(sc_c, 1)
                    e.wait_ge(u_d, L * (q + 1))
                    e.wait_ge(st_v, L * (q + 1) + 1)
                    y = b[0][:].rearrange("p l w -> p (l w)")[:, 0:L * CH]
                    e.copy(v[:, ds(q * (L * CH), L * CH)], y).then_inc(y_c, 1)

            @block.vector
            def _(e):
                e.memset(st[:, 0, :], 0.0).then_inc(st_v, 1)
                with e.Fori(0, NQUAD) as q:
                    ch = Chain(e, g_v, 6 * q)
                    e.wait_ge(gram, 2 * q + 1)
                    e.wait_ge(y_c, q)
                    ch(e.tensor_tensor(X[:], b[1][:], bc(self.low0[:]), ALU.mult))
                    e.wait_ge(araw_c, q + 1)
                    ch(e.tensor_tensor(Y[:], araw[:], bc(self.lmask[:, 0, :]), ALU.mult))
                    ch.settle()
                    ch(e.tensor_tensor(Y[:], bc(ident[:]), Y[:], ALU.subtract))
                    ch(e.tensor_tensor(X[:], bc(ident[:]), X[:], ALU.subtract))
                    e.wait_ge(gram, 2 * q + 2)
                    ch(e.tensor_tensor(bt[:], b[2][:], bc(self.before[:]), ALU.mult))
                    ch(e.tensor_tensor(brk[:], b[3][:].rearrange("p l (a w) -> p l a w", a=2),
                                       self.upto[:].unsqueeze(1).to_broadcast([P, L, 2, CH]), ALU.mult))
                    for n in range(NL):
                        e.wait_ge(xy_d, NL * q + n + 1)
                        e.tensor_tensor(X[:], X[:], b[1][:], ALU.subtract).then_inc(xy_v, 1)
                        e.tensor_tensor(Y[:], Y[:], b[2][:], ALU.subtract).then_inc(xy_v, 1)
                        e.wait_ge(xy_v, 2 * (NL * q + n + 1))
                    e.wait_ge(wa_c, 2 * (q + 1))
                    for l in range(L):
                        s = l % 2
                        e.wait_ge(sa_d, L * q + l + 1)
                        e.scalar_tensor_tensor(out=nsa[:, s, :], in0=b[6][:, l, :], scalar=-1.0, in1=wv[:, l, :],
                                               op0=ALU.mult, op1=ALU.subtract).then_inc(nsa_v, 1)
                        e.wait_ge(u_d, L * q + l + 1)
                        e.wait_ge(sc_c, L * q + l + 1)
                        e.scalar_tensor_tensor(out=st[:, 1 - s, :], in0=b[7][:, l, :], scalar=cq[:, l:l + 1],
                                               in1=sc[:, s, :], op0=ALU.mult, op1=ALU.add).then_inc(st_v, 1)
                e.wait_ge(st_v, TP // CH + 1)

            out_s, = self.sems("wkv_out")

            @block.sync
            def _(e):
                e.wait_ge(st_v, TP // CH + 1)
                for h in range(2):
                    rows = slice(h * HD, (h + 1) * HD)
                    e.dma_start(o["prompt_wkv"][ds(2 * j + h, 1)].rearrange("o a b -> (o a) b"), st[rows, 0, rows]
                                ).then_inc(out_s, 16)
                e.wait_ge(out_s, 32)


    def rwkv_decode(self):
        nc, i, o = self.nc, self.i, self.o
        ident, dv = self.ident, self.dv
        L, Q = NPAIR, 2 * TS
        with self.stage() as (c, block):
            sb = lambda n, *s: self.sb(c, "d_" + n, list(s))
            st0 = sb("state", P, L, NB, P)
            st1 = sb("state_new", P, L, NB, P)
            bd = [sb(f"bd{n}", P, L, 2, TS) for n in range(5)]
            tm = [sb(f"tm{n}", Q, L, P) for n in range(5)]
            mk = sb("masks", Q, 4, Q)
            mu = sb("upto", Q, 2, TS)
            own = sb("own", Q, NB)
            X, Y, Pm, a1, bt = (sb(n, Q, L, Q) for n in ("x", "y", "p", "a1", "bt"))
            yst = sb("yst", Q, L, TS)
            brk = sb("brk", Q, L, 2, TS)
            r1 = sb("r1", Q, L, P)
            apt = sb("apt", P, L, TS)
            vn = sb("vn", Q, 2, 2, NB, P)
            sums = sb("sums", P, 2, 4, P)
            b = [self.ps(c, f"db{n}", [P, 512]) for n in range(8)]
            d_in, bdp, gram, araw, g_v, p_d, p_c, y_d, y_v, r1_d, r1_c, ap_d, ap_c, sa_d, sa_c, bdn, nt_d, nt_c, y_f, \
                y_fc, vnp, u_d, u_v, u_c, out_s = self.sems(*[f"dec{n}" for n in range(25)])
            q4 = lambda m, rows, w: m[0:rows, 0:L * w].rearrange("p (l w) -> p l w", l=L)

            @block.sync
            def _(e):
                e.dma_start(mk[:], i["dec_masks"]).then_inc(d_in, 16)
                e.dma_start(mu[:], i["dec_upto"]).then_inc(d_in, 16)
                e.dma_start(own[:], i["dec_own"]).then_inc(d_in, 16)
                e.dma_start(st0[:], i["state0"]).then_inc(d_in, 16)
                e.wait_ge(u_c, 2 * L)
                for h in range(2):
                    rows = slice(h * HD, (h + 1) * HD)
                    for l in range(L):
                        e.dma_start(o["sample_wkv"][:, 2 * l + h].rearrange("b j i -> j b i"), st1[rows, l, :, rows]
                                    ).then_inc(out_s, 16)
                e.wait_ge(out_s, 32 * L)

            @block.gpsimd
            def _(e):
                for n, name in enumerate(("alpha", "beta", "kappa", "v")):
                    for h in range(2):
                        e.tensor_scalar(bd[n][:, :, h, :], dv[name][:], self.headones[:, h * HD:h * HD + 1], None,
                                        ALU.mult).then_inc(bdp, 1)
                e.wait_ge(nt_c, 1)
                e.wait_ge(d_in, 64)
                for l in range(L):
                    if l >= 2:
                        e.wait_ge(u_d, 2 * (l - 1))
                    for n, m in enumerate((tm[3], tm[4])):
                        e.tensor_tensor(vn[:, l % 2, n, :, :], m[:, l, :].unsqueeze(1).to_broadcast([Q, NB, P]),
                                        own[:].unsqueeze(2).to_broadcast([Q, NB, P]), ALU.mult).then_inc(vnp, 1)

            @block.tensor
            def _(e):
                e.wait_ge(bdp, 8)
                f = lambda m, l: m[:, l, :, :].rearrange("p a b -> p (a b)")
                for k, (x, y) in enumerate(((1, 0), (0, 1), (2, 0))):
                    for l in range(L):
                        mm = e.matmul(q4(b[k], Q, Q)[:, l, :], f(bd[x], l), f(bd[y], l), start=True, stop=True)
                    mm.then_inc(gram, 1)
                for l in range(L):
                    for n in range(2):
                        mm = e.matmul(q4(b[3], Q, Q)[:, l, n * TS:(n + 1) * TS], f(bd[1 + n], l), dv["rho"][:, l, :],
                                      start=True, stop=True)
                mm.then_inc(gram, 1)
                for n in range(4):
                    for l in range(L):
                        mm = e.transpose(q4(b[4 + n], Q, P)[:, l, :], f(bd[n], l), ident[:])
                    mm.then_inc(gram, 1)
                e.wait_ge(g_v, 7)
                for l in range(L):
                    mm = e.matmul(q4(b[0], Q, Q)[:, l, :], a1[:, l, :], X[:, l, :], start=True, stop=True)
                mm.then_inc(p_d, 1)
                e.wait_ge(p_c, 1)
                for l in range(L):
                    mm = e.matmul(q4(b[1], Q, Q)[:, l, :], Pm[:, l, :], Y[:, l, :], start=True, stop=True)
                mm.then_inc(y_d, 1)
                e.wait_ge(r1_c, 4)
                for l in range(L):
                    mm = e.matmul(q4(b[2], Q, P)[:, l, :], bt[:, l, :], tm[3][:, l, :], start=True, stop=True)
                mm.then_inc(r1_d, 1)
                e.wait_ge(y_v, 2)
                for l in range(L):
                    mm = e.matmul(q4(b[3], P, TS)[:, l, :], tm[0][:, l, :], yst[:, l, :], start=True, stop=True)
                mm.then_inc(ap_d, 1)
                e.wait_ge(ap_c, 1)
                e.wait_ge(r1_c, 5)
                e.wait_ge(d_in, 64)
                for l in range(L):
                    y = q4(b[4], P, TS)[:, l, :]
                    for k in range(NB):
                        e.matmul(y[:, k * NS:(k + 1) * NS], st0[:, l, k, :], apt[:, l, k * NS:(k + 1) * NS],
                                 start=(k == 0), stop=False)
                    mm = e.matmul(y, r1[:, l, :], yst[:, l, :], start=False, stop=True)
                mm.then_inc(sa_d, 1)
                e.wait_ge(bdn, 2)
                for l in range(L):
                    mm = e.transpose(q4(b[5], Q, P)[:, l, :], f(bd[4], l), ident[:])
                mm.then_inc(nt_d, 1)
                e.wait_ge(nt_c, 1)
                for l in range(L):
                    y = q4(b[6], P, TS)[:, l, :]
                    for k in range(NB):
                        e.matmul(y[:, k * NS:(k + 1) * NS], st0[:, l, k, :], dv["rho"][:, l, k * NS:(k + 1) * NS],
                                 start=(k == 0), stop=False)
                    e.matmul(y, tm[3][:, l, :], brk[:, l, 1, :], start=False, stop=False)
                    mm = e.matmul(y, tm[4][:, l, :], brk[:, l, 0, :], start=False, stop=True)
                mm.then_inc(y_f, 1)
                for l in range(L):
                    e.wait_ge(vnp, 2 * (l + 1))
                    for half in range(2):
                        n = 2 * l + half
                        if n >= 4:
                            e.wait_ge(u_v, n - 3)
                        for k in range(4):
                            u = q4(b[n % 4], P, P)[:, k, :]
                            e.matmul(u, tm[2][:, l, :], vn[:, l % 2, 0, 4 * half + k, :], start=True, stop=False)
                            mm = e.matmul(u, tm[1][:, l, :], vn[:, l % 2, 1, 4 * half + k, :], start=False, stop=True)
                        mm.then_inc(u_d, 1)

            @block.scalar
            def _(e):
                for n in range(4):
                    e.wait_ge(gram, 5 + n)
                    e.copy(tm[n][:], q4(b[4 + n], Q, P)).then_inc(r1_c, 1)
                e.wait_ge(p_d, 1)
                e.copy(Pm[:], q4(b[0], Q, Q)).then_inc(p_c, 1)
                e.wait_ge(r1_d, 1)
                e.copy(r1[:], q4(b[2], Q, P)).then_inc(r1_c, 1)
                e.wait_ge(ap_d, 1)
                e.copy(apt[:], q4(b[3], P, TS)).then_inc(ap_c, 1)
                e.wait_ge(nt_d, 1)
                e.copy(tm[4][:], q4(b[5], Q, P)).then_inc(nt_c, 1)
                e.wait_ge(y_f, 1)
                e.copy(self.mixed[:, 2 * NPAIR:3 * NPAIR, TP:T], q4(b[6], P, TS)).then_inc(y_fc, 1)
                for n in range(2 * L):
                    l, half = n // 2, n % 2
                    e.wait_ge(u_v, n + 1)
                    for k in range(4):
                        mm = e.mul(st1[:, l, 4 * half + k, :], sums[:, half, k, :],
                                   self.dcum[:, l, 4 * half + k:4 * half + k + 1])
                    mm.then_inc(u_c, 1)
                e.wait_ge(y_fc, 1)

            @block.vector
            def _(e):
                m = lambda k: mk[:, k, :].unsqueeze(1).to_broadcast([Q, L, Q])
                eye = ident[0:Q, 0:Q].unsqueeze(1).to_broadcast([Q, L, Q])
                e.wait_ge(d_in, 64)
                ch = Chain(e, g_v)
                e.wait_ge(gram, 1)
                ch(e.tensor_tensor(Y[:], q4(b[0], Q, Q), m(1), ALU.mult))
                ch(e.tensor_tensor(a1[:], q4(b[0], Q, Q), m(2), ALU.mult))
                e.wait_ge(gram, 2)
                ch(e.tensor_tensor(X[:], q4(b[1], Q, Q), m(3), ALU.mult))
                ch.settle()
                ch(e.tensor_tensor(Y[:], eye, Y[:], ALU.subtract))
                ch(e.tensor_tensor(X[:], eye, X[:], ALU.subtract))
                e.wait_ge(gram, 3)
                ch(e.tensor_tensor(bt[:], q4(b[2], Q, Q), m(0), ALU.mult))
                e.wait_ge(gram, 4)
                ch(e.tensor_tensor(brk[:], q4(b[3], Q, Q).rearrange("p l (a w) -> p l a w", a=2),
                                   mu[:].unsqueeze(1).to_broadcast([Q, L, 2, TS]), ALU.mult))
                e.wait_ge(y_d, 1)
                e.tensor_tensor(Y[:], Y[:], q4(b[1], Q, Q), ALU.subtract).then_inc(y_v, 1)
                e.wait_ge(y_v, 1)
                e.tensor_tensor(yst[:], Y[:, :, 0:TS], Y[:, :, TS:Q], ALU.add).then_inc(y_v, 1)
                e.wait_ge(sa_d, 1)
                e.tensor_scalar(bd[4][:, :, 0, :], q4(b[4], P, TS), self.headones[:, 0:1], -1.0, ALU.mult, ALU.mult
                                ).then_inc(bdn, 1)
                e.tensor_scalar(bd[4][:, :, 1, :], q4(b[4], P, TS), self.headones[:, HD:HD + 1], -1.0, ALU.mult,
                                ALU.mult).then_inc(bdn, 1)
                for n in range(2 * L):
                    l, half = n // 2, n % 2
                    e.wait_ge(u_d, n + 1)
                    if n >= 2:
                        e.wait_ge(u_c, n - 1)
                    e.tensor_tensor(sums[:, half, :, :], st0[:, l, 4 * half:4 * half + 4, :], q4(b[n % 4], P, P),
                                    ALU.add).then_inc(u_v, 1)

    def rwkv_out(self):
        nc, i = self.nc, self.i
        with self.stage() as (c, block):
            par = self.sb(c, "gn_par", [P, 2, NPAIR])
            epsc = self.sb(c, "gn_eps", [P, 1])
            yc = self.sb(c, "gn_yc", [P, 2, T])
            sq = self.sb(c, "gn_sq", [P, 2, T])
            rs = self.sb(c, "gn_rs", [P, 2, T])
            pm = self.ps(c, "gn_mean", [P, NC, 512])
            pv = self.ps(c, "gn_var", [P, NC, 512])
            par_in, eps_set, mean_d, cen, sqd, var_d, root, vst = self.sems(
                "gn_par_in", "gn_eps_set", "mean_d", "centred", "squared", "var_d", "gn_root", "gn_v")
            split = lambda x: x.rearrange("p (n w) -> p n w", n=NC)
            V = 5

            @block.sync
            def _(e):
                e.dma_start(par[:], i["gn_par"]).then_inc(par_in, 16)

            @block.tensor
            def _(e):
                for j in range(NPAIR):
                    y = self.mixed[:, 2 * NPAIR + j, :]
                    if j:
                        e.wait_ge(cen, j)
                    for n in range(NC):
                        mm = e.matmul(pm[:, n, 0:CW], self.headones[:], y[:, n * CW:(n + 1) * CW], start=True, stop=True)
                    mm.then_inc(mean_d, 1)
                    e.wait_ge(sqd, j + 1)
                    if j:
                        e.wait_ge(root, j)
                    for n in range(NC):
                        mm = e.matmul(pv[:, n, 0:CW], self.headones[:], sq[:, j % 2, n * CW:(n + 1) * CW],
                                      start=True, stop=True)
                    mm.then_inc(var_d, 1)

            @block.scalar
            def _(e):
                e.wait_ge(eps_set, 1)
                for j in range(NPAIR):
                    e.wait_ge(cen, j + 1)
                    e.activation(sq[:, j % 2, :], yc[:, j % 2, :], ACT.Square).then_inc(sqd, 1)
                    e.wait_ge(var_d, j + 1)
                    if j >= 2:
                        e.wait_ge(vst, V * (j - 1))
                    e.activation(split(rs[:, j % 2, :]), pv[:, :, 0:CW], ACT.Sqrt, bias=epsc[:], scale=1.0 / HD
                                 ).then_inc(root, 1)

            @block.vector
            def _(e):
                e.memset(epsc[:], GN_EPS).then_inc(eps_set, 1)
                e.wait_ge(par_in, 16)
                for j in range(NPAIR):
                    ch = Chain(e, vst, V * j)
                    y = self.mixed[:, 2 * NPAIR + j, :]
                    s = j % 2
                    e.wait_ge(mean_d, j + 1)
                    e.scalar_tensor_tensor(out=split(yc[:, s, :]), in0=pm[:, :, 0:CW], scalar=-1.0 / HD, in1=split(y),
                                           op0=ALU.mult, op1=ALU.add).then_inc(cen, 1)
                    e.wait_ge(root, j + 1)
                    ch(e.reciprocal(rs[:, s, :], rs[:, s, :]))
                    ch.settle()
                    ch(e.tensor_tensor(yc[:, s, :], yc[:, s, :], rs[:, s, :], ALU.mult))
                    ch.settle()
                    ch(e.tensor_scalar(yc[:, s, :], yc[:, s, :], par[:, 0, j:j + 1], par[:, 1, j:j + 1],
                                       ALU.mult, ALU.add))
                    ch.settle()
                    ch(e.tensor_tensor(yc[:, s, :], yc[:, s, :], self.mixed[:, j, :], ALU.add))
                    ch.settle()
                    ch(e.tensor_tensor(self.mixed[:, j, :], yc[:, s, :], self.mixed[:, NPAIR + j, :], ALU.mult))
                    ch.settle()
                    assert ch.n == V


    def merge(self):
        nc, i = self.nc, self.i
        rwT, outT = self.mixed[:, 0:NPAIR, :], self.mixed[:, NPAIR:NPAIR + KT, :]
        NW = 2 * KT + 2 * NPAIR
        with self.stage() as (c, block):
            w = self.sb(c, "w_merge", [P, 2, NW, P])
            gb = self.sb(c, "b_gate", [P, KT, 2])
            bcol = self.sb(c, "b_gate_now", [P, 2, 2])
            sg = self.sb(c, "sig", [P, 2, 2, CW])
            mm_ = self.sb(c, "gated", [P, 2, 2, CW])
            ps = self.ps(c, "ps_merge", [P, 2, 4, 512])
            b_in, prod, bcp, sgd, gated, summed = self.sems("bg_in", "mprod", "bcp", "sgd", "gated", "summed")
            w_in = self.sems("wm_in0", "wm_in1")

            @block.sync
            def _(e):
                e.dma_start(gb[:], i["b_gate"]).then_inc(b_in, 16)
                with e.Fori(0, KT // 2) as t:
                    for s in range(2):
                        e.wait_ge(prod, NC * (2 * t + s))
                        e.dma_start(w[:, s, :, :], i["w_merge"][ds(2 * t + s, 1)].rearrange("o p k f -> (o p) k f")
                                    ).then_inc(w_in[s], 16)

            @block.tensor
            def _(e):
                e.sem_inc(prod, NC)
                with e.Fori(0, KT // 2) as t:
                    for s in range(2):
                        e.wait_ge(w_in[s], 16 * (t + 1))
                        for n in range(NC):
                            u = (2 * t + s) * NC + n
                            z = (s * NC + n) % 2
                            e.wait_ge(gated, 2 * u)
                            cols = slice(n * CW, (n + 1) * CW)
                            k0 = 0
                            for m, (rhs, K) in enumerate(((self.hT, KT), (self.hT, KT), (self.attT, NPAIR),
                                                          (rwT, NPAIR))):
                                for k in range(K):
                                    mm = e.matmul(ps[:, z, m, 0:CW], w[:, s, k0 + k, :], rhs[:, k, cols],
                                                  start=(k == 0), stop=(k == K - 1))
                                k0 += K
                            mm.then_inc(prod, 1)

            @block.scalar
            def _(e):
                e.wait_ge(b_in, 16)
                with e.Fori(0, KT // 2) as t:
                    for s in range(2):
                        e.copy(bcol[:, s, :], gb[:, ds(2 * t + s, 1), :].rearrange("p o f -> p (o f)")
                               ).then_inc(bcp, 1)
                        e.wait_ge(bcp, 2 * t + s + 1)
                        for n in range(NC):
                            u = (2 * t + s) * NC + n
                            z = (s * NC + n) % 2
                            e.wait_ge(prod, NC + u + 1)
                            e.wait_ge(gated, 2 * u)
                            for m in range(2):
                                e.activation(sg[:, z, m, :], ps[:, z, m, 0:CW], ACT.Sigmoid,
                                             bias=bcol[:, s, m:m + 1]).then_inc(sgd, 1)

            @block.vector
            def _(e):
                e.sem_inc(gated, 2)
                with e.Fori(0, KT // 2) as t:
                    for s in range(2):
                        for n in range(NC):
                            u = (2 * t + s) * NC + n
                            z = (s * NC + n) % 2
                            e.wait_ge(sgd, 2 * (u + 1))
                            e.wait_ge(summed, u)
                            for m in range(2):
                                e.tensor_tensor(mm_[:, z, m, :], sg[:, z, m, :], ps[:, z, 2 + m, 0:CW], ALU.mult
                                                ).then_inc(gated, 1)

            @block.gpsimd
            def _(e):
                e.sem_inc(summed, 1)
                with e.Fori(0, KT // 2) as t:
                    for s in range(2):
                        for n in range(NC):
                            u = (2 * t + s) * NC + n
                            z = (s * NC + n) % 2
                            e.wait_ge(gated, 2 * (u + 2))
                            e.tensor_tensor(outT[:, ds(2 * t + s, 1), n * CW:(n + 1) * CW].rearrange("p o f -> p (o f)"),
                                            mm_[:, z, 0, :], mm_[:, z, 1, :], ALU.add).then_inc(summed, 1)

    def output_projection(self):
        nc, i = self.nc, self.i
        merged = self.mixed[:, NPAIR:NPAIR + KT, :]
        with self.stage() as (c, block):
            w = self.sb(c, "w_o", [P, KT, D])
            g = self.sb(c, "g2row", [P, D])
            epsc = self.sb(c, "eps2", [P, 1])
            x = self.sb(c, "x_rows", [P, 2, D])
            h = self.sb(c, "h_rows", [P, 2, D])
            sq = self.sb(c, "sq2", [P, D])
            col = self.sb(c, "col2", [P, 2, 2])
            ps = self.ps(c, "ps_o", [P, 2, 2, 512])
            pt = self.ps(c, "ps_t", [P, 2, 4, P])
            g_in, eps_set, prod, x1d, ssd, rootd, vst, hd, tp, tc = self.sems(
                "g2_in", "eps2_set", "oprod", "x1_done", "ssd", "root2", "v2", "h2_done", "h2_t", "h2_c")
            w_in = self.sems(*[f"wo_in{k}" for k in range(KT)])
            x_in = self.sems("xr_in0", "xr_in1")
            x1_out = self.sems("x1_out0", "x1_out1")
            h2_out = self.sems("h2_out0", "h2_out1")

            @block.sync
            def _(e):
                for k in range(KT):
                    e.dma_start(w[:, k, :], i["w_o"][k * P:(k + 1) * P, :]).then_inc(w_in[k], 16)
                e.dma_start(g[:], i["norm2_g"].to_broadcast([P, D])).then_inc(g_in, 16)
                for m in range(TT):
                    n, s = tokens_in(m), m % 2
                    if m >= 2:
                        e.wait_ge(x1_out[s], 16 * (m // 2))
                        e.wait_ge(hd, m - 1)
                        e.wait_ge(ssd, m - 1)
                    e.dma_start(x[0:n, s, :], i["x"][m * P:m * P + n, :]).then_inc(x_in[s], 16)

            @block.tensor
            def _(e):
                def product(m):
                    n, s = tokens_in(m), m % 2
                    if m >= 2:
                        e.wait_ge(x1d, m - 1)
                    for k in range(KT):
                        if m == 0:
                            e.wait_ge(w_in[k], 16)
                        for d in range(2):
                            mm = e.matmul(ps[0:n, s, d, :], merged[:, k, m * P:m * P + n],
                                          w[:, k, d * 512:(d + 1) * 512], start=(k == 0), stop=(k == KT - 1))
                    mm.then_inc(prod, 1)

                def turn(m):
                    n, s = tokens_in(m), m % 2
                    e.wait_ge(hd, m + 1)
                    for d in range(2):
                        if m:
                            e.wait_ge(tc, 2 * (m - 1) + d + 1)
                        for k in range(4):
                            mm = e.transpose(pt[:, d, k, 0:n], h[0:n, s, (4 * d + k) * P:(4 * d + k + 1) * P],
                                             self.ident[0:n, 0:n])
                        mm.then_inc(tp, 1)

                product(0)
                for m in range(TT):
                    if m + 1 < TT:
                        product(m + 1)
                    turn(m)

            @block.scalar
            def _(e):
                e.wait_ge(eps_set, 1)
                for m in range(TT):
                    n, s = tokens_in(m), m % 2
                    e.wait_ge(x1d, m + 1)
                    if m:
                        e.wait_ge(ssd, m)
                    e.activation(sq[0:n, :], x[0:n, s, :], ACT.Square, accum_out=col[0:n, s, 0:1]).then_inc(ssd, 1)
                    e.wait_ge(ssd, m + 1)
                    e.activation(col[0:n, s, 1:2], col[0:n, s, 0:1], ACT.Sqrt, bias=epsc[0:n, :], scale=1.0 / D
                                 ).then_inc(rootd, 1)
                    e.dma_start(self.x1_d[m * P:m * P + n, :], x[0:n, s, :]).then_inc(x1_out[s], 16)
                    for d in range(2):
                        e.wait_ge(tp, 2 * m + d + 1)
                        e.copy(self.hT[:, 4 * d:4 * d + 4, m * P:m * P + n], pt[:, d, :, 0:n]).then_inc(tc, 1)
                    e.dma_start(self.h2_d[m * P:m * P + n, :], h[0:n, s, :]).then_inc(h2_out[s], 16)
                e.wait_ge(tc, 2 * TT)
                for q in (x1_out, h2_out):
                    e.wait_ge(q[0], 16 * ((TT + 1) // 2))
                    e.wait_ge(q[1], 16 * (TT // 2))

            @block.vector
            def _(e):
                e.memset(epsc[:], EPS).then_inc(eps_set, 1)
                e.wait_ge(g_in, 16)
                for m in range(TT):
                    n, s = tokens_in(m), m % 2
                    e.wait_ge(prod, m + 1)
                    e.wait_ge(x_in[s], 16 * (m // 2 + 1))
                    e.tensor_tensor(x[0:n, s, :], ps[0:n, s, :, :].rearrange("p a b -> p (a b)"), x[0:n, s, :], ALU.add
                                    ).then_inc(x1d, 1)
                    e.wait_ge(rootd, m + 1)
                    e.reciprocal(col[0:n, s, 1:2], col[0:n, s, 1:2]).then_inc(vst, 1)
                    e.wait_ge(vst, m + 1)
                    if m >= 2:
                        e.wait_ge(h2_out[s], 16 * (m // 2))
                        e.wait_ge(tp, 2 * (m - 1))
                    e.scalar_tensor_tensor(out=h[0:n, s, :], in0=x[0:n, s, :], scalar=col[0:n, s, 1:2],
                                           in1=g[0:n, :], op0=ALU.mult, op1=ALU.mult).then_inc(hd, 1)

    def scores(self):
        nc, i = self.nc, self.i
        with self.stage() as (c, block):
            w = self.sb(c, "w_query", [P, 2, KT, P])
            sk = self.sb(c, "sub_keys", [P, 2, NKEY])
            q = self.sb(c, "query", [P, 2, T])
            so = self.sb(c, "scores", [P, 2, TT, NKEY])
            zs = self.sb(c, "no_scores", [P, PH, 2 * NKEY])
            pq = self.ps(c, "ps_query", [P, NC, 512])
            pscore = self.ps(c, "ps_score", [P, NC, 512])
            q_d, q_c, s_d, s_c, zs_set, zs_out = self.sems(
                "q_done", "q_copied", "s_done2", "s_copied", "zs_set", "zs_out")
            w_in, sk_in, s_out = (self.sems(n + "0", n + "1") for n in ("wq2_in", "sk_in", "s_out"))

            @block.sync
            def _(e):
                with e.Fori(0, PH) as h:
                    for z in range(2):
                        u = 2 * h + z
                        e.wait_ge(s_d, u)
                        e.dma_start(w[:, z, :, :], i["w_query"][ds(u, 1)].rearrange("o p k f -> (o p) k f")
                                    ).then_inc(w_in[z], 16)
                        e.dma_start(sk[:, z, :], i["sub_keys"][ds(u, 1)].rearrange("o p f -> (o p) f")
                                    ).then_inc(sk_in[z], 16)

            @block.tensor
            def _(e):
                e.sem_inc(s_d, 1)
                with e.Fori(0, PH) as h:
                    for z in range(2):
                        u = 2 * h + z
                        e.wait_ge(w_in[z], 16 * (h + 1))
                        e.wait_ge(q_c, u)
                        for k in range(KT):
                            for n in range(NC):
                                mm = e.matmul(pq[:, n, 0:CW], w[:, z, k, :], self.hT[:, k, n * CW:(n + 1) * CW],
                                              start=(k == 0), stop=(k == KT - 1))
                        mm.then_inc(q_d, 1)
                        e.wait_ge(q_c, u + 1)
                        e.wait_ge(sk_in[z], 16 * (h + 1))
                        e.wait_ge(s_c, 2 * u)
                        for m in range(TT):
                            n = tokens_in(m)
                            mm = e.matmul(pscore[0:n, m // 4, (m % 4) * P:(m % 4 + 1) * P], q[:, z, m * P:m * P + n],
                                          sk[:, z, :], start=True, stop=True)
                        mm.then_inc(s_d, 1)

            @block.scalar
            def _(e):
                with e.Fori(0, PH) as h:
                    for z in range(2):
                        u = 2 * h + z
                        e.wait_ge(q_d, u + 1)
                        e.wait_ge(s_d, u)
                        e.copy(q[:, z, :].rearrange("p (n w) -> p n w", n=NC), pq[:, :, 0:CW]).then_inc(q_c, 1)

            @block.vector
            def _(e):
                with e.Fori(0, PH) as h:
                    for z in range(2):
                        u = 2 * h + z
                        e.wait_ge(s_d, u + 2)
                        e.wait_ge(s_out[z], 32 * h)
                        e.tensor_copy(so[:, z, 0:8, :].rearrange("p (a b) k -> p a (b k)", a=2), pscore[:, 0:2, :]
                                      ).then_inc(s_c, 1)
                        e.tensor_copy(so[0:TS, z, 8, :], pscore[0:TS, 2, 0:P]).then_inc(s_c, 1)

            @block.gpsimd
            def _(e):
                e.memset(zs[:], 0.0).then_inc(zs_set, 1)
                e.wait_ge(zs_set, 1)
                e.dma_start(self.s_d[TT - 1, :, TS:P, :].rearrange("h p k -> p h k"), zs[0:P - TS]).then_inc(zs_out, 16)
                e.dma_start(self.s_d[TT, 0, :, :], zs[:, 0, :]).then_inc(zs_out, 16)
                e.wait_ge(zs_out, 32)
                with e.Fori(0, PH) as h:
                    for z in range(2):
                        u = 2 * h + z
                        e.wait_ge(s_c, 2 * (u + 1))
                        cols = slice(z * NKEY, (z + 1) * NKEY)
                        e.dma_start(self.s_d[0:TT - 1, ds(h, 1), :, cols].rearrange("m o p k -> p (m o) k"),
                                    so[:, z, 0:TT - 1, :]).then_inc(s_out[z], 16)
                        e.dma_start(self.s_d[TT - 1:TT, ds(h, 1), 0:TS, cols].rearrange("m o p k -> p (m o) k"),
                                    so[0:TS, z, TT - 1:TT, :]).then_inc(s_out[z], 16)
                for z in range(2):
                    e.wait_ge(s_out[z], 32 * PH)

    def experts(self, first, tiles, R):
        nc, i, o = self.nc, self.i, self.o
        RING, G = 16, 4
        NG = TOPK // G
        NU = tiles * PH
        with self.stage() as (c, block):
            sb = lambda name, shape, dt=F32: self.sb(c, f"{name}{first}", shape, dt)
            ring = sb("ring", [P, RING, 2 * D])
            hrow = sb("h2_tile", [P, D])
            xrow = sb("x1_tile", [P, D])
            grow = sb("gf_row", [P, D])
            epsc = sb("eps3", [P, 1])
            sc = sb("s_unit", [P, 2, 2, NKEY])
            sm = sb("s_left", [P, 2, NKEY])
            sv = sb("top_s", [P, 2, TOPK])
            si = sb("top_i", [P, 2, TOPK], U32)
            sif = sb("top_if", [P, 2, TOPK])
            cand = sb("cand", [P, TOPK * TOPK])
            cleft = sb("cand_left", [P, TOPK * TOPK])
            bs = sb("best_s", [P, TOPK])
            bp = sb("best_pos", [P, TOPK], U32)
            ab_ = sb("pos_ab", [P, 2, TOPK], U32)
            abf = sb("pos_abf", [P, 2, TOPK])
            iota = sb("iota", [P, TOPK])
            hot = sb("hot", [P, 2, TOPK, TOPK])
            pick = sb("pick", [P, 2, TOPK])
            idx = sb("expert_id", [P, 2, TOPK], U32)
            nmax = sb("neg_max", [P, 1])
            ex = sb("exp_s", [P, 2, TOPK])
            den = sb("gate_den", [P, 2, 1])
            gate = sb("gate", [P, 2, TOPK])
            dot = sb("dots", [P, 2, TOPK])
            act = sb("acts", [P, 2, TOPK])
            wt = sb("weights", [P, 2, TOPK])
            diag = sb("diag", [P, 2 * G, P])
            zero = sb("zero", [P, P])
            x2 = sb("x2", [P, D])
            sq = sb("sq3", [P, D])
            col = sb("col3", [P, 2])
            yrow = sb("y_tile", [P, D])
            acc = self.ps(c, f"acc{first}", [P, 2, 512])
            passed, c_in, zset, tk, idx_d, exp_d, gate_d, dots, gelu, wtd, diagd, pv, accd, x2d, ssd, rootd, vend, yd, y_out \
                = self.sems("passed", "c3_in", "zset3", "topk", "idx_done", "exp_done", "gate_done", "dots_done", "gelu_done",
                            "wt_done", "diag_done", "v_used", "acc_done", "x2_done", "ss3", "root3", "vend", "y_done",
                            "y_out")
            s_in = self.sems("su_in0", "su_in1")
            h_in, x_in = self.sems("hr_in", "x1r_in")
            uv_in = self.sems(*[f"uv_in{n}" for n in range(RING)])
            r = slice(0, R)
            TKN = 26

            @block.sync
            def _(e):
                e.dma_start(grow[:], i["final_g"].to_broadcast([P, D])).then_inc(c_in, 16)
                e.dma_start(iota[:], i["iota"].to_broadcast([P, TOPK])).then_inc(c_in, 16)

                def unit_scores(u, z):
                    e.dma_start(sc[r, z, :, :], self.s_d.rearrange("m h p k -> (m h) p k")
                                [ds(u + first * PH, 1), 0:R, :].rearrange("o p (z k) -> (o p) z k", z=2)
                                ).then_inc(s_in[z], 16)
                unit_scores(0, 0)
                with e.Fori(0, tiles) as m:
                    e.wait_ge(dots, NG * PH * m)
                    e.dma_start(hrow[r, :], self.h2_d[ds(first * P + m * P, R), :]).then_inc(h_in, 16)
                    e.wait_ge(accd, m)
                    e.dma_start(xrow[r, :], self.x1_d[ds(first * P + m * P, R), :]).then_inc(x_in, 16)
                    with e.Fori(0, PH // 2) as hh:
                        for z in range(2):
                            u = m * PH + 2 * hh + z
                            e.wait_ge(idx_d, u)
                            un = u + 1 if z == 0 else u + 1
                            if z == 0:
                                unit_scores(un, 1)
                            else:
                                unit_scores(un, 0)
                    e.wait_ge(yd, m + 1)
                    e.dma_start(o["y"][ds(first * P + m * P, R), :], yrow[r, :]).then_inc(y_out, 16)
                e.wait_ge(y_out, 16 * tiles)

            @block.gpsimd
            def _(e):
                with e.Fori(0, NU // 2) as t:
                    for z in range(2):
                        u = 2 * t + z
                        e.wait_ge(idx_d, u + 1)
                        for k in range(TOPK):
                            e.wait_ge(pv, TOPK * u + k + 1)
                            e.sem_inc(passed, 1)
                            e.indirect_dma_start(out=ring[r, k, :], out_offset=None, in_=i["uv"],
                                                 in_offset=bass.IndirectOffsetOnAxis(ap=idx[r, z, k:k + 1], axis=0)
                                                 ).then_inc(uv_in[k], 16)

            @block.vector
            def _(e):
                e.memset(epsc[:], EPS).then_inc(zset, 1)
                e.memset(zero[:], 0.0).then_inc(zset, 1)

                def find(u, z):
                    ch = Chain(e, tk, TKN * u)
                    e.wait_ge(s_in[z], 16 * (t_of(u, z) + 1))
                    e.sem_inc(passed, 1)
                    for half in range(2):
                        s_ = sc[r, z, half, :]
                        ch(e.max(out=sv[r, half, 0:8], in_=s_))
                    ch.settle()
                    e.sem_inc(passed, 1)
                    for half in range(2):
                        s_ = sc[r, z, half, :]
                        ch(e.max_index(out=si[r, half, 0:8], in_max=sv[r, half, 0:8], in_values=s_))
                        ch(e.match_replace(out=sm[r, half, :], in_to_replace=sv[r, half, 0:8], in_values=s_,
                                           imm_value=-3.0e38))
                    ch.settle()
                    e.sem_inc(passed, 1)
                    for half in range(2):
                        ch(e.max(out=sv[r, half, 8:16], in_=sm[r, half, :]))
                    ch.settle()
                    e.sem_inc(passed, 1)
                    for half in range(2):
                        ch(e.max_index(out=si[r, half, 8:16], in_max=sv[r, half, 8:16], in_values=sm[r, half, :]))
                    ch(e.tensor_tensor(cand[r, :].rearrange("p (a b) -> p a b", a=TOPK),
                                       sv[r, 0, :].unsqueeze(2).to_broadcast([R, TOPK, TOPK]),
                                       sv[r, 1, :].unsqueeze(1).to_broadcast([R, TOPK, TOPK]), ALU.add))
                    ch.settle()
                    ch(e.tensor_copy(sif[r], si[r]))
                    ch(e.max(out=bs[r, 0:8], in_=cand[r, :]))
                    ch.settle()
                    ch(e.tensor_scalar(nmax[r], bs[r, 0:1], -1.0, None, ALU.mult))
                    ch(e.max_index(out=bp[r, 0:8], in_max=bs[r, 0:8], in_values=cand[r, :]))
                    ch(e.match_replace(out=cleft[r, :], in_to_replace=bs[r, 0:8], in_values=cand[r, :],
                                       imm_value=-3.0e38))
                    ch.settle()
                    e.sem_inc(passed, 1)
                    ch(e.max(out=bs[r, 8:16], in_=cleft[r, :]))
                    ch.settle()
                    e.sem_inc(passed, 1)
                    ch(e.max_index(out=bp[r, 8:16], in_max=bs[r, 8:16], in_values=cleft[r, :]))
                    ch.settle()
                    ch(e.tensor_scalar(ab_[r, 0, :], bp[r, :], 4, None, ALU.logical_shift_right))
                    ch(e.tensor_scalar(ab_[r, 1, :], bp[r, :], 15, None, ALU.bitwise_and))
                    ch.settle()
                    ch(e.tensor_copy(abf[r], ab_[r]))
                    ch.settle()
                    for half in range(2):
                        ch(e.tensor_tensor(hot[r, half], abf[r, half, :].unsqueeze(2).to_broadcast([R, TOPK, TOPK]),
                                           iota[r, :].unsqueeze(1).to_broadcast([R, TOPK, TOPK]), ALU.is_equal))
                    ch.settle()
                    ch(e.tensor_tensor(hot[r], hot[r], sif[r].unsqueeze(2).to_broadcast([R, 2, TOPK, TOPK]), ALU.mult))
                    ch.settle()
                    ch(e.tensor_reduce(pick[r], hot[r], AX.X, ALU.add))
                    ch.settle()
                    assert ch.n == TKN - 1, ch.n
                    ch(e.scalar_tensor_tensor(out=idx[r, z, :], in0=pick[r, 0, :], scalar=float(NKEY),
                                              in1=pick[r, 1, :], op0=ALU.mult, op1=ALU.add))
                    ch.settle()
                    e.sem_inc(idx_d, 1)

                e.wait_ge(c_in, 32)

                def finish_gate(u, z):
                    e.wait_ge(exp_d, u + 1)
                    e.reciprocal(den[r, z, :], den[r, z, :]).then_inc(gate_d, 1)
                    e.wait_ge(gate_d, 2 * u + 1)
                    e.tensor_scalar(gate[r, z, :], ex[r, z, :], den[r, z, :], None, ALU.mult).then_inc(gate_d, 1)

                t_of = lambda u, z: 0
                find(0, 0)
                with e.Fori(0, tiles) as m:
                    with e.Fori(0, PH // 2) as hh:
                        for z in range(2):
                            u = m * PH + 2 * hh + z
                            v = (m * PH + 2 * hh) // 2 if False else m * (PH // 2) + hh
                            finish_gate(u, z)
                            if z == 0:
                                e.wait_ge(h_in, 16 * (m + 1))
                            for g in range(NG):
                                for k in range(G * g, G * (g + 1)):
                                    e.wait_ge(uv_in[k], 16 * (u + 1))
                                    mm = e.tensor_tensor_reduce(ring[r, k, 0:D], ring[r, k, 0:D], hrow[r, :], 1.0, 0.0,
                                                                ALU.mult, ALU.add, dot[r, z, k:k + 1])
                                mm.then_inc(dots, 1)
                                if g == 1:
                                    t_of = lambda u_, z_: v + (1 if z_ == 0 else 0)
                                    find(u + 1, 1 - z)
                                e.wait_ge(gelu, NG * u + g + 1)
                                ks = slice(G * g, G * (g + 1))
                                e.tensor_tensor(wt[r, z, ks], act[r, z, ks], gate[r, z, ks], ALU.mult
                                                ).then_inc(wtd, 1)
                    e.wait_ge(rootd, m + 1)
                    e.reciprocal(col[r, 1:2], col[r, 1:2]).then_inc(vend, 1)
                    e.wait_ge(vend, m + 1)
                    e.wait_ge(y_out, 16 * m)
                    e.scalar_tensor_tensor(out=yrow[r, :], in0=x2[r, :], scalar=col[r, 1:2], in1=grow[r, :],
                                           op0=ALU.mult, op1=ALU.mult).then_inc(yd, 1)

            @block.scalar
            def _(e):
                e.wait_ge(zset, 2)

                def exps(u, z):
                    e.wait_ge(idx_d, u + 1)
                    e.activation(ex[r, z, :], bs[r, :], ACT.Exp, bias=nmax[r], accum_out=den[r, z, :]).then_inc(exp_d, 1)

                exps(0, 0)
                with e.Fori(0, tiles) as m:
                    with e.Fori(0, PH // 2) as hh:
                        for z in range(2):
                            u = m * PH + 2 * hh + z
                            for g in range(NG):
                                ks = slice(G * g, G * (g + 1))
                                e.wait_ge(dots, NG * u + g + 1)
                                e.activation(act[r, z, ks], dot[r, z, ks], ACT.Gelu).then_inc(gelu, 1)
                                e.wait_ge(wtd, NG * u + g + 1)
                                for k in range(G * g, G * (g + 1)):
                                    e.wait_ge(pv, TOPK * u + k + TOPK - 2 * G + 1)
                                    e.mul(diag[r, k % (2 * G), :], self.ident[r, :], wt[r, z, k:k + 1]
                                          ).then_inc(diagd, 1)
                            exps(u + 1, 1 - z)
                    e.wait_ge(accd, m + 1)
                    e.wait_ge(yd, m)
                    e.copy(x2[r, :], acc[r, :, :].rearrange("p a b -> p (a b)")).then_inc(x2d, 1)
                    e.wait_ge(x2d, m + 1)
                    e.activation(sq[r, :], x2[r, :], ACT.Square, accum_out=col[r, 0:1]).then_inc(ssd, 1)
                    e.wait_ge(ssd, m + 1)
                    e.activation(col[r, 1:2], col[r, 0:1], ACT.Sqrt, bias=epsc[r], scale=1.0 / D).then_inc(rootd, 1)

            @block.tensor
            def _(e):
                e.wait_ge(zset, 2)
                e.sem_inc(pv, TOPK)
                with e.Fori(0, tiles) as m:
                    e.wait_ge(x_in, 16 * (m + 1))
                    e.wait_ge(x2d, m)
                    for d in range(2):
                        e.matmul(acc[r, d, :], self.ident[r, r], xrow[r, d * 512:(d + 1) * 512], start=True, stop=False)
                    with e.Fori(0, PH // 2) as hh:
                        for z in range(2):
                            u = m * PH + 2 * hh + z
                            for k in range(TOPK):
                                e.wait_ge(diagd, TOPK * u + k + 1)
                                if R < P:
                                    e.sem_inc(passed, 1)
                                for d in range(2):
                                    mm = e.matmul(acc[r, d, :], diag[r, k % (2 * G), r],
                                                  ring[r, k, D + d * 512:D + (d + 1) * 512], start=False, stop=False)
                                mm.then_inc(pv, 1)
                    for d in range(2):
                        mm = e.matmul(acc[r, d, :], zero[r, r], xrow[r, d * 512:(d + 1) * 512], start=False, stop=True)
                    mm.then_inc(accd, 1)


def layout(inp):
    a = {k: np.ascontiguousarray(v) for k, v in inp.items()}
    f = np.float32
    eye = np.eye(P, dtype=f)
    head = np.kron(np.eye(2, dtype=f), np.ones((HD, HD), f))
    x = np.concatenate([a["x_prompt"].reshape(TP, D), a["x_sample"].reshape(TS, D)])
    w_in = a["w_in"][0]
    main = slice(OFF_B, OFF_B + 3 * RW)
    lora = slice(OFF_B + 3 * RW, OFF_G)
    tiles = lambda v: v.reshape(-1, P).T

    def loras(v):
        v = np.moveaxis(v, -1, 0)
        out = np.zeros((LG, 3) + v.shape[1:], f)
        for m, (off, n) in enumerate(((0, LW), (LW, LA), (LW + LA, LG))):
            out[:n, m] = v[off:off + n]
        return out

    pos = np.concatenate([np.arange(TP), np.tile(8192 + np.arange(NS), NB)]).astype(f)
    pos = np.concatenate([pos, np.zeros(TT * P - T, f)])
    angle = pos[:, None] * (f(500000.0) ** (-np.arange(RH, dtype=f) / f(RH)))[None, :]
    rope = [fn(angle).astype(f).reshape(TT, P, RH).transpose(1, 0, 2) for fn in (np.cos, np.sin)]
    diff = WIN + np.arange(WIN)[:, None] - np.arange(2 * WIN)[None, :]
    seen = (diff >= 0) & (diff < WIN)
    band = np.where(seen, f(0), f(NEG))
    first = np.where(seen & (np.arange(2 * WIN) >= WIN)[None, :], f(0), f(NEG))
    row_b, row_n = (np.tile(z, NQ // NKV)[:, None] for z in (np.repeat(np.arange(NB), NS), np.tile(np.arange(NS), NB)))
    key_b = np.concatenate([np.repeat(np.arange(NB), WIN), np.repeat(np.arange(NB), NS)])[None, :]
    key_j = np.concatenate([np.tile(np.arange(WIN), NB), WIN + np.tile(np.arange(NS), NB)])[None, :]
    ddiff = WIN + row_n - key_j
    dmask = np.where((row_b == key_b) & (ddiff >= 0) & (ddiff < WIN), f(0), f(NEG))
    ct = np.tile(np.arange(CH), 2)
    levels = []
    for n in range(LEVELS):
        half = 1 << n
        same = ct[:, None] // (2 * half) == ct[None, :] // (2 * half)
        levels.append((head * same * ((ct // half) % 2 == 0)[:, None] * ((ct // half) % 2 == 1)[None, :]).astype(f))
    db, dn = np.tile(np.repeat(np.arange(NB), NS), 2), np.tile(np.arange(NS), 2 * NB)
    dh = np.repeat(np.arange(2), TS)
    dsame = (db[:, None] == db[None, :]) & (dh[:, None] == dh[None, :])
    dl0 = dsame & (dn[:, None] // 2 == dn[None, :] // 2) & (dn[:, None] < dn[None, :])
    dl1 = dsame & (dn[:, None] < 2) & (dn[None, :] >= 2)
    state0 = np.zeros((2, HD, NPAIR, NB, 2, HD), f)
    start = a["state_wkv"][0].reshape(NB, NPAIR, 2, HD, HD)
    for h in range(2):
        state0[h, :, :, :, h, :] = start[:, :, h].transpose(3, 1, 0, 2)
    state0 = state0.reshape(P, NPAIR, NB, P)
    blocks = lambda w: w.reshape(-1, P, w.shape[1] // P, P).transpose(2, 1, 0, 3)
    pairs = lambda w: w.reshape(w.shape[0], NPAIR, P).transpose(1, 0, 2)
    mu, b_in, sh = a["shift_mu"][0], a["b_in"][0], a["state_shift"][0]
    return {
        "ident": eye, "ones": np.ones((P, P), f), "headones": head,
        "xT": x.T, "x": x,
        "norm1_g": tiles(a["norm1_g"][0]),
        "w_in": w_in, "b_qkv": b_in[None, :QKV],
        "w_main": w_in[:, main].reshape(KT, P, NMAIN, P).transpose(2, 1, 0, 3),
        "w_lora": w_in[:, lora].reshape(KT, P, -1).transpose(1, 0, 2),
        "b_main": tiles(b_in[main]), "mu_main": tiles(mu[:3 * RW]),
        "shift_main": sh[:, :3 * RW].reshape(NB, NMAIN, P).transpose(2, 1, 0),
        "lora_b": loras(b_in[lora]), "lora_mu": loras(mu[3 * RW:]),
        "lora_shift": loras(sh[:, 3 * RW:]),
        "cos": rope[0], "sin": rope[1], "band": band, "band_first": first,
        "sinks": a["attn_sinks"].reshape(NKV, 2, 2).transpose(0, 2, 1).reshape(1, NQ),
        "cache_k": a["cache_win_k"].reshape(NB, WIN, KW), "cache_v": a["cache_win_v"].reshape(NB, WIN, KW),
        "w2": pairs(a["w2"][0]), "a2": pairs(a["a2"][0]), "g2": pairs(a["g2"][0]),
        "pair_par": np.stack([a[n][0].reshape(NPAIR, P) for n in ("w0", "a0", "k_k", "k_a", "r_k")], axis=-1),
        "level_masks": np.stack(levels, axis=1), "low0": levels[0].T,
        "before": (head * (ct[:, None] < ct[None, :])).astype(f),
        "upto": np.stack([(ct[:, None] <= np.arange(CH)[None, :])] * 2, axis=1).astype(f),
        "dec_masks": np.stack([dsame * (dn[:, None] < dn[None, :]), dl0, dl1, dl0.T], axis=1).astype(f),
        "dec_upto": np.stack([(db[:, None] == db[None, :TS]) & (dn[:, None] <= dn[None, :TS])] * 2, axis=1).astype(f),
        "dec_own": (db[:, None] == np.arange(NB)[None, :]).astype(f),
        "state0": state0,
        "gn_par": np.stack([tiles(a["ln_x_w"][0]), tiles(a["ln_x_b"][0])], axis=1),
        "w_merge": np.concatenate([blocks(w_in[:, OFF_G:OFF_G + D]), blocks(w_in[:, OFF_G + D:]),
                                   blocks(a["w_up_a"][0]), blocks(a["w_up_b"][0])], axis=2),
        "b_gate": b_in[OFF_G:].reshape(2, KT, P).transpose(2, 1, 0),
        "w_o": a["w_o"][0], "norm2_g": a["norm2_g"], "final_g": a["final_norm_g"][None],
        "w_query": blocks(a["w_query"][0]),
        "sub_keys": a["sub_keys"][0].reshape(NHALF, NKEY, P).transpose(0, 2, 1),
        "uv": np.concatenate([a["expert_u"][0], a["expert_v"][0]], axis=1),
        "iota": np.arange(TOPK, dtype=f)[None],
        "dmask": dmask, "dsink": np.repeat(a["attn_sinks"].reshape(NKV, NQ // NKV), TS, axis=1).T,
    }


OUTS = {"y": (T, D), "prompt_win_k": (WIN, KW), "prompt_win_v": (WIN, KW), "prompt_wkv": (NQ, HD, HD),
        "shift": (1 + NB, OFF_G - OFF_B), "sample_win_k": (NB, WIN, KW), "sample_win_v": (NB, WIN, KW),
        "sample_wkv": (NB, NQ, HD, HD)}


def kernel(**inputs):
    import concourse.bacc as _bacc
    from concourse.bass_utils import run_bass_kernel_spmd as _run

    nc = _bacc.Bacc("TRN2", target_bir_lowering=False, num_devices=1)
    arrays, ins, outs = {}, {}, {}
    for name, array in layout(inputs).items():
        array = np.ascontiguousarray(array)
        arrays[f"in_{name}_dram"] = array
        ins[name] = nc.dram_tensor(f"in_{name}_dram", array.shape, mybir.dt.from_np(array.dtype),
                                   kind="ExternalInput").ap()
    for name, shape in OUTS.items():
        outs[name] = nc.dram_tensor(f"out_{name}_dram", shape, F32, kind="ExternalOutput").ap()
    Program(nc, ins, outs).build()
    r = _run(nc, [arrays], core_ids=[0])
    got = {name: np.asarray(r.results[0][f"out_{name}_dram"]) for name in OUTS}
    win = lambda name, *lead: got[name].reshape(lead + (WIN, NKV, HD))
    wkv = lambda name, *lead: np.ascontiguousarray(got[name].reshape(lead + (NQ, HD, HD)).swapaxes(-1, -2))
    return (got["y"][:TP].reshape(1, TP, D), got["y"][TP:].reshape(NB, NS, D),
            win("prompt_win_k", 1, 1), win("prompt_win_v", 1, 1), wkv("prompt_wkv", 1, 1), got["shift"][None, :1],
            win("sample_win_k", 1, NB), win("sample_win_v", 1, NB), wkv("sample_wkv", 1, NB), got["shift"][None, 1:])
```

```python
from contextlib import ExitStack, contextmanager

import numpy as np
import concourse.bass as bass
from concourse import mybir

ALU = mybir.AluOpType
ACT = mybir.ActivationFunctionType
AX = mybir.AxisListType
F32 = mybir.dt.float32
U32 = mybir.dt.uint32
ds = bass.ds

P = 128
D = 1024
KT = D // P
TP = 1024
NB, NS = 8, 4
TS = NB * NS
T = TP + TS
TT = (T + P - 1) // P
NC = 3
CW = T // NC
HD = 64
NQ, NKV = 8, 2
QW, KW = NQ * HD, NKV * HD
QKV = QW + 2 * KW
ROT = HD // 4
RH = ROT // 2
WIN = 128
NBLK = TP // WIN
RW = 512
NPAIR = RW // P
LW, LA, LG = 32, 32, 96
NMAIN = 3 * RW // P
OFF_B = QKV
OFF_G = OFF_B + 3 * RW + LW + LA + LG
CH = 64
LANES = 4
NQUAD = TP // CH // LANES
LEVELS = 6
PH, NKEY, TOPK = 8, 128, 16
NHALF = 2 * PH
NSLOT = PH * TOPK
WORK = (25 + LEVELS - 1) * LANES * P + 2 * LANES + 6 * P
NEG = -1.0e30
EPS = 1e-5
GN_EPS = 64e-5
SCALE = HD ** -0.5


def tokens_in(tile):
    return P if tile < TP // P else TS


class Chain:

    def __init__(self, eng, sem, base=0):
        self.eng, self.sem, self.base, self.n = eng, sem, base, 0

    def __call__(self, ins):
        ins.then_inc(self.sem, 1)
        self.n += 1
        return ins

    def settle(self):
        self.eng.wait_ge(self.sem, self.base + self.n)


class Carver:

    def __init__(self, buffer):
        self.buffer, self.at = buffer, 0

    def __call__(self, *shape):
        n = int(np.prod(shape))
        part = self.buffer[:, self.at:self.at + n]
        self.at += n
        if len(shape) == 2:
            return part.rearrange("p (a b) -> p a b", a=shape[0])
        if len(shape) == 3:
            return part.rearrange("p (a b c) -> p a b c", a=shape[0], b=shape[1])
        return part


class Program:

    def __init__(self, nc, i, o):
        self.nc, self.i, self.o = nc, i, o
        self.life = ExitStack()

    def sb(self, ctx, name, shape, dt=F32):
        return ctx.enter_context(self.nc.sbuf_tensor(name, shape, dt))

    def ps(self, ctx, name, shape, dt=F32):
        return ctx.enter_context(self.nc.psum_tensor(name, shape, dt))

    def sems(self, *names):
        new = [self.held.enter_context(self.nc.semaphore(n)) for n in names]
        self.owned += new
        return new

    @contextmanager
    def stage(self):
        nc = self.nc
        with ExitStack() as self.held:
            self.owned = []
            with nc.Block() as block, ExitStack() as c:
                yield c, block
            numbers = sorted(s.num for s in self.owned)
            first = numbers[0]
            for a, b in zip(numbers, numbers[1:] + [None]):
                if b != a + 1:
                    nc.gpsimd.sem_clear(range(first, a + 1))
                    first = b
            nc.all_engine_barrier()

    def build(self, until=99):
        nc = self.nc
        dr = lambda n, s: nc.dram_tensor(n, s, F32).ap()
        self.x1_d = dr("x1_rows", [T, D])
        self.h2_d = dr("h2_rows", [T, D])
        self.s_d = dr("scores_by_unit", [T * PH // P, P, 2 * NKEY])
        with ExitStack() as c:
            self.ident = self.sb(c, "ident", [P, P])
            self.headones = self.sb(c, "headones", [P, P])
            self.ones = self.sb(c, "ones", [P, P])
            with ExitStack() as c1:
                self.hT = self.sb(c1, "hT", [P, KT, T])
                self.attT = self.sb(c1, "attT", [P, QW // P, T])
                with ExitStack() as c2:
                    self.mixed = self.sb(c2, "mixed", [P, NMAIN, T])
                    self.lw = self.sb(c2, "lw", [LW, T])
                    self.la = self.sb(c2, "la", [LA, T])
                    self.lg = self.sb(c2, "lg", [LG, T])
                    with ExitStack() as c3:
                        self.norm_in()
                        self.project_rwkv()
                    with ExitStack() as c3:
                        self.qkv_padded = self.sb(c3, "qkv", [P, 1 + TT, QKV])
                        self.qkv = self.qkv_padded[:, 1:, :]
                        self.project_qkv()
                        if until > 1:
                            self.attention()
                    if until > 2:
                        self.rwkv()
                    if until > 3:
                        self.merge()
                    if until > 4:
                        self.output_projection()
                if until > 5:
                    self.scores()
            if until > 6:
                self.experts()

    def norm_in(self):
        nc, i = self.nc, self.i
        with self.stage() as (c, block):
            rstd = self.sb(c, "rstd", [P, T])
            sq = self.sb(c, "sq", [P, 2, T])
            g = self.sb(c, "g1", [P, KT])
            epsc = self.sb(c, "epsc", [P, 1])
            ms = self.ps(c, "ms", [P, NC, 512])
            consts_in, g_in, eps_set, x_sq, sq_used, root, inv, normed = self.sems(
                "consts_in", "g_in", "eps_set", "x_sq", "sq_used", "root", "inv", "normed")
            x_in = self.sems(*[f"x_in{k}" for k in range(KT)])
            hT = self.hT

            @block.sync
            def _(e):
                e.dma_start(self.ones[:, :], i["ones"]).then_inc(consts_in, 16)
                e.dma_start(self.ident[:, :], i["ident"]).then_inc(consts_in, 16)
                e.dma_start(self.headones[:, :], i["headones"]).then_inc(consts_in, 16)
                for k in range(KT):
                    e.dma_start(hT[:, k, :], i["xT"][k * P:(k + 1) * P, :]).then_inc(x_in[k], 16)
                e.dma_start(g[:, :], i["norm1_g"]).then_inc(g_in, 16)

            @block.scalar
            def _(e):
                for k in range(KT):
                    e.wait_ge(x_in[k], 16)
                    if k >= 2:
                        e.wait_ge(sq_used, k - 1)
                    e.activation(sq[:, k % 2, :], hT[:, k, :], ACT.Square).then_inc(x_sq, 1)
                e.wait_ge(sq_used, KT)
                e.wait_ge(eps_set, 1)
                for n in range(NC):
                    e.activation(rstd[:, n * CW:(n + 1) * CW], ms[:, n, 0:CW], ACT.Sqrt,
                                 bias=epsc[:, 0:1], scale=1.0 / D).then_inc(root, 1)

            @block.tensor
            def _(e):
                e.wait_ge(consts_in, 48)
                for k in range(KT):
                    e.wait_ge(x_sq, k + 1)
                    for n in range(NC):
                        mm = e.matmul(ms[:, n, 0:CW], self.ones[:, :], sq[:, k % 2, n * CW:(n + 1) * CW],
                                      start=(k == 0), stop=(k == KT - 1))
                    mm.then_inc(sq_used, 1)

            @block.vector
            def _(e):
                e.memset(epsc[:, :], EPS).then_inc(eps_set, 1)
                e.wait_ge(root, NC)
                e.reciprocal(rstd[:, :], rstd[:, :]).then_inc(inv, 1)
                e.wait_ge(inv, 1)
                e.wait_ge(g_in, 16)
                for k in range(KT):
                    e.scalar_tensor_tensor(out=hT[:, k, :], in0=hT[:, k, :], scalar=g[:, k:k + 1],
                                           in1=rstd[:, :], op0=ALU.mult, op1=ALU.mult).then_inc(normed, 1)
                e.wait_ge(normed, KT)

    def project_rwkv(self):
        nc, i, o = self.nc, self.i, self.o
        hT = self.hT
        with self.stage() as (c, block):
            w = self.sb(c, "w_main", [P, 2, KT, P])
            wl = self.sb(c, "w_lora", [P, KT, LW + LA + LG])
            bias = self.sb(c, "b_main", [P, NMAIN])
            mu = self.sb(c, "mu_main", [P, NMAIN])
            sh = self.sb(c, "shift_main", [P, NMAIN, NB])
            lb = self.sb(c, "lora_bias", [LG, 3])
            lmu = self.sb(c, "lora_mu", [LG, 3])
            lsh = self.sb(c, "lora_shift", [LG, 3, NB])
            praw = self.sb(c, "praw", [P, 2, 1 + T])
            dif = self.sb(c, "dif", [P, 2, T])
            prevs = self.sb(c, "prevs", [P, 2, NB, NS])
            last = self.sb(c, "last", [P, NMAIN + 3, 1 + NB])
            lrow = self.sb(c, "lrow", [1 + NB, 3 * RW + LW + LA + LG])
            pp = [self.ps(c, f"pp{s}", [P, NC, 512]) for s in range(2)]
            pt = self.ps(c, "pt", [1 + NB, 512])
            par_in, lora_in, zeroed, prod, evac, mixstep, laststep, lrow_t, lrow_c, out_s = self.sems(
                "par_in", "lora_in", "zeroed", "prod", "evac", "mixstep", "laststep", "lrow_t", "lrow_c",
                "out_s")
            w_in = self.sems("w_in0", "w_in1")
            LORAS = [(0, LW, self.lw), (LW, LA, self.la), (LW + LA, LG, self.lg)]
            MIX = 6
            LASTS = 2

            @block.sync
            def _(e):
                for a, b in ((bias, "b_main"), (mu, "mu_main"), (sh, "shift_main"), (lb, "lora_b"),
                             (lmu, "lora_mu"), (lsh, "lora_shift")):
                    e.dma_start(a[:], i[b]).then_inc(par_in, 16)
                e.dma_start(wl[:, :, :], i["w_lora"]).then_inc(lora_in, 16)
                with e.Fori(0, NMAIN // 2) as t:
                    for s in range(2):
                        e.wait_ge(prod, 2 * t + s)
                        e.dma_start(w[:, s, :, :], i["w_main"][ds(2 * t + s, 1)].rearrange("o p k f -> (o p) k f")
                                    ).then_inc(w_in[s], 16)
                e.wait_ge(lrow_c, 1)
                e.dma_start(o["shift"], lrow[:, :]).then_inc(out_s, 16)
                e.wait_ge(out_s, 16)

            @block.tensor
            def _(e):
                e.sem_inc(prod, 1)
                with e.Fori(0, NMAIN // 2) as t:
                    for s in range(2):
                        e.wait_ge(w_in[s], 16 * (t + 1))
                        e.wait_ge(evac, NC * (2 * t + s))
                        for k in range(KT):
                            for n in range(NC):
                                mm = e.matmul(pp[s][:, n, 0:CW], w[:, s, k, :], hT[:, k, n * CW:(n + 1) * CW],
                                              start=(k == 0), stop=(k == KT - 1))
                        mm.then_inc(prod, 1)
                e.wait_ge(lora_in, 16)
                for m, (off, width, _) in enumerate(LORAS):
                    s = m % 2
                    e.wait_ge(evac, NC * (NMAIN + m))
                    for k in range(KT):
                        for n in range(NC):
                            mm = e.matmul(pp[s][0:width, n, 0:CW], wl[:, k, off:off + width],
                                          hT[:, k, n * CW:(n + 1) * CW], start=(k == 0), stop=(k == KT - 1))
                    mm.then_inc(prod, 1)
                e.wait_ge(laststep, NMAIN + 3 + 1)
                for m in range(NMAIN + 3):
                    width = P if m < NMAIN else LORAS[m - NMAIN][1]
                    off = m * P if m < NMAIN else NMAIN * P + LORAS[m - NMAIN][0]
                    if m:
                        e.wait_ge(lrow_t, m)
                    e.transpose(pt[:, 0:width], last[0:width, m, :], self.ident[0:width, 0:width]
                                ).then_inc(mixstep, 1)

            def evacuate(e, s, rows, b):
                for n in range(NC):
                    e.activation(praw[0:rows, s, 1 + n * CW:1 + (n + 1) * CW], pp[s][0:rows, n, 0:CW],
                                 ACT.Identity, bias=b).then_inc(evac, 1)

            bcol = self.sb(c, "bcol", [P, 2, 1])
            bstep, = self.sems("bstep")

            @block.scalar
            def _(e):
                e.sem_inc(evac, NC)
                e.wait_ge(par_in, 96)
                with e.Fori(0, NMAIN // 2) as t:
                    for s in range(2):
                        e.copy(bcol[:, s, :], bias[:, ds(2 * t + s, 1)]).then_inc(bstep, 1)
                        e.wait_ge(bstep, 2 * t + s + 1)
                        e.wait_ge(prod, 2 * t + s + 2)
                        e.wait_ge(laststep, 2 * t + s)
                        evacuate(e, s, P, bcol[:, s, :])
                for m in range(3):
                    s = m % 2
                    e.wait_ge(prod, NMAIN + m + 2)
                    e.wait_ge(laststep, NMAIN + m)
                    evacuate(e, s, LORAS[m][1], lb[0:LORAS[m][1], m:m + 1])

            mstep, = self.sems("mstep")

            def mix(e, ch, s, rows, shift, muc, out, lastout):
                p = praw[0:rows, s, :]
                ch(e.tensor_copy(prevs[0:rows, s, :, 0], shift))
                ch(e.tensor_copy(prevs[0:rows, s, :, 1:NS],
                                 p[:, 1 + TP:1 + T].rearrange("p (b n) -> p b n", b=NB)[:, :, 0:NS - 1]))
                ch(e.tensor_tensor(dif[0:rows, s, 0:TP], p[:, 0:TP], p[:, 1:1 + TP], ALU.subtract))
                ch.settle()
                ch(e.tensor_tensor(dif[0:rows, s, TP:T], prevs[0:rows, s, :, :].rearrange("p b n -> p (b n)"),
                                   p[:, 1 + TP:1 + T], ALU.subtract))
                ch(e.tensor_copy(lastout[:, 1:1 + NB],
                                 p[:, 1 + TP:1 + T].rearrange("p (b n) -> p b n", b=NB)[:, :, NS - 1]))
                ch(e.tensor_copy(lastout[:, 0:1], p[:, TP:TP + 1]))
                ch.settle()
                ch(e.scalar_tensor_tensor(out=out, in0=dif[0:rows, s, :], scalar=muc, in1=p[:, 1:1 + T],
                                          op0=ALU.mult, op1=ALU.add))
                ch.settle()

            mucol = self.sb(c, "mucol", [P, 2, 1])

            @block.vector
            def _(e):
                e.memset(praw[:, :, 0:1], 0.0).then_inc(zeroed, 1)
                e.wait_ge(zeroed, 1)
                e.wait_ge(par_in, 96)
                e.sem_inc(laststep, 1)
                with e.Fori(0, NMAIN // 2) as t:
                    for s in range(2):
                        ch = Chain(e, mstep, (2 * t + s) * 8)
                        ch(e.tensor_copy(mucol[:, s, :], mu[:, ds(2 * t + s, 1)]))
                        e.wait_ge(evac, NC * (2 * t + s + 2))
                        mix(e, ch, s, P, sh[:, ds(2 * t + s, 1), :].rearrange("p o b -> p (o b)"), mucol[:, s, :],
                            self.mixed[:, ds(2 * t + s, 1), :].rearrange("p o t -> p (o t)"),
                            last[:, ds(2 * t + s, 1), :].rearrange("p o b -> p (o b)"))
                        assert ch.n == 8
                        e.sem_inc(laststep, 1)
                ch = Chain(e, mstep, NMAIN * 8)
                for m, (off, width, out) in enumerate(LORAS):
                    e.wait_ge(evac, NC * (NMAIN + m + 2))
                    mix(e, ch, m % 2, width, lsh[0:width, m, :], lmu[0:width, m:m + 1], out[:, :],
                        last[0:width, NMAIN + m, :])
                    e.sem_inc(laststep, 1)
                for m in range(NMAIN + 3):
                    width = P if m < NMAIN else LORAS[m - NMAIN][1]
                    off = m * P if m < NMAIN else NMAIN * P + LORAS[m - NMAIN][0]
                    e.wait_ge(mixstep, m + 1)
                    e.tensor_copy(lrow[:, off:off + width], pt[:, 0:width]).then_inc(lrow_t, 1)
                e.wait_ge(lrow_t, NMAIN + 3)
                e.sem_inc(lrow_c, 1)

    def project_qkv(self):
        nc, i = self.nc, self.i
        hT, qkv = self.hT, self.qkv
        with self.stage() as (c, block):
            w = self.sb(c, "w_qkv", [P, KT, QKV])
            bb = self.sb(c, "b_qkv", [P, QKV])
            pq = [self.ps(c, f"pq{s}", [P, 2, 512]) for s in range(2)]
            prod, evac = self.sems("qkv_prod", "qkv_evac")
            w_in = self.sems(*[f"wq_in{k}" for k in range(KT)])
            b_in, = self.sems("bq_in")

            @block.sync
            def _(e):
                for k in range(KT):
                    e.dma_start(w[:, k, :], i["w_in"][k * P:(k + 1) * P, 0:QKV]).then_inc(w_in[k], 16)
                e.dma_start(bb[:, :], i["b_qkv"].to_broadcast([P, QKV])).then_inc(b_in, 16)

            @block.tensor
            def _(e):
                for m in range(TT):
                    n = tokens_in(m)
                    if m >= 2:
                        e.wait_ge(evac, m)
                    for k in range(KT):
                        if m == 0:
                            e.wait_ge(w_in[k], 16)
                        lhsT = hT[:, k, m * P:m * P + n]
                        e.matmul(pq[m % 2][0:n, 0, :], lhsT, w[:, k, 0:QW], start=(k == 0), stop=(k == KT - 1))
                        mm = e.matmul(pq[m % 2][0:n, 1, 0:2 * KW], lhsT, w[:, k, QW:QKV],
                                      start=(k == 0), stop=(k == KT - 1))
                    mm.then_inc(prod, 1)

            @block.vector
            def _(e):
                e.memset(self.qkv_padded[:, 0, QW + KW:QKV], 0.0).then_inc(evac, 1)
                e.wait_ge(b_in, 16)
                for m in range(TT):
                    n = tokens_in(m)
                    e.wait_ge(prod, m + 1)
                    e.tensor_tensor(qkv[0:n, m, :], pq[m % 2][0:n, :, :].rearrange("p a b -> p (a b)")[:, 0:QKV],
                                    bb[0:n, :], ALU.add).then_inc(evac, 1)
                e.wait_ge(evac, TT + 1)


    def rope(self):
        nc, i = self.nc, self.i
        NH = NQ + NKV
        with self.stage() as (c, block):
            cs = self.sb(c, "rope_cos", [P, TT, RH])
            sn = self.sb(c, "rope_sin", [P, TT, RH])
            tmp = [self.sb(c, f"rope_t{n}", [P, TT, NH, RH]) for n in range(4)]
            tab_in, step, = self.sems("tab_in", "rope_step")

            @block.sync
            def _(e):
                e.dma_start(cs[:], i["cos"]).then_inc(tab_in, 16)
                e.dma_start(sn[:], i["sin"]).then_inc(tab_in, 16)

            @block.vector
            def _(e):
                e.wait_ge(tab_in, 32)
                ch = Chain(e, step)
                for rows, a, b in ((P, 0, TT - 1), (TS, TT - 1, TT)):
                    heads = self.qkv[0:rows, a:b, 0:NH * HD].rearrange("p m (h d) -> p m h d", h=NH)
                    x1, x2 = heads[:, :, :, 0:RH], heads[:, :, :, RH:ROT]
                    n = b - a
                    co = cs[0:rows, a:b, :].unsqueeze(2).to_broadcast([rows, n, NH, RH])
                    si = sn[0:rows, a:b, :].unsqueeze(2).to_broadcast([rows, n, NH, RH])
                    t = [z[0:rows, a:b] for z in tmp]
                    ch(e.tensor_tensor(t[0], x1, co, ALU.mult))
                    ch(e.tensor_tensor(t[1], x2, si, ALU.mult))
                    ch(e.tensor_tensor(t[2], x2, co, ALU.mult))
                    ch(e.tensor_tensor(t[3], x1, si, ALU.mult))
                    ch.settle()
                    ch(e.tensor_tensor(x1, t[0], t[1], ALU.subtract))
                    ch(e.tensor_tensor(x2, t[2], t[3], ALU.add))
                ch.settle()

    def attention(self):
        nc, i, o = self.nc, self.i, self.o
        qkv, attT, ident = self.qkv, self.attT, self.ident
        self.rope()
        G = NQ // NKV
        with self.stage() as (c, block):
            band = self.sb(c, "band", [P, 2 * WIN])
            band1 = self.sb(c, "band_first", [P, 2 * WIN])
            sink = self.sb(c, "sinks", [P, NQ])
            qT = self.sb(c, "qT", [P, QW // P, P])
            kT = self.sb(c, "kT", [P, 2, NKV, P])
            rows = self.sb(c, "qk_rows", [P, 2, QW + KW])
            sc = self.sb(c, "sc", [P, 2, G, 2 * WIN])
            pr = self.sb(c, "probs", [P, 2, G, 2 * WIN])
            pT = self.sb(c, "probsT", [P, 4, 4 * P])
            mx = self.sb(c, "mx", [P, 2, G])
            nmx = self.sb(c, "nmx", [P, 2, G])
            sx = self.sb(c, "sx", [P, 2, G])
            es = self.sb(c, "es", [P, 2, G])
            den = self.sb(c, "den", [P, 2, G])
            att = self.sb(c, "att", [P, QW])
            psq = self.ps(c, "psq", [P, 4, P])
            psk = self.ps(c, "psk", [P, 4, P])
            pss = self.ps(c, "pss", [P, G, 2 * WIN])
            pst = [self.ps(c, f"pst{n}", [P, 4 * P]) for n in range(2)]
            pso = self.ps(c, "pso", [P, 2, G, HD])
            (consts2, kv_out, kT_set, rows_c, qk_t, qk_c, s_done, s_taken, neg, expd, p_t, p_c, o_done, o_taken,
             a_t, a_c, vstep) = self.sems(
                "consts2", "kv_out", "kT_set", "rows_copied", "qk_t", "qk_c", "s_done", "s_taken", "neg", "expd",
                "p_t", "p_c", "o_done", "o_taken", "a_t", "a_c", "vstep")
            NP = 2 * G // 4
            VS = 8
            LAST = NBLK - 2

            def blocks(e, block_of):
                with e.Fori(0, LAST // 2) as t:
                    for s in range(2):
                        block_of(2 * t + s, s, False)
                for u in range(LAST, NBLK):
                    block_of(u, u % 2, u == NBLK - 1)

            @block.sync
            def _(e):
                e.dma_start(band[:], i["band"]).then_inc(consts2, 16)
                e.dma_start(band1[:], i["band_first"]).then_inc(consts2, 16)
                e.dma_start(sink[:], i["sinks"].to_broadcast([P, NQ])).then_inc(consts2, 16)
                e.dma_start(o["prompt_win_k"], qkv[:, TT - 2, QW:QW + KW]).then_inc(kv_out, 16)
                e.dma_start(o["prompt_win_v"], qkv[:, TT - 2, QW + KW:QKV]).then_inc(kv_out, 16)
                for name, cache, off in (("sample_win_k", "cache_k", QW), ("sample_win_v", "cache_v", QW + KW)):
                    e.dma_start(o[name][:, 0:WIN - NS, :], i[cache][:, NS:WIN, :]).then_inc(kv_out, 16)
                    for b in range(NB):
                        e.dma_start(o[name][b, WIN - NS:WIN, :], qkv[b * NS:(b + 1) * NS, TT - 1, off:off + KW]
                                    ).then_inc(kv_out, 16)
                e.wait_ge(kv_out, 16 * (4 + 2 * NB))

            @block.gpsimd
            def _(e):
                e.sem_inc(rows_c, 1)
                e.sem_inc(qk_t, 1)

                def rows_of(u, s, last):
                    e.wait_ge(qk_t, u)
                    e.tensor_copy(rows[:, s, :], qkv[:, ds(u, 1), 0:QW + KW].rearrange("p o f -> p (o f)")
                                  ).then_inc(rows_c, 1)

                rows_of(0, 0, False)
                with e.Fori(0, LAST // 2) as t:
                    rows_of(2 * t + 1, 1, False)
                    rows_of(2 * t + 2, 0, False)
                rows_of(NBLK - 1, 1, True)

            @block.tensor
            def _(e):
                def turn(u, s):
                    e.wait_ge(rows_c, u + 2)
                    for j in range(4):
                        e.transpose(psq[:, j, :], rows[:, s, j * P:(j + 1) * P], ident[:, :])
                    for g in range(NKV):
                        for d in range(2):
                            mm = e.matmul(psk[d * HD:(d + 1) * HD, g, :],
                                          rows[:, s, QW + g * HD:QW + (g + 1) * HD], ident[:, :],
                                          start=True, stop=True)
                    mm.then_inc(qk_t, 1)

                def block_of(u, s, last):
                    e.wait_ge(qk_c, 2 * (u + 1))
                    for g in range(NKV):
                        w = 2 * u + g
                        e.wait_ge(s_taken, w + 1)
                        for z in range(G):
                            h = 2 * (z % 2) + z // 2
                            q0 = (h % 2) * HD
                            lhsT = qT[q0:q0 + HD, (g * G + h) // 2, :]
                            e.matmul(pss[:, z, 0:WIN], lhsT, kT[q0:q0 + HD, 1 - s, g, :], start=True, stop=True)
                            mm = e.matmul(pss[:, z, WIN:2 * WIN], lhsT, kT[q0:q0 + HD, s, g, :],
                                          start=True, stop=True)
                        mm.then_inc(s_done, 1)
                    if not last:
                        e.wait_ge(a_c, u + 1)
                        turn(u + 1, 1 - s)
                    for g in range(NKV):
                        w = 2 * u + g
                        e.wait_ge(expd, (G + 1) * (w + 1))
                        e.wait_ge(o_taken, w + 1)
                        for n in range(NP):
                            e.wait_ge(p_c, NP * w + n + 1)
                            for q in range(4):
                                h, half = 2 * n + q // 2, q % 2
                                mm = e.transpose(pst[n % 2][:, q * P:(q + 1) * P],
                                                 pr[:, g, h, half * WIN:(half + 1) * WIN], ident[:, :])
                            mm.then_inc(p_t, 1)
                        e.wait_ge(p_c, NP * (w + 1) + 2)
                        for h in range(G):
                            n = h // 2
                            q = 2 * (h % 2)
                            v_at = slice(QW + KW + g * HD, QW + KW + (g + 1) * HD)
                            v_of = lambda block: self.qkv_padded[:, ds(block, 1), v_at].rearrange("p o f -> p (o f)")
                            e.matmul(pso[:, g, h, :], pT[:, 2 * g + n, q * P:(q + 1) * P], v_of(u),
                                     start=True, stop=False)
                            mm = e.matmul(pso[:, g, h, :], pT[:, 2 * g + n, (q + 1) * P:(q + 2) * P], v_of(u + 1),
                                          start=False, stop=True)
                        mm.then_inc(o_done, 1)
                    e.wait_ge(o_taken, 2 * (u + 1) + 1)
                    if not last:
                        e.wait_ge(qk_c, 2 * (u + 2))
                    for j in range(4):
                        mm = e.transpose(psq[:, j, :], att[:, j * P:(j + 1) * P], ident[:, :])
                    mm.then_inc(a_t, 1)

                e.sem_inc(a_c, 1)
                e.sem_inc(s_taken, 1)
                e.sem_inc(o_taken, 1)
                e.sem_inc(p_c, 2)
                e.wait_ge(kT_set, 1)
                turn(0, 0)
                blocks(e, block_of)

            @block.scalar
            def _(e):
                def turned(u, s):
                    e.wait_ge(qk_t, u + 2)
                    e.copy(qT[:], psq[:]).then_inc(qk_c, 1)
                    e.copy(kT[:, s, :, :], psk[:, 0:NKV, :]).then_inc(qk_c, 1)

                def block_of(u, s, last):
                    for g in range(NKV):
                        w = 2 * u + g
                        e.wait_ge(neg, w + 1)
                        for h in range(G):
                            e.activation(pr[:, g, h, :], sc[:, g, h, :], ACT.Exp, bias=nmx[:, g, h:h + 1],
                                         accum_out=den[:, g, h:h + 1]).then_inc(expd, 1)
                        e.activation(es[:, g, :], sx[:, g, :], ACT.Exp).then_inc(expd, 1)
                        if g == 0 and not last:
                            turned(u + 1, 1 - s)
                        for n in range(NP):
                            e.wait_ge(p_t, NP * w + n + 1)
                            e.copy(pT[:, 2 * g + n, :], pst[n % 2][:, :]).then_inc(p_c, 1)
                    e.wait_ge(a_t, u + 1)
                    e.copy(attT[:, :, ds(u * P, P)], psq[:]).then_inc(a_c, 1)

                e.wait_ge(kT_set, 1)
                turned(0, 0)
                blocks(e, block_of)
                e.wait_ge(a_c, NBLK + 1)

            @block.vector
            def _(e):
                def masked(u, s, g, mask):
                    w = 2 * u + g
                    ch = Chain(e, vstep, VS * u * 2 + g * (VS - 3))
                    e.wait_ge(s_done, w + 1)
                    ch(e.scalar_tensor_tensor(out=sc[:, g], in0=pss[:], scalar=SCALE,
                                              in1=mask[:].unsqueeze(1).to_broadcast([P, G, 2 * WIN]),
                                              op0=ALU.mult, op1=ALU.add))
                    ch.settle()
                    e.sem_inc(s_taken, 1)
                    ch(e.tensor_reduce(mx[:, g, :], sc[:, g], AX.X, ALU.max))
                    ch.settle()
                    ch(e.tensor_tensor(mx[:, g, :], mx[:, g, :], sink[:, g * G:(g + 1) * G], ALU.max))
                    ch.settle()
                    ch(e.tensor_scalar(nmx[:, g, :], mx[:, g, :], -1.0, None, ALU.mult))
                    ch(e.tensor_tensor(sx[:, g, :], sink[:, g * G:(g + 1) * G], mx[:, g, :], ALU.subtract))
                    ch.settle()
                    e.sem_inc(neg, 1)

                def weighted(u, s, g):
                    w = 2 * u + g
                    ch = Chain(e, vstep, VS * u * 2 + 2 * (VS - 3) + 3 * g)
                    e.wait_ge(expd, (G + 1) * (w + 1))
                    ch(e.tensor_tensor(den[:, g, :], den[:, g, :], es[:, g, :], ALU.add))
                    ch.settle()
                    ch(e.reciprocal(den[:, g, :], den[:, g, :]))
                    ch.settle()
                    e.wait_ge(o_done, w + 1)
                    e.wait_ge(a_c, u + 1)
                    ch(e.tensor_tensor(
                        att[:, g * G * HD:(g + 1) * G * HD].rearrange("p (b a d) -> p a b d", a=2, b=2),
                        pso[:, g, :, :].rearrange("p (a b) d -> p a b d", a=2),
                        den[:, g, :].rearrange("p (a b) -> p a b", a=2).unsqueeze(3).to_broadcast([P, 2, 2, HD]),
                        ALU.mult))
                    ch.settle()
                    e.sem_inc(o_taken, 1)

                def block_of(u, s, last, mask=band):
                    for g in range(NKV):
                        masked(u, s, g, mask)
                    for g in range(NKV):
                        weighted(u, s, g)

                e.memset(kT[:, 1, :, :], 0.0).then_inc(kT_set, 1)
                e.wait_ge(consts2, 48)
                block_of(0, 0, False, band1)
                block_of(1, 1, False)
                with e.Fori(1, LAST // 2) as t:
                    for s in range(2):
                        block_of(2 * t + s, s, False)
                for u in range(LAST, NBLK):
                    block_of(u, u % 2, u == NBLK - 1)
        self.attention_decode()

    def attention_decode(self):
        nc, i = self.nc, self.i
        qkv, attT, ident = self.qkv, self.attT, self.ident
        G = NQ // NKV
        NKC = NB * WIN
        with self.stage() as (c, block):
            ck = self.sb(c, "ck", [P, NB, KW])
            cv = self.sb(c, "cv", [P, NB, KW])
            mask = self.sb(c, "dmask", [P, T])
            sink = self.sb(c, "dsink", [P, NKV])
            kT = self.sb(c, "dkT", [P, T])
            qT = self.sb(c, "dqT", [P, NKV, P])
            sc = self.sb(c, "dsc", [P, T])
            pr = self.sb(c, "dpr", [P, T])
            pT = self.sb(c, "dpT", [P, TT, P])
            col = self.sb(c, "dcol", [P, 8])
            pss = self.ps(c, "dpss", [P, NC, 512])
            psa = self.ps(c, "dpsa", [P, 4, P])
            psb = self.ps(c, "dpsb", [P, 4, P])
            pso = self.ps(c, "dpso", [P, P])
            dk_in, kt, kc, qt, qc, sdone, vst, ex, ptt, ptc, od, oc = self.sems(
                "dk_in", "dkt", "dkc", "dqt", "dqc", "dsdone", "dvst", "dex", "dptt", "dptc", "dod", "doc")

            @block.sync
            def _(e):
                e.dma_start(ck[:], i["cache_k"].rearrange("b s f -> s b f")).then_inc(dk_in, 16)
                e.dma_start(cv[:], i["cache_v"].rearrange("b s f -> s b f")).then_inc(dk_in, 16)
                e.dma_start(mask[:], i["dmask"]).then_inc(dk_in, 16)
                e.dma_start(sink[:], i["dsink"]).then_inc(dk_in, 16)

            @block.tensor
            def _(e):
                e.wait_ge(dk_in, 64)
                for q in range(3):
                    ps = (psa, psb, psa)[q]
                    if q == 2:
                        e.wait_ge(kc, 1)
                        mm = e.transpose(ps[:, 0, 0:TS], qkv[0:TS, TT - 1, QW:QW + KW], ident[0:TS, 0:TS])
                    else:
                        for b in range(4):
                            mm = e.transpose(ps[:, b, :], ck[:, 4 * q + b, :], ident[:, :])
                    mm.then_inc(kt, 1)
                e.wait_ge(kc, 2)
                for g in range(NKV):
                    for h in range(G):
                        a = (g * G + h) * HD
                        mm = e.matmul(psb[g * HD:(g + 1) * HD, g, h * TS:(h + 1) * TS],
                                      qkv[0:TS, TT - 1, a:a + HD], ident[0:TS, 0:TS], start=True, stop=True)
                mm.then_inc(qt, 1)
                e.wait_ge(qc, 2)
                e.wait_ge(kc, 3)
                for g in range(NKV):
                    rows = slice(g * HD, (g + 1) * HD)
                    if g:
                        e.wait_ge(vst, 1)
                    for n in range(NC):
                        mm = e.matmul(pss[:, n, 0:CW], qT[rows, g, :], kT[rows, n * CW:(n + 1) * CW],
                                      start=True, stop=True)
                    mm.then_inc(sdone, 1)
                    e.wait_ge(vst, 7 * g + 7)
                    for q in range(3):
                        if q or g:
                            e.wait_ge(ptc, 3 * g + q)
                        ps = (psa, psb, psa)[q]
                        if q == 2:
                            mm = e.transpose(ps[0:TS, 0, :], pr[:, NKC:T], ident[:, :])
                        else:
                            for b in range(4):
                                mm = e.transpose(ps[:, b, :], pr[:, (4 * q + b) * P:(4 * q + b + 1) * P], ident[:, :])
                        mm.then_inc(ptt, 1)
                    e.wait_ge(ptc, 3 * g + 3)
                    if g:
                        e.wait_ge(oc, 4)
                    for b in range(NB):
                        e.matmul(pso[0:HD, :], cv[:, b, g * HD:(g + 1) * HD], pT[:, b, :], start=(b == 0), stop=False)
                    a = QW + KW + g * HD
                    e.matmul(pso[0:HD, :], qkv[0:TS, TT - 1, a:a + HD], pT[0:TS, NB, :], start=False, stop=True
                             ).then_inc(od, 1)

            @block.scalar
            def _(e):
                for q in range(3):
                    e.wait_ge(kt, q + 1)
                    ps = (psa, psb, psa)[q]
                    if q == 2:
                        e.copy(kT[:, NKC:T], ps[:, 0, 0:TS]).then_inc(kc, 1)
                    else:
                        e.copy(kT[:, q * 512:(q + 1) * 512], ps[:].rearrange("p a b -> p (a b)")).then_inc(kc, 1)
                e.wait_ge(qt, 1)
                for g in range(NKV):
                    rows = slice(g * HD, (g + 1) * HD)
                    e.copy(qT[rows, g, :], psb[rows, g, :]).then_inc(qc, 1)
                for g in range(NKV):
                    e.wait_ge(vst, 7 * g + 4)
                    e.activation(pr[:, :], sc[:, :], ACT.Exp, bias=col[:, 1:2], accum_out=col[:, 2:3]).then_inc(ex, 1)
                    e.activation(col[:, 3:4], sink[:, g:g + 1], ACT.Exp, bias=col[:, 1:2]).then_inc(ex, 1)
                    for q in range(3):
                        e.wait_ge(ptt, 3 * g + q + 1)
                        ps = (psa, psb, psa)[q]
                        if q == 2:
                            e.copy(pT[0:TS, NB, :], ps[0:TS, 0, :]).then_inc(ptc, 1)
                        else:
                            e.copy(pT[:, 4 * q:4 * q + 4, :], ps[:]).then_inc(ptc, 1)

            @block.vector
            def _(e):
                for g in range(NKV):
                    ch = Chain(e, vst, 7 * g)
                    e.wait_ge(sdone, g + 1)
                    e.wait_ge(ptt, 3 * g)
                    ch(e.scalar_tensor_tensor(out=sc[:].rearrange("p (n w) -> p n w", n=NC), in0=pss[:, :, 0:CW],
                                              scalar=SCALE, in1=mask[:].rearrange("p (n w) -> p n w", n=NC),
                                              op0=ALU.mult, op1=ALU.add))
                    ch.settle()
                    ch(e.tensor_reduce(col[:, 0:1], sc[:], AX.X, ALU.max))
                    ch.settle()
                    ch(e.tensor_tensor(col[:, 0:1], col[:, 0:1], sink[:, g:g + 1], ALU.max))
                    ch.settle()
                    ch(e.tensor_scalar(col[:, 1:2], col[:, 0:1], -1.0, None, ALU.mult))
                    e.wait_ge(ex, 2 * g + 2)
                    ch(e.tensor_tensor(col[:, 4:5], col[:, 2:3], col[:, 3:4], ALU.add))
                    ch.settle()
                    ch(e.reciprocal(col[:, 5:6], col[:, 4:5]))
                    ch.settle()
                    ch(e.tensor_scalar(pr[:, :], pr[:, :], col[:, 5:6], None, ALU.mult))
                    e.wait_ge(od, g + 1)
                    for h in range(G):
                        hh = g * G + h
                        e.tensor_copy(attT[(hh % 2) * HD:(hh % 2 + 1) * HD, hh // 2, TP:T],
                                      pso[0:HD, h * TS:(h + 1) * TS]).then_inc(oc, 1)
                e.wait_ge(oc, NQ)


    def rwkv(self):
        nc, i, o = self.nc, self.i, self.o
        with ExitStack() as c:
            self.dv = {n: self.sb(c, "dec_" + n, [P, NPAIR, TS]) for n in ("alpha", "beta", "kappa", "rho", "v")}
            self.dcum = self.sb(c, "dec_cum", [P, NPAIR, NB])
            self.lmask = self.sb(c, "level_masks", [P, LEVELS, P])
            self.low0 = self.sb(c, "low0", [P, P])
            self.before = self.sb(c, "before", [P, P])
            self.upto = self.sb(c, "upto", [P, 2, CH])
            with ExitStack() as c2:
                al, be, ka, rh, cu = (self.sb(c2, n, [P, T]) for n in ("alpha", "beta", "kappa", "rho", "cum"))
                self.al, self.be, self.ka, self.rh, self.cu = al, be, ka, rh, cu
                self.w2, self.a2 = self.sb(c2, "w2", [LW, P]), self.sb(c2, "a2", [LA, P])
                self.g2 = self.sb(c2, "g2", [LG, P])
                self.par = self.sb(c2, "pair_par", [P, 5])
                self.omka = self.sb(c2, "omka", [P, 1])
                self.work = self.sb(c2, "work", [P, WORK])
                self.banks = self.ps(c2, "banks", [P, 8, 512])
                self.lora_inputs()
                with nc.Fori(0, NPAIR) as j:
                    self.rwkv_elementwise(j)
                    self.rwkv_chunks(j)
            self.rwkv_decode()
        self.rwkv_out()

    def lora_inputs(self):
        nc, i = self.nc, self.i
        with self.stage() as (c, block):
            m_in, done = self.sems("m_in", "lora_done")

            @block.sync
            def _(e):
                e.dma_start(self.lmask[:], i["level_masks"]).then_inc(m_in, 16)
                e.dma_start(self.low0[:], i["low0"]).then_inc(m_in, 16)
                e.dma_start(self.before[:], i["before"]).then_inc(m_in, 16)
                e.dma_start(self.upto[:], i["upto"]).then_inc(m_in, 16)
                e.wait_ge(m_in, 64)

            @block.scalar
            def _(e):
                e.activation(self.lw[:], self.lw[:], ACT.Tanh).then_inc(done, 1)
                e.activation(self.lg[:], self.lg[:], ACT.Sigmoid).then_inc(done, 1)
                e.wait_ge(done, 2)

    def rwkv_elementwise(self, j):
        nc, i = self.nc, self.i
        al, be, ka, rh, cu = self.al, self.be, self.ka, self.rh, self.cu
        plane = lambda n: self.mixed[:, ds(j + n, 1), :].rearrange("p o t -> p (o t)")
        r, k, v = plane(0), plane(NPAIR), plane(2 * NPAIR)
        with self.stage() as (c, block):
            w2, a2, g2, par, omka = self.w2, self.a2, self.g2, self.par, self.omka
            carve = Carver(self.work)
            dec, a, kk, t0, t1 = (carve(T) for _ in range(5))
            pa, pb = self.banks[:, 0:NC, :], self.banks[:, NC:2 * NC, :]
            par_in, pz, az, va, pv, vz = self.sems("par_in2", "pz", "az", "va", "pv", "vz")
            split = lambda x: x.rearrange("p (n w) -> p n w", n=NC)
            used = lambda p: p[:, :, 0:CW]
            starts = lambda x: (x[:, 0:TP].rearrange("p (n w) -> p n w", w=CH)[:, :, 0],
                                x[:, TP:T].rearrange("p (n w) -> p n w", w=NS)[:, :, 0])

            @block.sync
            def _(e):
                for a_, b_ in ((w2, "w2"), (a2, "a2"), (g2, "g2"), (par, "pair_par")):
                    e.dma_start(a_[:], i[b_][ds(j, 1)].rearrange("o p f -> (o p) f")).then_inc(par_in, 16)

            @block.tensor
            def _(e):
                def product(ps, lhsT, rhs):
                    for n in range(NC):
                        mm = e.matmul(ps[:, n, 0:CW], lhsT, rhs[:, n * CW:(n + 1) * CW], start=True, stop=True)
                    mm.then_inc(pz, 1)
                e.wait_ge(par_in, 64)
                product(pa, w2[:], self.lw[:])
                product(pb, a2[:], self.la[:])
                e.wait_ge(az, 1)
                product(pa, g2[:], self.lg[:])
                e.wait_ge(az, 2)
                e.wait_ge(pv, 1)
                product(pb, self.headones[:], t0[:])
                e.wait_ge(az, 4)
                e.wait_ge(va, 14)
                product(pa, self.headones[:], t1[:])

            @block.scalar
            def _(e):
                e.wait_ge(pz, 1)
                e.activation(split(dec[:]), used(pa), ACT.Sigmoid, bias=par[:, 0:1]).then_inc(az, 1)
                e.wait_ge(pz, 2)
                e.activation(split(a[:]), used(pb), ACT.Sigmoid, bias=par[:, 1:2]).then_inc(az, 1)
                e.wait_ge(az, 1)
                e.activation(dec[:], dec[:], ACT.Exp, scale=-float(np.exp(-0.5))).then_inc(az, 1)
                e.wait_ge(pz, 3)
                e.wait_ge(va, 9)
                e.copy(split(k), used(pa)).then_inc(az, 1)
                e.wait_ge(va, 10)
                e.activation(t0[:], t0[:], ACT.Sqrt).then_inc(az, 1)

            @block.gpsimd
            def _(e):
                e.wait_ge(va, 2)
                e.tensor_tensor(t0[:], kk[:], kk[:], ALU.mult).then_inc(pv, 1)

            @block.vector
            def _(e):
                ch = Chain(e, va)
                e.wait_ge(par_in, 64)
                ch(e.tensor_scalar(omka[:], par[:, 3:4], -1.0, 1.0, ALU.mult, ALU.add))
                ch(e.tensor_scalar(kk[:], k, par[:, 2:3], None, ALU.mult))
                e.wait_ge(az, 3)
                ch(e.tensor_copy(al[:], dec[:]))
                ch(e.memset(be[:], 0.0))
                ch.settle()
                for n, (x, y) in enumerate(zip(starts(be[:]), starts(dec[:]))):
                    ch(e.tensor_copy(x, y))
                for x in starts(al[:]):
                    e.memset(x, 0.0).then_inc(vz, 1)
                e.wait_ge(vz, 2)
                ch.settle()
                ch(e.tensor_tensor_scan(cu[:], al[:], be[:], 0.0, ALU.mult, ALU.add))
                ch(e.tensor_scalar(t1[:], a[:], par[:, 3:4], omka[:, 0:1], ALU.mult, ALU.add))
                ch.settle()
                ch(e.tensor_tensor(ka[:], t1[:], k, ALU.mult))
                e.wait_ge(pz, 4)
                ch(e.tensor_scalar(split(t0[:]), used(pb), 1e-24, None, ALU.max))
                ch.settle()
                ch(e.scalar_tensor_tensor(out=t1[:], in0=ka[:], scalar=par[:, 4:5], in1=r, op0=ALU.mult,
                                          op1=ALU.mult))
                ch(e.tensor_tensor(rh[:], cu[:], r, ALU.mult))
                ch(e.reciprocal(be[:], cu[:]))
                ch.settle()
                ch(e.tensor_tensor(ka[:], ka[:], be[:], ALU.mult))
                e.wait_ge(az, 5)
                ch(e.reciprocal(t0[:], t0[:]))
                ch.settle()
                ch(e.tensor_tensor(kk[:], kk[:], t0[:], ALU.mult))
                ch(e.tensor_copy(dec[:, 1:T], cu[:, 0:T - 1]))
                ch.settle()
                for x in starts(dec[:]):
                    ch(e.memset(x, 1.0))
                ch(e.tensor_tensor(a[:], a[:], kk[:], ALU.mult))
                ch.settle()
                ch(e.tensor_tensor(al[:], dec[:], kk[:], ALU.mult))
                ch(e.tensor_tensor(be[:], be[:], a[:], ALU.mult))
                e.wait_ge(pz, 5)
                ch(e.tensor_tensor(split(r), used(pa), split(v), ALU.mult))
                ch.settle()
                for n, x in (("alpha", al), ("beta", be), ("kappa", ka), ("rho", rh)):
                    ch(e.tensor_copy(self.dv[n][:, ds(j, 1), :].rearrange("p o t -> p (o t)"), x[:, TP:T]))
                ch(e.tensor_copy(self.dv["v"][:, ds(j, 1), :].rearrange("p o t -> p (o t)"), v[:, TP:T]))
                ch(e.tensor_copy(self.dcum[:, ds(j, 1), :].rearrange("p o t -> p (o t)"),
                                 cu[:, TP:T].rearrange("p (b n) -> p b n", n=NS)[:, :, NS - 1]))
                ch.settle()

    def rwkv_chunks(self, j):
        nc, i, o = self.nc, self.i, self.o
        ident = self.ident
        v = self.mixed[:, ds(j + 2 * NPAIR, 1), :].rearrange("p o t -> p (o t)")
        L = LANES
        H2 = L // 2
        with self.stage() as (c, block):
            carve = Carver(self.work)
            big = lambda: carve(L, P)
            ab, bb, kb, vb = (big() for _ in range(4))
            cq = carve(2, L)
            araw = big()
            alv = carve(LEVELS - 1, L, P)
            XY = [big(), big()]
            Pm = [carve(H2, P), carve(H2, P)]
            bt = big()
            brk = [carve(L, 2, CH), carve(L, 2, CH)]
            at = big()
            bT, kT, vT, wv, apt = ([big(), big()] for _ in range(5))
            r1 = big()
            st, sc, nsa = carve(2, P), carve(2, P), carve(2, P)
            b = [self.banks[:, n, :].rearrange("p (l w) -> p l w", l=L) for n in range(8)]
            b_p = (b[0], b[3])
            b_xy = (b[1], b[2])
            b_y = self.banks[:, 7, 0:L * CH]
            b_u = self.banks[:, 7, L * CH:].rearrange("p (s w) -> p s w", s=2)
            names = ("built", "cq_set", "gram", "tposed", "araw_c", "t_c", "lvl", "g_v", "xy0", "r1_d", "r1_c", "wa_d",
                     "wa_c", "sa_d", "nsa_v", "u_d", "sc_c", "st_v", "y_c", "wkv_out")
            (built, cq_set, gram, tposed, araw_c, t_c, lvl, g_v, xy0, r1_d, r1_c, wa_d, wa_c, sa_d, nsa_v, u_d, sc_c,
             st_v, y_c, out_s) = self.sems(*names)
            p_d, p_c, xy_d, xy_v = (self.sems(n + "0", n + "1") for n in ("p_d", "p_c", "xy_d", "xy_v"))
            NL = LEVELS - 1
            MASKED = 4
            bc = lambda m: m.unsqueeze(1).to_broadcast([P, L, P])
            cols = lambda q, l=0, n=L: slice((q * L + l) * CH, (q * L + l + n) * CH)
            rho = lambda q, l: self.rh[:, cols(q, l, 1)]
            x_of = lambda l: XY[l // H2][:, l % H2, :]
            y_of = lambda l: XY[l // H2][:, H2 + l % H2, :]

            @block.gpsimd
            def _(e):
                def build(q):
                    if q:
                        e.wait_ge(tposed, 4 * q)
                    for src, dst in ((self.al[:], ab), (self.be[:], bb), (self.ka[:], kb), (v, vb)):
                        for h in range(2):
                            mine = self.headones[:, h * HD:(h + 1) * HD].unsqueeze(1).to_broadcast([P, L, CH])
                            e.tensor_tensor(dst[:, :, h * CH:(h + 1) * CH],
                                            src[:, cols(q)].rearrange("p (l w) -> p l w", l=L),
                                            mine, ALU.mult).then_inc(built, 1)
                    if q >= 2:
                        e.wait_ge(y_c, q - 1)
                    e.tensor_copy(cq[:, q % 2, :], self.cu[:, cols(q)].rearrange("p (l w) -> p l w", l=L)[:, :, CH - 1]
                                  ).then_inc(cq_set, 1)

                build(0)
                for q in range(NQUAD):
                    e.wait_ge(araw_c, q + 1)
                    for n in range(NL):
                        e.tensor_tensor(alv[:, n, :, :], araw[:], bc(self.lmask[:, n + 1, :]), ALU.mult
                                        ).then_inc(lvl, 1)
                    if q + 1 < NQUAD:
                        build(q + 1)

            @block.tensor
            def _(e):
                def step_sa(q, l):
                    if l == 0:
                        e.wait_ge(wa_c, 2 * (q + 1))
                    e.wait_ge(st_v, L * q + l + 1)
                    e.matmul(b[6][:, l, :], apt[q % 2][:, l, :], st[:, l % 2, :], start=True, stop=True
                             ).then_inc(sa_d, 1)

                def step_out(q, l):
                    s, z = l % 2, q % 2
                    if l == 0 and q:
                        e.wait_ge(y_c, q)
                    e.wait_ge(nsa_v, L * q + l + 1)
                    y = b_y[:, l * CH:(l + 1) * CH]
                    e.matmul(b_u[:, s, :], kT[z][:, l, :], vT[z][:, l, :], start=True, stop=False)
                    e.matmul(b_u[:, s, :], bT[z][:, l, :], nsa[:, s, :], start=False, stop=True)
                    e.matmul(y, st[:, s, :], rho(q, l), start=True, stop=False)
                    e.matmul(y, vT[z][:, l, :], brk[z][:, l, 1, :], start=False, stop=False)
                    e.matmul(y, nsa[:, s, :], brk[z][:, l, 0, :], start=False, stop=True).then_inc(u_d, 1)

                def prepare(q, steps):
                    e.wait_ge(built, 8 * (q + 1))
                    for l in range(L):
                        e.matmul(b[0][:, l, :], bb[:, l, :], ab[:, l, :], start=True, stop=True)
                    for l in range(L):
                        mm = e.matmul(b[1][:, l, :], ab[:, l, :], bb[:, l, :], start=True, stop=True)
                    mm.then_inc(gram, 1)
                    for l in range(L):
                        e.matmul(b[2][:, l, :], kb[:, l, :], ab[:, l, :], start=True, stop=True)
                    for l in range(L):
                        e.matmul(b[3][:, l, 0:CH], bb[:, l, :], rho(q, l), start=True, stop=True)
                        mm = e.matmul(b[3][:, l, CH:P], kb[:, l, :], rho(q, l), start=True, stop=True)
                    mm.then_inc(gram, 1)
                    if steps:
                        step_sa(q - 1, 0)
                    for n, m in enumerate((ab, bb, kb, vb)):
                        if n >= 2:
                            e.wait_ge(t_c, 4 * q + n - 1)
                        if n == 2 and steps:
                            step_out(q - 1, 0)
                        for l in range(L):
                            mm = e.transpose(b[4 + n % 2][:, l, :], m[:, l, :], ident[:])
                        mm.then_inc(tposed, 1)
                    for n in range(NL):
                        e.wait_ge(lvl, NL * q + n + 1)
                        if n == 0:
                            e.wait_ge(g_v, MASKED * (q + 1))
                        for h in range(2):
                            if n:
                                e.wait_ge(xy_v[h], NL * q + n)
                            for l in range(H2 * h, H2 * (h + 1)):
                                mm = e.matmul(b_p[h][:, l % H2, :], alv[:, n, l, :], x_of(l), start=True, stop=True)
                            mm.then_inc(p_d[h], 1)
                        if steps and n + 1 < L:
                            step_sa(q - 1, n + 1)
                        for h in range(2):
                            e.wait_ge(p_c[h], NL * q + n + 1)
                            for l in range(H2 * h, H2 * (h + 1)):
                                p_ = Pm[h][:, l % H2, :]
                                if n + 1 < NL:
                                    e.matmul(b_xy[h][:, l % H2, :], y_of(l), p_, start=True, stop=True)
                                mm = e.matmul(b_xy[h][:, H2 + l % H2, :], p_, y_of(l), start=True, stop=True)
                            mm.then_inc(xy_d[h], 1)
                        if steps and n + 1 < L:
                            step_out(q - 1, n + 1)
                    e.wait_ge(t_c, 4 * (q + 1))
                    for l in range(L):
                        mm = e.matmul(b[3][:, l, :], bt[:, l, :], vT[q % 2][:, l, :], start=True, stop=True)
                    mm.then_inc(r1_d, 1)
                    for h in range(2):
                        e.wait_ge(xy_v[h], NL * (q + 1))
                        for l in range(H2 * h, H2 * (h + 1)):
                            mm = e.matmul(b[5][:, l, :], at[:, l, :], y_of(l), start=True, stop=True)
                    mm.then_inc(wa_d, 1)
                    e.wait_ge(r1_c, q + 1)
                    for l in range(L):
                        mm = e.matmul(b[4][:, l, :], y_of(l), r1[:, l, :], start=True, stop=True)
                    mm.then_inc(wa_d, 1)

                for q in range(NQUAD):
                    prepare(q, steps=q > 0)
                for l in range(L):
                    step_sa(NQUAD - 1, l)
                    step_out(NQUAD - 1, l)

            @block.scalar
            def _(e):
                def step_decay(q, l):
                    if l == 0:
                        e.wait_ge(cq_set, q + 1)
                    e.wait_ge(st_v, L * q + l + 1)
                    e.mul(sc[:, l % 2, :], st[:, l % 2, :], cq[:, q % 2, l:l + 1]).then_inc(sc_c, 1)

                def outputs(q):
                    e.wait_ge(u_d, L * (q + 1))
                    e.wait_ge(st_v, L * (q + 1) + 1)
                    e.copy(v[:, cols(q)], b_y).then_inc(y_c, 1)

                def prepare(q, steps):
                    e.wait_ge(gram, 2 * q + 1)
                    e.copy(araw[:], b[0][:]).then_inc(araw_c, 1)
                    if steps:
                        step_decay(q - 1, 0)
                    for n, m in enumerate((at, bT[q % 2], kT[q % 2], vT[q % 2])):
                        e.wait_ge(tposed, 4 * q + n + 1)
                        e.copy(m[:], b[4 + n % 2][:]).then_inc(t_c, 1)
                    for n in range(NL):
                        for h in range(2):
                            e.wait_ge(p_d[h], NL * q + n + 1)
                            e.copy(Pm[h][:], b_p[h][:, 0:H2, :]).then_inc(p_c[h], 1)
                        if steps and n + 1 < L:
                            step_decay(q - 1, n + 1)
                        if steps and n + 1 == L:
                            outputs(q - 1)
                    e.wait_ge(r1_d, q + 1)
                    e.copy(r1[:], b[3][:]).then_inc(r1_c, 1)
                    e.wait_ge(wa_d, 2 * q + 1)
                    e.copy(apt[q % 2][:], b[5][:]).then_inc(wa_c, 1)
                    e.wait_ge(wa_d, 2 * q + 2)
                    e.copy(wv[q % 2][:], b[4][:]).then_inc(wa_c, 1)

                for q in range(NQUAD):
                    prepare(q, steps=q > 0)
                for l in range(L):
                    step_decay(NQUAD - 1, l)
                outputs(NQUAD - 1)

            @block.vector
            def _(e):
                def step_sa(q, l):
                    e.wait_ge(sa_d, L * q + l + 1)
                    e.scalar_tensor_tensor(out=nsa[:, l % 2, :], in0=b[6][:, l, :], scalar=-1.0,
                                           in1=wv[q % 2][:, l, :], op0=ALU.mult, op1=ALU.subtract).then_inc(nsa_v, 1)

                def step_state(q, l):
                    s = l % 2
                    e.wait_ge(u_d, L * q + l + 1)
                    e.wait_ge(sc_c, L * q + l + 1)
                    e.scalar_tensor_tensor(out=st[:, 1 - s, :], in0=b_u[:, s, :], scalar=cq[:, q % 2, l:l + 1],
                                           in1=sc[:, s, :], op0=ALU.mult, op1=ALU.add).then_inc(st_v, 1)

                def prepare(q, steps):
                    ch = Chain(e, g_v, MASKED * q)
                    e.wait_ge(gram, 2 * q + 1)
                    for h in range(2):
                        lanes = slice(H2 * h, H2 * (h + 1))
                        e.tensor_tensor(XY[h][:, 0:H2, :], b[1][:, lanes, :],
                                        self.low0[:].unsqueeze(1).to_broadcast([P, H2, P]), ALU.mult
                                        ).then_inc(xy0, 1)
                    e.wait_ge(araw_c, q + 1)
                    for h in range(2):
                        lanes = slice(H2 * h, H2 * (h + 1))
                        e.tensor_tensor(XY[h][:, H2:L, :], araw[:, lanes, :],
                                        self.lmask[:, 0, :].unsqueeze(1).to_broadcast([P, H2, P]), ALU.mult
                                        ).then_inc(xy0, 1)
                    e.wait_ge(xy0, 4 * (q + 1))
                    for h in range(2):
                        ch(e.tensor_tensor(XY[h][:], bc(ident[:]), XY[h][:], ALU.subtract))
                    if steps:
                        step_sa(q - 1, 0)
                    e.wait_ge(gram, 2 * q + 2)
                    ch(e.tensor_tensor(bt[:], b[2][:], bc(self.before[:]), ALU.mult))
                    ch(e.tensor_tensor(brk[q % 2][:], b[3][:].rearrange("p l (a w) -> p l a w", a=2),
                                       self.upto[:].unsqueeze(1).to_broadcast([P, L, 2, CH]), ALU.mult))
                    assert ch.n == MASKED
                    if steps:
                        step_state(q - 1, 0)
                    for n in range(NL):
                        if steps and n + 1 < L:
                            step_sa(q - 1, n + 1)
                        for h in range(2):
                            e.wait_ge(xy_d[h], NL * q + n + 1)
                            part = slice(0 if n + 1 < NL else H2, L)
                            e.tensor_tensor(XY[h][:, part, :], XY[h][:, part, :], b_xy[h][:, part, :], ALU.subtract
                                            ).then_inc(xy_v[h], 1)
                        if steps and n + 1 < L:
                            step_state(q - 1, n + 1)

                e.memset(st[:, 0, :], 0.0).then_inc(st_v, 1)
                for q in range(NQUAD):
                    prepare(q, steps=q > 0)
                for l in range(L):
                    step_sa(NQUAD - 1, l)
                    step_state(NQUAD - 1, l)
                e.wait_ge(st_v, TP // CH + 1)

            @block.sync
            def _(e):
                e.wait_ge(st_v, TP // CH + 1)
                for h in range(2):
                    rows = slice(h * HD, (h + 1) * HD)
                    e.dma_start(o["prompt_wkv"][ds(2 * j + h, 1)].rearrange("o a b -> (o a) b"), st[rows, 0, rows]
                                ).then_inc(out_s, 16)
                e.wait_ge(out_s, 32)

    def rwkv_decode(self):
        nc, i, o = self.nc, self.i, self.o
        ident, dv = self.ident, self.dv
        L, Q = NPAIR, 2 * TS
        with self.stage() as (c, block):
            sb = lambda n, *s: self.sb(c, "d_" + n, list(s))
            st0 = sb("state", P, L, NB, P)
            st1 = sb("state_new", P, L, NB, P)
            bd = [sb(f"bd{n}", P, L, 2, TS) for n in range(5)]
            tm = [sb(f"tm{n}", Q, L, P) for n in range(5)]
            mk = sb("masks", Q, 4, Q)
            mu = sb("upto", Q, 2, TS)
            own = sb("own", Q, NB)
            X, Y, Pm, a1, bt = (sb(n, Q, L, Q) for n in ("x", "y", "p", "a1", "bt"))
            yst = sb("yst", Q, L, TS)
            brk = sb("brk", Q, L, 2, TS)
            r1 = sb("r1", Q, L, P)
            apt = sb("apt", P, L, TS)
            vn = sb("vn", Q, 2, 2, NB, P)
            sums = sb("sums", P, 2, 4, P)
            b = [self.ps(c, f"db{n}", [P, 512]) for n in range(8)]
            d_in, bdp, gram, araw, g_v, p_d, p_c, y_d, y_v, r1_d, r1_c, ap_d, ap_c, sa_d, sa_c, bdn, nt_d, nt_c, y_f, \
                y_fc, vnp, u_d, u_v, u_c, out_s = self.sems(*[f"dec{n}" for n in range(25)])
            q4 = lambda m, rows, w: m[0:rows, 0:L * w].rearrange("p (l w) -> p l w", l=L)

            @block.sync
            def _(e):
                e.dma_start(mk[:], i["dec_masks"]).then_inc(d_in, 16)
                e.dma_start(mu[:], i["dec_upto"]).then_inc(d_in, 16)
                e.dma_start(own[:], i["dec_own"]).then_inc(d_in, 16)
                e.dma_start(st0[:], i["state0"]).then_inc(d_in, 16)
                e.wait_ge(u_c, 2 * L)
                for h in range(2):
                    rows = slice(h * HD, (h + 1) * HD)
                    for l in range(L):
                        e.dma_start(o["sample_wkv"][:, 2 * l + h].rearrange("b j i -> j b i"), st1[rows, l, :, rows]
                                    ).then_inc(out_s, 16)
                e.wait_ge(out_s, 32 * L)

            @block.gpsimd
            def _(e):
                for n, name in enumerate(("alpha", "beta", "kappa", "v")):
                    for h in range(2):
                        e.tensor_scalar(bd[n][:, :, h, :], dv[name][:], self.headones[:, h * HD:h * HD + 1], None,
                                        ALU.mult).then_inc(bdp, 1)
                e.wait_ge(nt_c, 1)
                e.wait_ge(d_in, 64)
                for l in range(L):
                    if l >= 2:
                        e.wait_ge(u_d, 2 * (l - 1))
                    for n, m in enumerate((tm[3], tm[4])):
                        e.tensor_tensor(vn[:, l % 2, n, :, :], m[:, l, :].unsqueeze(1).to_broadcast([Q, NB, P]),
                                        own[:].unsqueeze(2).to_broadcast([Q, NB, P]), ALU.mult).then_inc(vnp, 1)

            @block.tensor
            def _(e):
                e.wait_ge(bdp, 8)
                f = lambda m, l: m[:, l, :, :].rearrange("p a b -> p (a b)")
                for k, (x, y) in enumerate(((1, 0), (0, 1), (2, 0))):
                    for l in range(L):
                        mm = e.matmul(q4(b[k], Q, Q)[:, l, :], f(bd[x], l), f(bd[y], l), start=True, stop=True)
                    mm.then_inc(gram, 1)
                for l in range(L):
                    for n in range(2):
                        mm = e.matmul(q4(b[3], Q, Q)[:, l, n * TS:(n + 1) * TS], f(bd[1 + n], l), dv["rho"][:, l, :],
                                      start=True, stop=True)
                mm.then_inc(gram, 1)
                for n in range(4):
                    for l in range(L):
                        mm = e.transpose(q4(b[4 + n], Q, P)[:, l, :], f(bd[n], l), ident[:])
                    mm.then_inc(gram, 1)
                e.wait_ge(g_v, 7)
                for l in range(L):
                    mm = e.matmul(q4(b[0], Q, Q)[:, l, :], a1[:, l, :], X[:, l, :], start=True, stop=True)
                mm.then_inc(p_d, 1)
                e.wait_ge(p_c, 1)
                for l in range(L):
                    mm = e.matmul(q4(b[1], Q, Q)[:, l, :], Pm[:, l, :], Y[:, l, :], start=True, stop=True)
                mm.then_inc(y_d, 1)
                e.wait_ge(r1_c, 4)
                for l in range(L):
                    mm = e.matmul(q4(b[2], Q, P)[:, l, :], bt[:, l, :], tm[3][:, l, :], start=True, stop=True)
                mm.then_inc(r1_d, 1)
                e.wait_ge(y_v, 2)
                for l in range(L):
                    mm = e.matmul(q4(b[3], P, TS)[:, l, :], tm[0][:, l, :], yst[:, l, :], start=True, stop=True)
                mm.then_inc(ap_d, 1)
                e.wait_ge(ap_c, 1)
                e.wait_ge(r1_c, 5)
                e.wait_ge(d_in, 64)
                for l in range(L):
                    y = q4(b[4], P, TS)[:, l, :]
                    for k in range(NB):
                        e.matmul(y[:, k * NS:(k + 1) * NS], st0[:, l, k, :], apt[:, l, k * NS:(k + 1) * NS],
                                 start=(k == 0), stop=False)
                    mm = e.matmul(y, r1[:, l, :], yst[:, l, :], start=False, stop=True)
                mm.then_inc(sa_d, 1)
                e.wait_ge(bdn, 2)
                for l in range(L):
                    mm = e.transpose(q4(b[5], Q, P)[:, l, :], f(bd[4], l), ident[:])
                mm.then_inc(nt_d, 1)
                e.wait_ge(nt_c, 1)
                for l in range(L):
                    y = q4(b[6], P, TS)[:, l, :]
                    for k in range(NB):
                        e.matmul(y[:, k * NS:(k + 1) * NS], st0[:, l, k, :], dv["rho"][:, l, k * NS:(k + 1) * NS],
                                 start=(k == 0), stop=False)
                    e.matmul(y, tm[3][:, l, :], brk[:, l, 1, :], start=False, stop=False)
                    mm = e.matmul(y, tm[4][:, l, :], brk[:, l, 0, :], start=False, stop=True)
                mm.then_inc(y_f, 1)
                for l in range(L):
                    e.wait_ge(vnp, 2 * (l + 1))
                    for half in range(2):
                        n = 2 * l + half
                        if n >= 4:
                            e.wait_ge(u_v, n - 3)
                        for k in range(4):
                            u = q4(b[n % 4], P, P)[:, k, :]
                            e.matmul(u, tm[2][:, l, :], vn[:, l % 2, 0, 4 * half + k, :], start=True, stop=False)
                            mm = e.matmul(u, tm[1][:, l, :], vn[:, l % 2, 1, 4 * half + k, :], start=False, stop=True)
                        mm.then_inc(u_d, 1)

            @block.scalar
            def _(e):
                for n in range(4):
                    e.wait_ge(gram, 5 + n)
                    e.copy(tm[n][:], q4(b[4 + n], Q, P)).then_inc(r1_c, 1)
                e.wait_ge(p_d, 1)
                e.copy(Pm[:], q4(b[0], Q, Q)).then_inc(p_c, 1)
                e.wait_ge(r1_d, 1)
                e.copy(r1[:], q4(b[2], Q, P)).then_inc(r1_c, 1)
                e.wait_ge(ap_d, 1)
                e.copy(apt[:], q4(b[3], P, TS)).then_inc(ap_c, 1)
                e.wait_ge(nt_d, 1)
                e.copy(tm[4][:], q4(b[5], Q, P)).then_inc(nt_c, 1)
                e.wait_ge(y_f, 1)
                e.copy(self.mixed[:, 2 * NPAIR:3 * NPAIR, TP:T], q4(b[6], P, TS)).then_inc(y_fc, 1)
                for n in range(2 * L):
                    l, half = n // 2, n % 2
                    e.wait_ge(u_v, n + 1)
                    for k in range(4):
                        mm = e.mul(st1[:, l, 4 * half + k, :], sums[:, half, k, :],
                                   self.dcum[:, l, 4 * half + k:4 * half + k + 1])
                    mm.then_inc(u_c, 1)
                e.wait_ge(y_fc, 1)

            @block.vector
            def _(e):
                m = lambda k: mk[:, k, :].unsqueeze(1).to_broadcast([Q, L, Q])
                eye = ident[0:Q, 0:Q].unsqueeze(1).to_broadcast([Q, L, Q])
                e.wait_ge(d_in, 64)
                ch = Chain(e, g_v)
                e.wait_ge(gram, 1)
                ch(e.tensor_tensor(Y[:], q4(b[0], Q, Q), m(1), ALU.mult))
                ch(e.tensor_tensor(a1[:], q4(b[0], Q, Q), m(2), ALU.mult))
                e.wait_ge(gram, 2)
                ch(e.tensor_tensor(X[:], q4(b[1], Q, Q), m(3), ALU.mult))
                ch.settle()
                ch(e.tensor_tensor(Y[:], eye, Y[:], ALU.subtract))
                ch(e.tensor_tensor(X[:], eye, X[:], ALU.subtract))
                e.wait_ge(gram, 3)
                ch(e.tensor_tensor(bt[:], q4(b[2], Q, Q), m(0), ALU.mult))
                e.wait_ge(gram, 4)
                ch(e.tensor_tensor(brk[:], q4(b[3], Q, Q).rearrange("p l (a w) -> p l a w", a=2),
                                   mu[:].unsqueeze(1).to_broadcast([Q, L, 2, TS]), ALU.mult))
                e.wait_ge(y_d, 1)
                e.tensor_tensor(Y[:], Y[:], q4(b[1], Q, Q), ALU.subtract).then_inc(y_v, 1)
                e.wait_ge(y_v, 1)
                e.tensor_tensor(yst[:], Y[:, :, 0:TS], Y[:, :, TS:Q], ALU.add).then_inc(y_v, 1)
                e.wait_ge(sa_d, 1)
                e.tensor_scalar(bd[4][:, :, 0, :], q4(b[4], P, TS), self.headones[:, 0:1], -1.0, ALU.mult, ALU.mult
                                ).then_inc(bdn, 1)
                e.tensor_scalar(bd[4][:, :, 1, :], q4(b[4], P, TS), self.headones[:, HD:HD + 1], -1.0, ALU.mult,
                                ALU.mult).then_inc(bdn, 1)
                for n in range(2 * L):
                    l, half = n // 2, n % 2
                    e.wait_ge(u_d, n + 1)
                    if n >= 2:
                        e.wait_ge(u_c, n - 1)
                    e.tensor_tensor(sums[:, half, :, :], st0[:, l, 4 * half:4 * half + 4, :], q4(b[n % 4], P, P),
                                    ALU.add).then_inc(u_v, 1)

    def rwkv_out(self):
        nc, i = self.nc, self.i
        with self.stage() as (c, block):
            par = self.sb(c, "gn_par", [P, 2, NPAIR])
            epsc = self.sb(c, "gn_eps", [P, 1])
            yc = self.sb(c, "gn_yc", [P, 2, T])
            sq = self.sb(c, "gn_sq", [P, 2, T])
            rs = self.sb(c, "gn_rs", [P, 2, T])
            pm = self.ps(c, "gn_mean", [P, NC, 512])
            pv = self.ps(c, "gn_var", [P, NC, 512])
            par_in, eps_set, mean_d, cen, sqd, var_d, root, vst = self.sems(
                "gn_par_in", "gn_eps_set", "mean_d", "centred", "squared", "var_d", "gn_root", "gn_v")
            split = lambda x: x.rearrange("p (n w) -> p n w", n=NC)
            V = 5

            @block.sync
            def _(e):
                e.dma_start(par[:], i["gn_par"]).then_inc(par_in, 16)

            @block.tensor
            def _(e):
                for j in range(NPAIR):
                    y = self.mixed[:, 2 * NPAIR + j, :]
                    if j:
                        e.wait_ge(cen, j)
                    for n in range(NC):
                        mm = e.matmul(pm[:, n, 0:CW], self.headones[:], y[:, n * CW:(n + 1) * CW], start=True, stop=True)
                    mm.then_inc(mean_d, 1)
                    e.wait_ge(sqd, j + 1)
                    if j:
                        e.wait_ge(root, j)
                    for n in range(NC):
                        mm = e.matmul(pv[:, n, 0:CW], self.headones[:], sq[:, j % 2, n * CW:(n + 1) * CW],
                                      start=True, stop=True)
                    mm.then_inc(var_d, 1)

            @block.scalar
            def _(e):
                e.wait_ge(eps_set, 1)
                for j in range(NPAIR):
                    e.wait_ge(cen, j + 1)
                    e.activation(sq[:, j % 2, :], yc[:, j % 2, :], ACT.Square).then_inc(sqd, 1)
                    e.wait_ge(var_d, j + 1)
                    if j >= 2:
                        e.wait_ge(vst, V * (j - 1))
                    e.activation(split(rs[:, j % 2, :]), pv[:, :, 0:CW], ACT.Sqrt, bias=epsc[:], scale=1.0 / HD
                                 ).then_inc(root, 1)

            @block.vector
            def _(e):
                e.memset(epsc[:], GN_EPS).then_inc(eps_set, 1)
                e.wait_ge(par_in, 16)
                for j in range(NPAIR):
                    ch = Chain(e, vst, V * j)
                    y = self.mixed[:, 2 * NPAIR + j, :]
                    s = j % 2
                    e.wait_ge(mean_d, j + 1)
                    e.scalar_tensor_tensor(out=split(yc[:, s, :]), in0=pm[:, :, 0:CW], scalar=-1.0 / HD, in1=split(y),
                                           op0=ALU.mult, op1=ALU.add).then_inc(cen, 1)
                    e.wait_ge(root, j + 1)
                    ch(e.reciprocal(rs[:, s, :], rs[:, s, :]))
                    ch.settle()
                    ch(e.tensor_tensor(yc[:, s, :], yc[:, s, :], rs[:, s, :], ALU.mult))
                    ch.settle()
                    ch(e.tensor_scalar(yc[:, s, :], yc[:, s, :], par[:, 0, j:j + 1], par[:, 1, j:j + 1],
                                       ALU.mult, ALU.add))
                    ch.settle()
                    ch(e.tensor_tensor(yc[:, s, :], yc[:, s, :], self.mixed[:, j, :], ALU.add))
                    ch.settle()
                    ch(e.tensor_tensor(self.mixed[:, j, :], yc[:, s, :], self.mixed[:, NPAIR + j, :], ALU.mult))
                    ch.settle()
                    assert ch.n == V


    def merge(self):
        nc, i = self.nc, self.i
        rwT, outT = self.mixed[:, 0:NPAIR, :], self.mixed[:, NPAIR:NPAIR + KT, :]
        NW = 2 * KT + 2 * NPAIR
        with self.stage() as (c, block):
            w = self.sb(c, "w_merge", [P, 2, NW, P])
            gb = self.sb(c, "b_gate", [P, KT, 2])
            bcol = self.sb(c, "b_gate_now", [P, 2, 2])
            sg = self.sb(c, "sig", [P, 2, 2, CW])
            mm_ = self.sb(c, "gated", [P, 2, 2, CW])
            ps = self.ps(c, "ps_merge", [P, 2, 4, 512])
            b_in, prod, bcp, sgd, gated, summed = self.sems("bg_in", "mprod", "bcp", "sgd", "gated", "summed")
            w_in = self.sems("wm_in0", "wm_in1")

            @block.sync
            def _(e):
                e.dma_start(gb[:], i["b_gate"]).then_inc(b_in, 16)
                with e.Fori(0, KT // 2) as t:
                    for s in range(2):
                        e.wait_ge(prod, NC * (2 * t + s))
                        e.dma_start(w[:, s, :, :], i["w_merge"][ds(2 * t + s, 1)].rearrange("o p k f -> (o p) k f")
                                    ).then_inc(w_in[s], 16)

            @block.tensor
            def _(e):
                e.sem_inc(prod, NC)
                with e.Fori(0, KT // 2) as t:
                    for s in range(2):
                        e.wait_ge(w_in[s], 16 * (t + 1))
                        for n in range(NC):
                            u = (2 * t + s) * NC + n
                            z = (s * NC + n) % 2
                            e.wait_ge(gated, 2 * u)
                            cols = slice(n * CW, (n + 1) * CW)
                            k0 = 0
                            for m, (rhs, K) in enumerate(((self.hT, KT), (self.hT, KT), (self.attT, NPAIR),
                                                          (rwT, NPAIR))):
                                for k in range(K):
                                    mm = e.matmul(ps[:, z, m, 0:CW], w[:, s, k0 + k, :], rhs[:, k, cols],
                                                  start=(k == 0), stop=(k == K - 1))
                                k0 += K
                            mm.then_inc(prod, 1)

            @block.scalar
            def _(e):
                e.wait_ge(b_in, 16)
                with e.Fori(0, KT // 2) as t:
                    for s in range(2):
                        e.copy(bcol[:, s, :], gb[:, ds(2 * t + s, 1), :].rearrange("p o f -> p (o f)")
                               ).then_inc(bcp, 1)
                        e.wait_ge(bcp, 2 * t + s + 1)
                        for n in range(NC):
                            u = (2 * t + s) * NC + n
                            z = (s * NC + n) % 2
                            e.wait_ge(prod, NC + u + 1)
                            e.wait_ge(gated, 2 * u)
                            for m in range(2):
                                e.activation(sg[:, z, m, :], ps[:, z, m, 0:CW], ACT.Sigmoid,
                                             bias=bcol[:, s, m:m + 1]).then_inc(sgd, 1)

            @block.vector
            def _(e):
                e.sem_inc(gated, 2)
                with e.Fori(0, KT // 2) as t:
                    for s in range(2):
                        for n in range(NC):
                            u = (2 * t + s) * NC + n
                            z = (s * NC + n) % 2
                            e.wait_ge(sgd, 2 * (u + 1))
                            e.wait_ge(summed, u)
                            for m in range(2):
                                e.tensor_tensor(mm_[:, z, m, :], sg[:, z, m, :], ps[:, z, 2 + m, 0:CW], ALU.mult
                                                ).then_inc(gated, 1)

            @block.gpsimd
            def _(e):
                e.sem_inc(summed, 1)
                with e.Fori(0, KT // 2) as t:
                    for s in range(2):
                        for n in range(NC):
                            u = (2 * t + s) * NC + n
                            z = (s * NC + n) % 2
                            e.wait_ge(gated, 2 * (u + 2))
                            e.tensor_tensor(outT[:, ds(2 * t + s, 1), n * CW:(n + 1) * CW].rearrange("p o f -> p (o f)"),
                                            mm_[:, z, 0, :], mm_[:, z, 1, :], ALU.add).then_inc(summed, 1)

    def output_projection(self):
        nc, i = self.nc, self.i
        merged = self.mixed[:, NPAIR:NPAIR + KT, :]
        with self.stage() as (c, block):
            w = self.sb(c, "w_o", [P, KT, D])
            g = self.sb(c, "g2row", [P, D])
            epsc = self.sb(c, "eps2", [P, 1])
            x = self.sb(c, "x_rows", [P, 2, D])
            h = self.sb(c, "h_rows", [P, 2, D])
            sq = self.sb(c, "sq2", [P, D])
            col = self.sb(c, "col2", [P, 2, 2])
            ps = self.ps(c, "ps_o", [P, 2, 2, 512])
            pt = self.ps(c, "ps_t", [P, 2, 4, P])
            g_in, eps_set, prod, x1d, ssd, rootd, vst, hd, tp, tc = self.sems(
                "g2_in", "eps2_set", "oprod", "x1_done", "ssd", "root2", "v2", "h2_done", "h2_t", "h2_c")
            w_in = self.sems(*[f"wo_in{k}" for k in range(KT)])
            x_in = self.sems("xr_in0", "xr_in1")
            x1_out = self.sems("x1_out0", "x1_out1")
            h2_out = self.sems("h2_out0", "h2_out1")

            @block.sync
            def _(e):
                for k in range(KT):
                    e.dma_start(w[:, k, :], i["w_o"][k * P:(k + 1) * P, :]).then_inc(w_in[k], 16)
                e.dma_start(g[:], i["norm2_g"].to_broadcast([P, D])).then_inc(g_in, 16)
                for m in range(TT):
                    n, s = tokens_in(m), m % 2
                    if m >= 2:
                        e.wait_ge(x1_out[s], 16 * (m // 2))
                        e.wait_ge(hd, m - 1)
                        e.wait_ge(ssd, m - 1)
                    e.dma_start(x[0:n, s, :], i["x"][m * P:m * P + n, :]).then_inc(x_in[s], 16)

            @block.tensor
            def _(e):
                def product(m):
                    n, s = tokens_in(m), m % 2
                    if m >= 2:
                        e.wait_ge(x1d, m - 1)
                    for k in range(KT):
                        if m == 0:
                            e.wait_ge(w_in[k], 16)
                        for d in range(2):
                            mm = e.matmul(ps[0:n, s, d, :], merged[:, k, m * P:m * P + n],
                                          w[:, k, d * 512:(d + 1) * 512], start=(k == 0), stop=(k == KT - 1))
                    mm.then_inc(prod, 1)

                def turn(m):
                    n, s = tokens_in(m), m % 2
                    e.wait_ge(hd, m + 1)
                    for d in range(2):
                        if m:
                            e.wait_ge(tc, 2 * (m - 1) + d + 1)
                        for k in range(4):
                            mm = e.transpose(pt[:, d, k, 0:n], h[0:n, s, (4 * d + k) * P:(4 * d + k + 1) * P],
                                             self.ident[0:n, 0:n])
                        mm.then_inc(tp, 1)

                product(0)
                for m in range(TT):
                    if m + 1 < TT:
                        product(m + 1)
                    turn(m)

            @block.scalar
            def _(e):
                e.wait_ge(eps_set, 1)
                for m in range(TT):
                    n, s = tokens_in(m), m % 2
                    e.wait_ge(x1d, m + 1)
                    if m:
                        e.wait_ge(ssd, m)
                    e.activation(sq[0:n, :], x[0:n, s, :], ACT.Square, accum_out=col[0:n, s, 0:1]).then_inc(ssd, 1)
                    e.wait_ge(ssd, m + 1)
                    e.activation(col[0:n, s, 1:2], col[0:n, s, 0:1], ACT.Sqrt, bias=epsc[0:n, :], scale=1.0 / D
                                 ).then_inc(rootd, 1)
                    e.dma_start(self.x1_d[m * P:m * P + n, :], x[0:n, s, :]).then_inc(x1_out[s], 16)
                    for d in range(2):
                        e.wait_ge(tp, 2 * m + d + 1)
                        e.copy(self.hT[:, 4 * d:4 * d + 4, m * P:m * P + n], pt[:, d, :, 0:n]).then_inc(tc, 1)
                    e.dma_start(self.h2_d[m * P:m * P + n, :], h[0:n, s, :]).then_inc(h2_out[s], 16)
                e.wait_ge(tc, 2 * TT)
                for q in (x1_out, h2_out):
                    e.wait_ge(q[0], 16 * ((TT + 1) // 2))
                    e.wait_ge(q[1], 16 * (TT // 2))

            @block.vector
            def _(e):
                e.memset(epsc[:], EPS).then_inc(eps_set, 1)
                e.wait_ge(g_in, 16)
                for m in range(TT):
                    n, s = tokens_in(m), m % 2
                    e.wait_ge(prod, m + 1)
                    e.wait_ge(x_in[s], 16 * (m // 2 + 1))
                    e.tensor_tensor(x[0:n, s, :], ps[0:n, s, :, :].rearrange("p a b -> p (a b)"), x[0:n, s, :], ALU.add
                                    ).then_inc(x1d, 1)
                    e.wait_ge(rootd, m + 1)
                    e.reciprocal(col[0:n, s, 1:2], col[0:n, s, 1:2]).then_inc(vst, 1)
                    e.wait_ge(vst, m + 1)
                    if m >= 2:
                        e.wait_ge(h2_out[s], 16 * (m // 2))
                        e.wait_ge(tp, 2 * (m - 1))
                    e.scalar_tensor_tensor(out=h[0:n, s, :], in0=x[0:n, s, :], scalar=col[0:n, s, 1:2],
                                           in1=g[0:n, :], op0=ALU.mult, op1=ALU.mult).then_inc(hd, 1)

    def scores(self):
        nc, i = self.nc, self.i
        with self.stage() as (c, block):
            w = self.sb(c, "w_query", [P, 2, KT, P])
            sk = self.sb(c, "sub_keys", [P, 2, NKEY])
            q = self.sb(c, "query", [P, 2, T])
            so = self.sb(c, "scores", [P, 2, TT, NKEY])
            pq = self.ps(c, "ps_query", [P, NC, 512])
            pscore = self.ps(c, "ps_score", [P, NC, 512])
            q_d, q_c, s_d, s_c = self.sems("q_done", "q_copied", "s_done2", "s_copied")
            w_in, sk_in, s_out = (self.sems(n + "0", n + "1") for n in ("wq2_in", "sk_in", "s_out"))

            @block.sync
            def _(e):
                with e.Fori(0, PH) as h:
                    for z in range(2):
                        u = 2 * h + z
                        e.wait_ge(s_d, u)
                        e.dma_start(w[:, z, :, :], i["w_query"][ds(u, 1)].rearrange("o p k f -> (o p) k f")
                                    ).then_inc(w_in[z], 16)
                        e.dma_start(sk[:, z, :], i["sub_keys"][ds(u, 1)].rearrange("o p f -> (o p) f")
                                    ).then_inc(sk_in[z], 16)

            @block.tensor
            def _(e):
                e.sem_inc(s_d, 1)
                with e.Fori(0, PH) as h:
                    for z in range(2):
                        u = 2 * h + z
                        e.wait_ge(w_in[z], 16 * (h + 1))
                        e.wait_ge(q_c, u)
                        for k in range(KT):
                            for n in range(NC):
                                mm = e.matmul(pq[:, n, 0:CW], w[:, z, k, :], self.hT[:, k, n * CW:(n + 1) * CW],
                                              start=(k == 0), stop=(k == KT - 1))
                        mm.then_inc(q_d, 1)
                        e.wait_ge(q_c, u + 1)
                        e.wait_ge(sk_in[z], 16 * (h + 1))
                        e.wait_ge(s_c, 2 * u)
                        for m in range(TT):
                            n = tokens_in(m)
                            mm = e.matmul(pscore[0:n, m // 4, (m % 4) * P:(m % 4 + 1) * P], q[:, z, m * P:m * P + n],
                                          sk[:, z, :], start=True, stop=True)
                        mm.then_inc(s_d, 1)

            @block.scalar
            def _(e):
                with e.Fori(0, PH) as h:
                    for z in range(2):
                        u = 2 * h + z
                        e.wait_ge(q_d, u + 1)
                        e.wait_ge(s_d, u)
                        e.copy(q[:, z, :].rearrange("p (n w) -> p n w", n=NC), pq[:, :, 0:CW]).then_inc(q_c, 1)

            @block.vector
            def _(e):
                with e.Fori(0, PH) as h:
                    for z in range(2):
                        u = 2 * h + z
                        e.wait_ge(s_d, u + 2)
                        e.wait_ge(s_out[z], 32 * h)
                        e.tensor_copy(so[:, z, 0:8, :].rearrange("p (a b) k -> p a (b k)", a=2), pscore[:, 0:2, :]
                                      ).then_inc(s_c, 1)
                        e.tensor_copy(so[0:TS, z, 8, :], pscore[0:TS, 2, 0:P]).then_inc(s_c, 1)

            @block.gpsimd
            def _(e):
                with e.Fori(0, PH) as h:
                    for z in range(2):
                        u = 2 * h + z
                        e.wait_ge(s_c, 2 * (u + 1))
                        cols = slice(z * NKEY, (z + 1) * NKEY)
                        e.dma_start(self.s_d[0:TP * PH // P, :, cols].rearrange("(m h) p k -> h p m k", h=PH)[ds(h, 1)]
                                    .rearrange("o p m k -> (o p) m k"), so[:, z, 0:TT - 1, :]).then_inc(s_out[z], 16)
                        e.dma_start(self.s_d[TP * PH // P:, :, cols].rearrange("u (q p) k -> (u q) p k", p=TS)[ds(h, 1)]
                                    .rearrange("o p k -> (o p) k"), so[0:TS, z, TT - 1, :]).then_inc(s_out[z], 16)
                for z in range(2):
                    e.wait_ge(s_out[z], 32 * PH)

    def experts(self):
        nc, i, o = self.nc, self.i, self.o
        RING, G = TOPK, 4
        NG = TOPK // G
        PT = TP // P
        HU = P // TS
        DU = PH // HU
        NU = PT * PH + DU
        with self.stage() as (c, block):
            ring = self.sb(c, "ring", [P, RING, 2 * D])
            hrow = self.sb(c, "h2_tile", [P, D])
            hnext = self.sb(c, "h2_next", [P, D])
            xrow = self.sb(c, "x1_tile", [P, D])
            grow = self.sb(c, "gf_row", [P, D])
            epsc = self.sb(c, "eps3", [P, 1])
            fold = self.sb(c, "fold", [P, TS])
            sc = self.sb(c, "s_unit", [P, 2, 2, NKEY])
            sm = self.sb(c, "s_left", [P, 2, NKEY])
            sv = self.sb(c, "top_s", [P, 2, TOPK])
            si = self.sb(c, "top_i", [P, 2, TOPK], U32)
            sif = self.sb(c, "top_if", [P, 2, TOPK])
            cand = self.sb(c, "cand", [P, TOPK * TOPK])
            cleft = self.sb(c, "cand_left", [P, TOPK * TOPK])
            bs = self.sb(c, "best_s", [P, TOPK])
            bp = self.sb(c, "best_pos", [P, TOPK], U32)
            ranks = self.sb(c, "ranks", [P, 2, TOPK], U32)
            ranksf = self.sb(c, "ranks_f", [P, 2, TOPK])
            iota = self.sb(c, "iota", [P, TOPK])
            hot = self.sb(c, "hot", [P, 2, TOPK, TOPK])
            pick = self.sb(c, "pick", [P, 2, TOPK])
            idx = self.sb(c, "expert_id", [P, 2, TOPK], U32)
            nmax = self.sb(c, "neg_max", [P, 1])
            ex = self.sb(c, "exp_s", [P, 2, TOPK])
            den = self.sb(c, "gate_den", [P, 2, 1])
            gate = self.sb(c, "gate", [P, 2, TOPK])
            dot = self.sb(c, "dots", [P, 2, TOPK])
            act = self.sb(c, "acts", [P, 2, TOPK])
            wt = self.sb(c, "weights", [P, 2, TOPK])
            diag = self.sb(c, "diag", [P, 2 * G, P])
            zero = self.sb(c, "zero", [P, P])
            x2 = self.sb(c, "x2", [P, D])
            sq = self.sb(c, "sq3", [P, D])
            col = self.sb(c, "col3", [P, 2])
            yrow = self.sb(c, "y_tile", [P, D])
            acc = self.ps(c, "acc", [P, 2, 512])
            (passed, c_in, const_set, found, idx_d, exp_d, gate_d, dots, gelu, wtd, diagd, pv, accd, x2d, ssd, rootd,
             norm_d, yd, y_out) = self.sems(
                "passed", "c3_in", "const3_set", "topk", "idx_done", "exp_done", "gate_done", "dots_done", "gelu_done",
                "wt_done", "diag_done", "v_used", "acc_done", "x2_done", "ss3", "root3", "norm3", "y_done", "y_out")
            s_in = self.sems("su_in0", "su_in1")
            h_in, x_in, h_c = self.sems("hr_in", "x1r_in", "h2_copied")
            uv_in = self.sems(*[f"uv_in{n}" for n in range(RING)])
            FOUND = 26

            @block.sync
            def _(e):
                e.dma_start(grow[:], i["final_g"].to_broadcast([P, D])).then_inc(c_in, 16)
                e.dma_start(iota[:], i["iota"].to_broadcast([P, TOPK])).then_inc(c_in, 16)
                e.dma_start(fold[:], i["fold"]).then_inc(c_in, 16)

                def unit_scores(u, z):
                    e.dma_start(sc[:, z, :, :], self.s_d[ds(u, 1)].rearrange("o p (z k) -> (o p) z k", z=2)
                                ).then_inc(s_in[z], 16)

                def tile_rows(m, first):
                    decode = isinstance(m, int) and m == PT
                    for n in range(HU):
                        row = first + (0 if decode else n * TS)
                        e.dma_start(hnext[n * TS:(n + 1) * TS, :], self.h2_d[ds(row, TS), :]).then_inc(h_in, 16)
                    n = TS if decode else P
                    return lambda: e.dma_start(xrow[0:n, :], self.x1_d[ds(first, n), :]).then_inc(x_in, 16)

                def tile(m, units, next_first):
                    e.wait_ge(h_c, m + 1)
                    x_rows = tile_rows(m + 1, next_first)
                    e.wait_ge(pv, TOPK * (PH * m + 1) + 1)
                    x_rows()
                    with e.Fori(0, units // 2) as hh:
                        for z in range(2):
                            u = m * PH + 2 * hh + z
                            e.wait_ge(idx_d, u)
                            unit_scores(u + 1, 1 - z)

                unit_scores(0, 0)
                tile_rows(0, 0)()
                with e.Fori(0, PT - 1) as m:
                    tile(m, PH, (m + 1) * P)
                tile(PT - 1, PH, TP)
                for u in range(PT * PH, NU - 1):
                    e.wait_ge(idx_d, u)
                    unit_scores(u + 1, (u + 1) % 2)

            @block.gpsimd
            def _(e):
                with e.Fori(0, NU // 2) as t:
                    for z in range(2):
                        u = 2 * t + z
                        e.wait_ge(idx_d, u + 1)
                        for k in range(TOPK):
                            e.wait_ge(pv, TOPK * u + k + 1)
                            e.sem_inc(passed, 1)
                            e.indirect_dma_start(out=ring[:, k, :], out_offset=None, in_=i["uv"],
                                                 in_offset=bass.IndirectOffsetOnAxis(ap=idx[:, z, k:k + 1], axis=0)
                                                 ).then_inc(uv_in[k], 16)

            @block.vector
            def _(e):
                e.memset(epsc[:], EPS).then_inc(const_set, 1)
                e.memset(zero[:], 0.0).then_inc(const_set, 1)

                def find(u, z, loaded):
                    ch = Chain(e, found, FOUND * u)
                    e.wait_ge(s_in[z], 16 * loaded)
                    e.sem_inc(passed, 1)
                    for half in range(2):
                        ch(e.max(out=sv[:, half, 0:8], in_=sc[:, z, half, :]))
                    ch.settle()
                    e.sem_inc(passed, 1)
                    for half in range(2):
                        ch(e.max_index(out=si[:, half, 0:8], in_max=sv[:, half, 0:8], in_values=sc[:, z, half, :]))
                        ch(e.match_replace(out=sm[:, half, :], in_to_replace=sv[:, half, 0:8],
                                           in_values=sc[:, z, half, :], imm_value=-3.0e38))
                    ch.settle()
                    e.sem_inc(passed, 1)
                    for half in range(2):
                        ch(e.max(out=sv[:, half, 8:16], in_=sm[:, half, :]))
                    ch.settle()
                    e.sem_inc(passed, 1)
                    for half in range(2):
                        ch(e.max_index(out=si[:, half, 8:16], in_max=sv[:, half, 8:16], in_values=sm[:, half, :]))
                    ch(e.tensor_tensor(cand[:].rearrange("p (a b) -> p a b", a=TOPK),
                                       sv[:, 0, :].unsqueeze(2).to_broadcast([P, TOPK, TOPK]),
                                       sv[:, 1, :].unsqueeze(1).to_broadcast([P, TOPK, TOPK]), ALU.add))
                    ch.settle()
                    ch(e.tensor_copy(sif[:], si[:]))
                    ch(e.max(out=bs[:, 0:8], in_=cand[:]))
                    ch.settle()
                    ch(e.tensor_scalar(nmax[:], bs[:, 0:1], -1.0, None, ALU.mult))
                    ch(e.max_index(out=bp[:, 0:8], in_max=bs[:, 0:8], in_values=cand[:]))
                    ch(e.match_replace(out=cleft[:], in_to_replace=bs[:, 0:8], in_values=cand[:], imm_value=-3.0e38))
                    ch.settle()
                    e.sem_inc(passed, 1)
                    ch(e.max(out=bs[:, 8:16], in_=cleft[:]))
                    ch.settle()
                    e.sem_inc(passed, 1)
                    ch(e.max_index(out=bp[:, 8:16], in_max=bs[:, 8:16], in_values=cleft[:]))
                    ch.settle()
                    ch(e.tensor_scalar(ranks[:, 0, :], bp[:], 4, None, ALU.logical_shift_right))
                    ch(e.tensor_scalar(ranks[:, 1, :], bp[:], 15, None, ALU.bitwise_and))
                    ch.settle()
                    ch(e.tensor_copy(ranksf[:], ranks[:]))
                    ch.settle()
                    for half in range(2):
                        ch(e.tensor_tensor(hot[:, half], ranksf[:, half, :].unsqueeze(2).to_broadcast([P, TOPK, TOPK]),
                                           iota[:].unsqueeze(1).to_broadcast([P, TOPK, TOPK]), ALU.is_equal))
                    ch.settle()
                    ch(e.tensor_tensor(hot[:], hot[:], sif[:].unsqueeze(2).to_broadcast([P, 2, TOPK, TOPK]), ALU.mult))
                    ch.settle()
                    ch(e.tensor_reduce(pick[:], hot[:], AX.X, ALU.add))
                    ch.settle()
                    ch(e.scalar_tensor_tensor(out=idx[:, z, :], in0=pick[:, 0, :], scalar=float(NKEY),
                                              in1=pick[:, 1, :], op0=ALU.mult, op1=ALU.add))
                    assert ch.n == FOUND, ch.n
                    ch.settle()
                    e.sem_inc(idx_d, 1)

                def unit(u, z, loaded, rows=None, norm=None):
                    e.wait_ge(exp_d, u + 1)
                    e.reciprocal(den[:, z, :], den[:, z, :]).then_inc(gate_d, 1)
                    e.wait_ge(gate_d, 2 * u + 1)
                    e.tensor_scalar(gate[:, z, :], ex[:, z, :], den[:, z, :], None, ALU.mult).then_inc(gate_d, 1)
                    if rows is not None:
                        e.wait_ge(h_c, rows)
                    for g in range(NG):
                        for k in range(G * g, G * (g + 1)):
                            e.wait_ge(uv_in[k], 16 * (u + 1))
                            mm = e.tensor_tensor_reduce(ring[:, k, 0:D], ring[:, k, 0:D], hrow[:], 1.0, 0.0,
                                                        ALU.mult, ALU.add, dot[:, z, k:k + 1])
                        mm.then_inc(dots, 1)
                        if g == 0 and norm is not None:
                            last_norm(norm, P)
                        if g == 1 and loaded is not None:
                            find(u + 1, 1 - z, loaded)
                        e.wait_ge(gelu, NG * u + g + 1)
                        ks = slice(G * g, G * (g + 1))
                        e.tensor_tensor(wt[:, z, ks], act[:, z, ks], gate[:, z, ks], ALU.mult).then_inc(wtd, 1)

                def last_norm(m, n):
                    e.wait_ge(rootd, m + 1)
                    e.reciprocal(col[0:n, 1:2], col[0:n, 1:2]).then_inc(norm_d, 1)
                    e.wait_ge(norm_d, m + 1)
                    e.wait_ge(y_out, 16 * m)
                    e.scalar_tensor_tensor(out=yrow[0:n, :], in0=x2[0:n, :], scalar=col[0:n, 1:2], in1=grow[0:n, :],
                                           op0=ALU.mult, op1=ALU.mult).then_inc(yd, 1)

                e.wait_ge(c_in, 48)
                find(0, 0, 1)
                unit(0, 0, 1, rows=1)
                with e.Fori(0, PT) as m:
                    t = m * (PH // 2)
                    unit(2 * t + 1, 1, t + 2)
                    with e.Fori(1, PH // 2) as hh:
                        unit(2 * (t + hh), 0, t + hh + 1)
                        unit(2 * (t + hh) + 1, 1, t + hh + 2)
                    unit(2 * (t + PH // 2), 0, t + PH // 2 + 1, rows=m + 2, norm=m)
                for u in range(PT * PH + 1, NU):
                    unit(u, u % 2, (u + 1) // 2 + 1 if u + 1 < NU else None)
                last_norm(PT, TS)

            @block.scalar
            def _(e):
                e.wait_ge(const_set, 2)
                e.wait_ge(c_in, 48)

                def exps(u, z):
                    e.wait_ge(idx_d, u + 1)
                    e.activation(ex[:, z, :], bs[:], ACT.Exp, bias=nmax[:], accum_out=den[:, z, :]).then_inc(exp_d, 1)

                def unit(u, z, places, last=False):
                    n = P if places is self.ident else TS
                    for g in range(NG):
                        ks = slice(G * g, G * (g + 1))
                        e.wait_ge(dots, NG * u + g + 1)
                        e.activation(act[:, z, ks], dot[:, z, ks], ACT.Gelu).then_inc(gelu, 1)
                        e.wait_ge(wtd, NG * u + g + 1)
                        for k in range(G * g, G * (g + 1)):
                            e.wait_ge(pv, TOPK * u + k + TOPK - 2 * G + 1)
                            e.mul(diag[:, k % (2 * G), 0:n], places[:], wt[:, z, k:k + 1]).then_inc(diagd, 1)
                    if not last:
                        exps(u + 1, 1 - z)

                def root_mean_square(m, n):
                    e.wait_ge(accd, m + 1)
                    e.wait_ge(yd, m)
                    e.copy(x2[0:n, :], acc[0:n, :, :].rearrange("p a b -> p (a b)")).then_inc(x2d, 1)
                    e.wait_ge(x2d, m + 1)
                    e.activation(sq[0:n, :], x2[0:n, :], ACT.Square, accum_out=col[0:n, 0:1]).then_inc(ssd, 1)
                    e.wait_ge(ssd, m + 1)
                    e.activation(col[0:n, 1:2], col[0:n, 0:1], ACT.Sqrt, bias=epsc[0:n], scale=1.0 / D
                                 ).then_inc(rootd, 1)

                def copy_rows(m):
                    e.wait_ge(h_in, 16 * HU * (m + 1))
                    e.copy(hrow[:], hnext[:]).then_inc(h_c, 1)

                def store(m, n, row):
                    e.wait_ge(yd, m + 1)
                    e.dma_start(o["y"][ds(row, n), :], yrow[0:n, :]).then_inc(y_out, 16)

                exps(0, 0)
                copy_rows(0)
                with e.Fori(0, PT) as m:
                    with e.Fori(0, PH // 2) as hh:
                        for z in range(2):
                            unit(m * PH + 2 * hh + z, z, self.ident)
                    copy_rows(m + 1)
                    root_mean_square(m, P)
                    store(m, P, m * P)
                for u in range(PT * PH, NU):
                    unit(u, u % 2, fold, u == NU - 1)
                root_mean_square(PT, TS)
                store(PT, TS, TP)
                e.wait_ge(y_out, 16 * (PT + 1))

            @block.tensor
            def _(e):
                def begin(m, n):
                    e.wait_ge(x_in, 16 * (m + 1))
                    e.wait_ge(x2d, m)
                    for d in range(2):
                        e.matmul(acc[0:n, d, :], self.ident[0:n, 0:n], xrow[0:n, d * 512:(d + 1) * 512],
                                 start=True, stop=False)

                def unit(u, n):
                    for k in range(TOPK):
                        e.wait_ge(diagd, TOPK * u + k + 1)
                        for d in range(2):
                            mm = e.matmul(acc[0:n, d, :], diag[:, k % (2 * G), 0:n],
                                          ring[:, k, D + d * 512:D + (d + 1) * 512], start=False, stop=False)
                        mm.then_inc(pv, 1)

                def end(n):
                    for d in range(2):
                        mm = e.matmul(acc[0:n, d, :], zero[0:n, 0:n], grow[0:n, d * 512:(d + 1) * 512],
                                      start=False, stop=True)
                    mm.then_inc(accd, 1)

                e.wait_ge(const_set, 2)
                e.wait_ge(c_in, 48)
                e.sem_inc(pv, TOPK)
                with e.Fori(0, PT) as m:
                    begin(m, P)
                    with e.Fori(0, PH) as h:
                        unit(m * PH + h, P)
                    end(P)
                begin(PT, TS)
                for u in range(PT * PH, NU):
                    unit(u, TS)
                end(TS)


def layout(inp):
    a = {k: np.ascontiguousarray(v) for k, v in inp.items()}
    f = np.float32
    eye = np.eye(P, dtype=f)
    head = np.kron(np.eye(2, dtype=f), np.ones((HD, HD), f))
    x = np.concatenate([a["x_prompt"].reshape(TP, D), a["x_sample"].reshape(TS, D)])
    w_in = a["w_in"][0]
    main = slice(OFF_B, OFF_B + 3 * RW)
    lora = slice(OFF_B + 3 * RW, OFF_G)
    tiles = lambda v: v.reshape(-1, P).T

    def loras(v):
        v = np.moveaxis(v, -1, 0)
        out = np.zeros((LG, 3) + v.shape[1:], f)
        for m, (off, n) in enumerate(((0, LW), (LW, LA), (LW + LA, LG))):
            out[:n, m] = v[off:off + n]
        return out

    pos = np.concatenate([np.arange(TP), np.tile(8192 + np.arange(NS), NB)]).astype(f)
    pos = np.concatenate([pos, np.zeros(TT * P - T, f)])
    angle = pos[:, None] * (f(500000.0) ** (-np.arange(RH, dtype=f) / f(RH)))[None, :]
    rope = [fn(angle).astype(f).reshape(TT, P, RH).transpose(1, 0, 2) for fn in (np.cos, np.sin)]
    diff = WIN + np.arange(WIN)[:, None] - np.arange(2 * WIN)[None, :]
    seen = (diff >= 0) & (diff < WIN)
    band = np.where(seen, f(0), f(NEG))
    first = np.where(seen & (np.arange(2 * WIN) >= WIN)[None, :], f(0), f(NEG))
    row_b, row_n = (np.tile(z, NQ // NKV)[:, None] for z in (np.repeat(np.arange(NB), NS), np.tile(np.arange(NS), NB)))
    key_b = np.concatenate([np.repeat(np.arange(NB), WIN), np.repeat(np.arange(NB), NS)])[None, :]
    key_j = np.concatenate([np.tile(np.arange(WIN), NB), WIN + np.tile(np.arange(NS), NB)])[None, :]
    ddiff = WIN + row_n - key_j
    dmask = np.where((row_b == key_b) & (ddiff >= 0) & (ddiff < WIN), f(0), f(NEG))
    ct = np.tile(np.arange(CH), 2)
    levels = []
    for n in range(LEVELS):
        half = 1 << n
        same = ct[:, None] // (2 * half) == ct[None, :] // (2 * half)
        levels.append((head * same * ((ct // half) % 2 == 0)[:, None] * ((ct // half) % 2 == 1)[None, :]).astype(f))
    db, dn = np.tile(np.repeat(np.arange(NB), NS), 2), np.tile(np.arange(NS), 2 * NB)
    dh = np.repeat(np.arange(2), TS)
    dsame = (db[:, None] == db[None, :]) & (dh[:, None] == dh[None, :])
    dl0 = dsame & (dn[:, None] // 2 == dn[None, :] // 2) & (dn[:, None] < dn[None, :])
    dl1 = dsame & (dn[:, None] < 2) & (dn[None, :] >= 2)
    state0 = np.zeros((2, HD, NPAIR, NB, 2, HD), f)
    start = a["state_wkv"][0].reshape(NB, NPAIR, 2, HD, HD)
    for h in range(2):
        state0[h, :, :, :, h, :] = start[:, :, h].transpose(3, 1, 0, 2)
    state0 = state0.reshape(P, NPAIR, NB, P)
    blocks = lambda w: w.reshape(-1, P, w.shape[1] // P, P).transpose(2, 1, 0, 3)
    pairs = lambda w: w.reshape(w.shape[0], NPAIR, P).transpose(1, 0, 2)
    mu, b_in, sh = a["shift_mu"][0], a["b_in"][0], a["state_shift"][0]
    return {
        "ident": eye, "ones": np.ones((P, P), f), "headones": head,
        "xT": x.T, "x": x,
        "norm1_g": tiles(a["norm1_g"][0]),
        "w_in": w_in, "b_qkv": b_in[None, :QKV],
        "w_main": w_in[:, main].reshape(KT, P, NMAIN, P).transpose(2, 1, 0, 3),
        "w_lora": w_in[:, lora].reshape(KT, P, -1).transpose(1, 0, 2),
        "b_main": tiles(b_in[main]), "mu_main": tiles(mu[:3 * RW]),
        "shift_main": sh[:, :3 * RW].reshape(NB, NMAIN, P).transpose(2, 1, 0),
        "lora_b": loras(b_in[lora]), "lora_mu": loras(mu[3 * RW:]),
        "lora_shift": loras(sh[:, 3 * RW:]),
        "cos": rope[0], "sin": rope[1], "band": band, "band_first": first,
        "sinks": a["attn_sinks"].reshape(NKV, 2, 2).transpose(0, 2, 1).reshape(1, NQ),
        "cache_k": a["cache_win_k"].reshape(NB, WIN, KW), "cache_v": a["cache_win_v"].reshape(NB, WIN, KW),
        "w2": pairs(a["w2"][0]), "a2": pairs(a["a2"][0]), "g2": pairs(a["g2"][0]),
        "pair_par": np.stack([a[n][0].reshape(NPAIR, P) for n in ("w0", "a0", "k_k", "k_a", "r_k")], axis=-1),
        "level_masks": np.stack(levels, axis=1), "low0": levels[0].T,
        "before": (head * (ct[:, None] < ct[None, :])).astype(f),
        "upto": np.stack([(ct[:, None] <= np.arange(CH)[None, :])] * 2, axis=1).astype(f),
        "dec_masks": np.stack([dsame * (dn[:, None] < dn[None, :]), dl0, dl1, dl0.T], axis=1).astype(f),
        "dec_upto": np.stack([(db[:, None] == db[None, :TS]) & (dn[:, None] <= dn[None, :TS])] * 2, axis=1).astype(f),
        "dec_own": (db[:, None] == np.arange(NB)[None, :]).astype(f),
        "state0": state0,
        "gn_par": np.stack([tiles(a["ln_x_w"][0]), tiles(a["ln_x_b"][0])], axis=1),
        "w_merge": np.concatenate([blocks(w_in[:, OFF_G:OFF_G + D]), blocks(w_in[:, OFF_G + D:]),
                                   blocks(a["w_up_a"][0]), blocks(a["w_up_b"][0])], axis=2),
        "b_gate": b_in[OFF_G:].reshape(2, KT, P).transpose(2, 1, 0),
        "w_o": a["w_o"][0], "norm2_g": a["norm2_g"], "final_g": a["final_norm_g"][None],
        "w_query": blocks(a["w_query"][0]),
        "sub_keys": a["sub_keys"][0].reshape(NHALF, NKEY, P).transpose(0, 2, 1),
        "uv": np.concatenate([a["expert_u"][0], a["expert_v"][0]], axis=1),
        "fold": np.tile(np.eye(TS, dtype=f), (P // TS, 1)),
        "iota": np.arange(TOPK, dtype=f)[None],
        "dmask": dmask, "dsink": np.repeat(a["attn_sinks"].reshape(NKV, NQ // NKV), TS, axis=1).T,
    }


OUTS = {"y": (T, D), "prompt_win_k": (WIN, KW), "prompt_win_v": (WIN, KW), "prompt_wkv": (NQ, HD, HD),
        "shift": (1 + NB, OFF_G - OFF_B), "sample_win_k": (NB, WIN, KW), "sample_win_v": (NB, WIN, KW),
        "sample_wkv": (NB, NQ, HD, HD)}


def kernel(**inputs):
    import concourse.bacc as _bacc
    from concourse.bass_utils import run_bass_kernel_spmd as _run

    nc = _bacc.Bacc("TRN2", target_bir_lowering=False, num_devices=1)
    arrays, ins, outs = {}, {}, {}
    for name, array in layout(inputs).items():
        array = np.ascontiguousarray(array)
        arrays[f"in_{name}_dram"] = array
        ins[name] = nc.dram_tensor(f"in_{name}_dram", array.shape, mybir.dt.from_np(array.dtype),
                                   kind="ExternalInput").ap()
    for name, shape in OUTS.items():
        outs[name] = nc.dram_tensor(f"out_{name}_dram", shape, F32, kind="ExternalOutput").ap()
    Program(nc, ins, outs).build()
    r = _run(nc, [arrays], core_ids=[0])
    got = {name: np.asarray(r.results[0][f"out_{name}_dram"]) for name in OUTS}
    win = lambda name, *lead: got[name].reshape(lead + (WIN, NKV, HD))
    wkv = lambda name, *lead: np.ascontiguousarray(got[name].reshape(lead + (NQ, HD, HD)).swapaxes(-1, -2))
    return (got["y"][:TP].reshape(1, TP, D), got["y"][TP:].reshape(NB, NS, D),
            win("prompt_win_k", 1, 1), win("prompt_win_v", 1, 1), wkv("prompt_wkv", 1, 1), got["shift"][None, :1],
            win("sample_win_k", 1, NB), win("sample_win_v", 1, NB), wkv("sample_wkv", 1, NB), got["shift"][None, 1:])
```

```python
from contextlib import ExitStack, contextmanager

import numpy as np
import concourse.bass as bass
from concourse import mybir

ALU = mybir.AluOpType
ACT = mybir.ActivationFunctionType
AX = mybir.AxisListType
F32 = mybir.dt.float32
U32 = mybir.dt.uint32
ds = bass.ds

P = 128
D = 1024
KT = D // P
TP = 1024
NB, NS = 8, 4
TS = NB * NS
T = TP + TS
TT = (T + P - 1) // P
NC = 3
CW = T // NC
HD = 64
NQ, NKV = 8, 2
QW, KW = NQ * HD, NKV * HD
QKV = QW + 2 * KW
ROT = HD // 4
RH = ROT // 2
WIN = 128
NBLK = TP // WIN
RW = 512
NPAIR = RW // P
LW, LA, LG = 32, 32, 96
NMAIN = 3 * RW // P
OFF_B = QKV
OFF_G = OFF_B + 3 * RW + LW + LA + LG
CH = 64
LANES = 4
NQUAD = TP // CH // LANES
LEVELS = 6
PH, NKEY, TOPK = 8, 128, 16
NHALF = 2 * PH
WORK = (25 + LEVELS - 1) * LANES * P + 2 * LANES + 6 * P
NEG = -1.0e30
EPS = 1e-5
GN_EPS = 64e-5
SCALE = HD ** -0.5


def tokens_in(tile):
    return P if tile < TP // P else TS


class Chain:

    def __init__(self, eng, sem, base=0):
        self.eng, self.sem, self.base, self.n = eng, sem, base, 0

    def __call__(self, ins):
        ins.then_inc(self.sem, 1)
        self.n += 1
        return ins

    def settle(self):
        self.eng.wait_ge(self.sem, self.base + self.n)


class Carver:

    def __init__(self, buffer):
        self.buffer, self.at = buffer, 0

    def __call__(self, *shape):
        n = int(np.prod(shape))
        part = self.buffer[:, self.at:self.at + n]
        self.at += n
        if len(shape) == 2:
            return part.rearrange("p (a b) -> p a b", a=shape[0])
        if len(shape) == 3:
            return part.rearrange("p (a b c) -> p a b c", a=shape[0], b=shape[1])
        return part


class Program:

    def __init__(self, nc, i, o):
        self.nc, self.i, self.o = nc, i, o

    def sb(self, ctx, name, shape, dt=F32):
        return ctx.enter_context(self.nc.sbuf_tensor(name, shape, dt))

    def ps(self, ctx, name, shape, dt=F32):
        return ctx.enter_context(self.nc.psum_tensor(name, shape, dt))

    def sems(self, *names):
        new = [self.held.enter_context(self.nc.semaphore(n)) for n in names]
        self.owned += new
        return new

    @contextmanager
    def stage(self):
        nc = self.nc
        with ExitStack() as self.held:
            self.owned = []
            with nc.Block() as block, ExitStack() as c:
                yield c, block
            numbers = sorted(s.num for s in self.owned)
            first = numbers[0]
            for a, b in zip(numbers, numbers[1:] + [None]):
                if b != a + 1:
                    nc.gpsimd.sem_clear(range(first, a + 1))
                    first = b
            nc.all_engine_barrier()

    def build(self):
        nc = self.nc
        dr = lambda n, s: nc.dram_tensor(n, s, F32).ap()
        self.x1_d = dr("x1_rows", [T, D])
        self.h2_d = dr("h2_rows", [T, D])
        self.gate_d = dr("gate_b_tiles", [KT, P, T])
        with ExitStack() as c:
            self.ident = self.sb(c, "ident", [P, P])
            self.headones = self.sb(c, "headones", [P, P])
            self.ones = self.sb(c, "ones", [P, P])
            with ExitStack() as c1:
                self.hT = self.sb(c1, "hT", [P, KT, T])
                self.attT = self.sb(c1, "attT", [P, QW // P, T])
                with ExitStack() as c2:
                    self.mixed = self.sb(c2, "mixed", [P, NMAIN, T])
                    self.lw = self.sb(c2, "lw", [LW, T])
                    self.la = self.sb(c2, "la", [LA, T])
                    self.lg = self.sb(c2, "lg", [LG, T])
                    self.norm_in()
                    with ExitStack() as c3:
                        self.w_qkv = self.sb(c3, "w_qkv", [P, KT, QKV])
                        self.project_rwkv()
                        self.qkv_padded = self.sb(c3, "qkv", [P, 1 + TT, QKV])
                        self.qkv = self.qkv_padded[:, 1:, :]
                        self.project_qkv()
                        self.attention()
                    self.rwkv()
                    with ExitStack() as c3:
                        self.w_o = self.sb(c3, "w_o", [P, KT, D])
                        self.merge()
                        self.output_projection()
            self.experts()

    def norm_in(self):
        i = self.i
        with self.stage() as (c, block):
            rstd = self.sb(c, "rstd", [P, T])
            sq = self.sb(c, "sq", [P, 2, T])
            g = self.sb(c, "g1", [P, KT])
            epsc = self.sb(c, "epsc", [P, 1])
            ms = self.ps(c, "ms", [P, NC, 512])
            consts_in, g_in, eps_set, x_sq, sq_used, root, inv, normed = self.sems(
                "consts_in", "g_in", "eps_set", "x_sq", "sq_used", "root", "inv", "normed")
            x_in = self.sems(*[f"x_in{k}" for k in range(KT)])
            hT = self.hT

            @block.sync
            def _(e):
                e.dma_start(self.ones[:, :], i["ones"]).then_inc(consts_in, 16)
                e.dma_start(self.ident[:, :], i["ident"]).then_inc(consts_in, 16)
                e.dma_start(self.headones[:, :], i["headones"]).then_inc(consts_in, 16)
                for k in range(KT):
                    e.dma_start(hT[:, k, :], i["xT"][k * P:(k + 1) * P, :]).then_inc(x_in[k], 16)
                e.dma_start(g[:, :], i["norm1_g"]).then_inc(g_in, 16)

            @block.scalar
            def _(e):
                for k in range(KT):
                    e.wait_ge(x_in[k], 16)
                    if k >= 2:
                        e.wait_ge(sq_used, k - 1)
                    e.activation(sq[:, k % 2, :], hT[:, k, :], ACT.Square).then_inc(x_sq, 1)
                e.wait_ge(sq_used, KT)
                e.wait_ge(eps_set, 1)
                for n in range(NC):
                    e.activation(rstd[:, n * CW:(n + 1) * CW], ms[:, n, 0:CW], ACT.Sqrt,
                                 bias=epsc[:, 0:1], scale=1.0 / D).then_inc(root, 1)

            @block.tensor
            def _(e):
                e.wait_ge(consts_in, 48)
                for k in range(KT):
                    e.wait_ge(x_sq, k + 1)
                    for n in range(NC):
                        mm = e.matmul(ms[:, n, 0:CW], self.ones[:, :], sq[:, k % 2, n * CW:(n + 1) * CW],
                                      start=(k == 0), stop=(k == KT - 1))
                    mm.then_inc(sq_used, 1)

            @block.vector
            def _(e):
                e.memset(epsc[:, :], EPS).then_inc(eps_set, 1)
                e.wait_ge(root, NC)
                e.reciprocal(rstd[:, :], rstd[:, :]).then_inc(inv, 1)
                e.wait_ge(inv, 1)
                e.wait_ge(g_in, 16)
                for k in range(KT):
                    e.scalar_tensor_tensor(out=hT[:, k, :], in0=hT[:, k, :], scalar=g[:, k:k + 1],
                                           in1=rstd[:, :], op0=ALU.mult, op1=ALU.mult).then_inc(normed, 1)
                e.wait_ge(normed, KT)

    def project_rwkv(self):
        i, o = self.i, self.o
        hT = self.hT
        with self.stage() as (c, block):
            w = self.sb(c, "w_main", [P, 2, KT, P])
            wl = self.sb(c, "w_lora", [P, KT, LW + LA + LG])
            bias = self.sb(c, "b_main", [P, NMAIN])
            mu = self.sb(c, "mu_main", [P, NMAIN])
            sh = self.sb(c, "shift_main", [P, NMAIN, NB])
            lb = self.sb(c, "lora_bias", [LG, 3])
            lmu = self.sb(c, "lora_mu", [LG, 3])
            lsh = self.sb(c, "lora_shift", [LG, 3, NB])
            praw = self.sb(c, "praw", [P, 2, 1 + T])
            dif = self.sb(c, "dif", [P, 2, T])
            prevs = self.sb(c, "prevs", [P, 2, NB, NS])
            last = self.sb(c, "last", [P, NMAIN + 3, 1 + NB])
            lrow = self.sb(c, "lrow", [1 + NB, 3 * RW + LW + LA + LG])
            pp = [self.ps(c, f"pp{s}", [P, NC, 512]) for s in range(2)]
            pt = self.ps(c, "pt", [1 + NB, 512])
            par_in, lora_in, zeroed, prod, evac, mixstep, laststep, lrow_t, lrow_c, out_s = self.sems(
                "par_in", "lora_in", "zeroed", "prod", "evac", "mixstep", "laststep", "lrow_t", "lrow_c",
                "out_s")
            w_in = self.sems("w_in0", "w_in1")
            LORAS = [(0, LW, self.lw), (LW, LA, self.la), (LW + LA, LG, self.lg)]

            wq_in, = self.sems("w_qkv_in")

            @block.sync
            def _(e):
                for a, b in ((bias, "b_main"), (mu, "mu_main"), (sh, "shift_main"), (lb, "lora_b"),
                             (lmu, "lora_mu"), (lsh, "lora_shift")):
                    e.dma_start(a[:], i[b]).then_inc(par_in, 16)
                e.dma_start(wl[:, :, :], i["w_lora"]).then_inc(lora_in, 16)
                with e.Fori(0, NMAIN // 2) as t:
                    for s in range(2):
                        e.wait_ge(prod, 2 * t + s + 1)
                        e.dma_start(w[:, s, :, :], i["w_main"][ds(2 * t + s, 1)].rearrange("o p k f -> (o p) k f")
                                    ).then_inc(w_in[s], 16)
                e.dma_start(self.w_qkv[:], i["w_in"][:, 0:QKV].rearrange("(k p) f -> p k f", p=P)).then_inc(wq_in, 16)
                e.wait_ge(lrow_c, 1)
                e.dma_start(o["shift"], lrow[:, :]).then_inc(out_s, 16)
                e.wait_ge(out_s, 16)
                e.wait_ge(wq_in, 16)

            @block.tensor
            def _(e):
                e.sem_inc(prod, 2)
                with e.Fori(0, NMAIN // 2) as t:
                    for s in range(2):
                        e.wait_ge(w_in[s], 16 * (t + 1))
                        e.wait_ge(evac, NC * (2 * t + s) + 1)
                        for k in range(KT):
                            for n in range(NC):
                                mm = e.matmul(pp[s][:, n, 0:CW], w[:, s, k, :], hT[:, k, n * CW:(n + 1) * CW],
                                              start=(k == 0), stop=(k == KT - 1))
                        mm.then_inc(prod, 1)
                e.wait_ge(lora_in, 16)
                for m, (off, width, _) in enumerate(LORAS):
                    s = m % 2
                    e.wait_ge(evac, NC * (NMAIN + m) + 1)
                    for k in range(KT):
                        for n in range(NC):
                            mm = e.matmul(pp[s][0:width, n, 0:CW], wl[:, k, off:off + width],
                                          hT[:, k, n * CW:(n + 1) * CW], start=(k == 0), stop=(k == KT - 1))
                    mm.then_inc(prod, 1)
                e.wait_ge(laststep, NMAIN + 3 + 2)
                for m in range(NMAIN + 3):
                    width = P if m < NMAIN else LORAS[m - NMAIN][1]
                    off = m * P if m < NMAIN else NMAIN * P + LORAS[m - NMAIN][0]
                    if m:
                        e.wait_ge(lrow_t, m)
                    e.transpose(pt[:, 0:width], last[0:width, m, :], self.ident[0:width, 0:width]
                                ).then_inc(mixstep, 1)

            def evacuate(e, s, rows, b):
                for n in range(NC):
                    e.activation(praw[0:rows, s, 1 + n * CW:1 + (n + 1) * CW], pp[s][0:rows, n, 0:CW],
                                 ACT.Identity, bias=b).then_inc(evac, 1)

            bcol = self.sb(c, "bcol", [P, 2, 1])
            bstep, = self.sems("bstep")

            @block.scalar
            def _(e):
                e.sem_inc(evac, NC + 1)
                e.wait_ge(par_in, 96)
                with e.Fori(0, NMAIN // 2) as t:
                    for s in range(2):
                        e.copy(bcol[:, s, :], bias[:, ds(2 * t + s, 1)]).then_inc(bstep, 1)
                        e.wait_ge(bstep, 2 * t + s + 1)
                        e.wait_ge(prod, 2 * t + s + 3)
                        e.wait_ge(laststep, 2 * t + s + 1)
                        evacuate(e, s, P, bcol[:, s, :])
                for m in range(3):
                    s = m % 2
                    e.wait_ge(prod, NMAIN + m + 3)
                    e.wait_ge(laststep, NMAIN + m + 1)
                    evacuate(e, s, LORAS[m][1], lb[0:LORAS[m][1], m:m + 1])

            mstep, = self.sems("mstep")

            def mix(e, ch, s, rows, shift, muc, out, lastout):
                p = praw[0:rows, s, :]
                ch(e.tensor_copy(prevs[0:rows, s, :, 0], shift))
                ch(e.tensor_copy(prevs[0:rows, s, :, 1:NS],
                                 p[:, 1 + TP:1 + T].rearrange("p (b n) -> p b n", b=NB)[:, :, 0:NS - 1]))
                ch(e.tensor_tensor(dif[0:rows, s, 0:TP], p[:, 0:TP], p[:, 1:1 + TP], ALU.subtract))
                ch.settle()
                ch(e.tensor_tensor(dif[0:rows, s, TP:T], prevs[0:rows, s, :, :].rearrange("p b n -> p (b n)"),
                                   p[:, 1 + TP:1 + T], ALU.subtract))
                ch(e.tensor_copy(lastout[:, 1:1 + NB],
                                 p[:, 1 + TP:1 + T].rearrange("p (b n) -> p b n", b=NB)[:, :, NS - 1]))
                ch(e.tensor_copy(lastout[:, 0:1], p[:, TP:TP + 1]))
                ch.settle()
                ch(e.scalar_tensor_tensor(out=out, in0=dif[0:rows, s, :], scalar=muc, in1=p[:, 1:1 + T],
                                          op0=ALU.mult, op1=ALU.add))
                ch.settle()

            mucol = self.sb(c, "mucol", [P, 2, 1])

            @block.vector
            def _(e):
                e.memset(praw[:, :, 0:1], 0.0).then_inc(zeroed, 1)
                e.wait_ge(zeroed, 1)
                e.wait_ge(par_in, 96)
                e.sem_inc(laststep, 2)
                with e.Fori(0, NMAIN // 2) as t:
                    for s in range(2):
                        ch = Chain(e, mstep, (2 * t + s) * 8)
                        ch(e.tensor_copy(mucol[:, s, :], mu[:, ds(2 * t + s, 1)]))
                        e.wait_ge(evac, NC * (2 * t + s + 2) + 1)
                        mix(e, ch, s, P, sh[:, ds(2 * t + s, 1), :].rearrange("p o b -> p (o b)"), mucol[:, s, :],
                            self.mixed[:, ds(2 * t + s, 1), :].rearrange("p o t -> p (o t)"),
                            last[:, ds(2 * t + s, 1), :].rearrange("p o b -> p (o b)"))
                        assert ch.n == 8
                        e.sem_inc(laststep, 1)
                ch = Chain(e, mstep, NMAIN * 8)
                for m, (off, width, out) in enumerate(LORAS):
                    e.wait_ge(evac, NC * (NMAIN + m + 2) + 1)
                    mix(e, ch, m % 2, width, lsh[0:width, m, :], lmu[0:width, m:m + 1], out[:, :],
                        last[0:width, NMAIN + m, :])
                    e.sem_inc(laststep, 1)
                for m in range(NMAIN + 3):
                    width = P if m < NMAIN else LORAS[m - NMAIN][1]
                    off = m * P if m < NMAIN else NMAIN * P + LORAS[m - NMAIN][0]
                    e.wait_ge(mixstep, m + 1)
                    e.tensor_copy(lrow[:, off:off + width], pt[:, 0:width]).then_inc(lrow_t, 1)
                e.wait_ge(lrow_t, NMAIN + 3)
                e.sem_inc(lrow_c, 1)

    def project_qkv(self):
        i = self.i
        hT, qkv = self.hT, self.qkv
        with self.stage() as (c, block):
            w = self.w_qkv
            bb = self.sb(c, "b_qkv", [P, QKV])
            pq = [self.ps(c, f"pq{s}", [P, 2, 512]) for s in range(2)]
            prod, evac = self.sems("qkv_prod", "qkv_evac")
            b_in, = self.sems("bq_in")

            @block.sync
            def _(e):
                e.dma_start(bb[:, :], i["b_qkv"].to_broadcast([P, QKV])).then_inc(b_in, 16)

            @block.tensor
            def _(e):
                for m in range(TT):
                    n = tokens_in(m)
                    if m >= 2:
                        e.wait_ge(evac, m)
                    for k in range(KT):
                        lhsT = hT[:, k, m * P:m * P + n]
                        e.matmul(pq[m % 2][0:n, 0, :], lhsT, w[:, k, 0:QW], start=(k == 0), stop=(k == KT - 1))
                        mm = e.matmul(pq[m % 2][0:n, 1, 0:2 * KW], lhsT, w[:, k, QW:QKV],
                                      start=(k == 0), stop=(k == KT - 1))
                    mm.then_inc(prod, 1)

            @block.vector
            def _(e):
                e.memset(self.qkv_padded[:, 0, QW + KW:QKV], 0.0).then_inc(evac, 1)
                e.wait_ge(b_in, 16)
                for m in range(TT):
                    n = tokens_in(m)
                    e.wait_ge(prod, m + 1)
                    e.tensor_tensor(qkv[0:n, m, :], pq[m % 2][0:n, :, :].rearrange("p a b -> p (a b)")[:, 0:QKV],
                                    bb[0:n, :], ALU.add).then_inc(evac, 1)
                e.wait_ge(evac, TT + 1)

    def rope(self):
        i = self.i
        NH = NQ + NKV
        with self.stage() as (c, block):
            cs = self.sb(c, "rope_cos", [P, TT, RH])
            sn = self.sb(c, "rope_sin", [P, TT, RH])
            tmp = [self.sb(c, f"rope_t{n}", [P, TT, NH, RH]) for n in range(4)]
            tab_in, step, = self.sems("tab_in", "rope_step")

            @block.sync
            def _(e):
                e.dma_start(cs[:], i["cos"]).then_inc(tab_in, 16)
                e.dma_start(sn[:], i["sin"]).then_inc(tab_in, 16)

            @block.vector
            def _(e):
                e.wait_ge(tab_in, 32)
                ch = Chain(e, step)
                for rows, a, b in ((P, 0, TT - 1), (TS, TT - 1, TT)):
                    heads = self.qkv[0:rows, a:b, 0:NH * HD].rearrange("p m (h d) -> p m h d", h=NH)
                    x1, x2 = heads[:, :, :, 0:RH], heads[:, :, :, RH:ROT]
                    n = b - a
                    co = cs[0:rows, a:b, :].unsqueeze(2).to_broadcast([rows, n, NH, RH])
                    si = sn[0:rows, a:b, :].unsqueeze(2).to_broadcast([rows, n, NH, RH])
                    t = [z[0:rows, a:b] for z in tmp]
                    ch(e.tensor_tensor(t[0], x1, co, ALU.mult))
                    ch(e.tensor_tensor(t[1], x2, si, ALU.mult))
                    ch(e.tensor_tensor(t[2], x2, co, ALU.mult))
                    ch(e.tensor_tensor(t[3], x1, si, ALU.mult))
                    ch.settle()
                    ch(e.tensor_tensor(x1, t[0], t[1], ALU.subtract))
                    ch(e.tensor_tensor(x2, t[2], t[3], ALU.add))
                ch.settle()

    def attention(self):
        i, o = self.i, self.o
        qkv, attT, ident = self.qkv, self.attT, self.ident
        self.rope()
        G = NQ // NKV
        with self.stage() as (c, block):
            band = self.sb(c, "band", [P, 2 * WIN])
            band1 = self.sb(c, "band_first", [P, 2 * WIN])
            sink = self.sb(c, "sinks", [P, NQ])
            qT = self.sb(c, "qT", [P, QW // P, P])
            kT = self.sb(c, "kT", [P, 2, NKV, P])
            rows = self.sb(c, "qk_rows", [P, 2, QW + KW])
            sc = self.sb(c, "sc", [P, 2, G, 2 * WIN])
            pr = self.sb(c, "probs", [P, 2, G, 2 * WIN])
            pT = self.sb(c, "probsT", [P, 4, 4 * P])
            mx = self.sb(c, "mx", [P, 2, G])
            nmx = self.sb(c, "nmx", [P, 2, G])
            sx = self.sb(c, "sx", [P, 2, G])
            es = self.sb(c, "es", [P, 2, G])
            den = self.sb(c, "den", [P, 2, G])
            att = self.sb(c, "att", [P, QW])
            psq = self.ps(c, "psq", [P, 4, P])
            psk = self.ps(c, "psk", [P, 4, P])
            pss = self.ps(c, "pss", [P, G, 2 * WIN])
            pst = [self.ps(c, f"pst{n}", [P, 4 * P]) for n in range(2)]
            pso = self.ps(c, "pso", [P, 2, G, HD])
            (consts2, kv_out, kT_set, rows_c, qk_t, qk_c, s_done, s_taken, neg, expd, p_t, p_c, o_done, o_taken,
             a_t, a_c, vstep) = self.sems(
                "consts2", "kv_out", "kT_set", "rows_copied", "qk_t", "qk_c", "s_done", "s_taken", "neg", "expd",
                "p_t", "p_c", "o_done", "o_taken", "a_t", "a_c", "vstep")
            NP = 2 * G // 4
            VS = 8
            LAST = NBLK - 2

            def blocks(e, block_of):
                with e.Fori(0, LAST // 2) as t:
                    for s in range(2):
                        block_of(2 * t + s, s, False)
                for u in range(LAST, NBLK):
                    block_of(u, u % 2, u == NBLK - 1)

            @block.sync
            def _(e):
                e.dma_start(band[:], i["band"]).then_inc(consts2, 16)
                e.dma_start(band1[:], i["band_first"]).then_inc(consts2, 16)
                e.dma_start(sink[:], i["sinks"].to_broadcast([P, NQ])).then_inc(consts2, 16)
                e.dma_start(o["prompt_win_k"], qkv[:, TT - 2, QW:QW + KW]).then_inc(kv_out, 16)
                e.dma_start(o["prompt_win_v"], qkv[:, TT - 2, QW + KW:QKV]).then_inc(kv_out, 16)
                for name, cache, off in (("sample_win_k", "cache_k", QW), ("sample_win_v", "cache_v", QW + KW)):
                    e.dma_start(o[name][:, 0:WIN - NS, :], i[cache][:, NS:WIN, :]).then_inc(kv_out, 16)
                    for b in range(NB):
                        e.dma_start(o[name][b, WIN - NS:WIN, :], qkv[b * NS:(b + 1) * NS, TT - 1, off:off + KW]
                                    ).then_inc(kv_out, 16)
                e.wait_ge(kv_out, 16 * (4 + 2 * NB))

            @block.gpsimd
            def _(e):
                e.sem_inc(rows_c, 1)
                e.sem_inc(qk_t, 1)

                def rows_of(u, s, last):
                    e.wait_ge(qk_t, u)
                    e.tensor_copy(rows[:, s, :], qkv[:, ds(u, 1), 0:QW + KW].rearrange("p o f -> p (o f)")
                                  ).then_inc(rows_c, 1)

                rows_of(0, 0, False)
                with e.Fori(0, LAST // 2) as t:
                    rows_of(2 * t + 1, 1, False)
                    rows_of(2 * t + 2, 0, False)
                rows_of(NBLK - 1, 1, True)

            @block.tensor
            def _(e):
                def turn(u, s):
                    e.wait_ge(rows_c, u + 2)
                    for j in range(4):
                        e.transpose(psq[:, j, :], rows[:, s, j * P:(j + 1) * P], ident[:, :])
                    for g in range(NKV):
                        for d in range(2):
                            mm = e.matmul(psk[d * HD:(d + 1) * HD, g, :],
                                          rows[:, s, QW + g * HD:QW + (g + 1) * HD], ident[:, :],
                                          start=True, stop=True)
                    mm.then_inc(qk_t, 1)

                def block_of(u, s, last):
                    e.wait_ge(qk_c, 2 * (u + 1))
                    for g in range(NKV):
                        w = 2 * u + g
                        e.wait_ge(s_taken, w + 1)
                        for z in range(G):
                            h = 2 * (z % 2) + z // 2
                            q0 = (h % 2) * HD
                            lhsT = qT[q0:q0 + HD, (g * G + h) // 2, :]
                            e.matmul(pss[:, z, 0:WIN], lhsT, kT[q0:q0 + HD, 1 - s, g, :], start=True, stop=True)
                            mm = e.matmul(pss[:, z, WIN:2 * WIN], lhsT, kT[q0:q0 + HD, s, g, :],
                                          start=True, stop=True)
                        mm.then_inc(s_done, 1)
                    if not last:
                        e.wait_ge(a_c, u + 1)
                        turn(u + 1, 1 - s)
                    for g in range(NKV):
                        w = 2 * u + g
                        e.wait_ge(expd, (G + 1) * (w + 1))
                        e.wait_ge(o_taken, w + 1)
                        for n in range(NP):
                            e.wait_ge(p_c, NP * w + n + 1)
                            for q in range(4):
                                h, half = 2 * n + q // 2, q % 2
                                mm = e.transpose(pst[n % 2][:, q * P:(q + 1) * P],
                                                 pr[:, g, h, half * WIN:(half + 1) * WIN], ident[:, :])
                            mm.then_inc(p_t, 1)
                        e.wait_ge(p_c, NP * (w + 1) + 2)
                        for h in range(G):
                            n = h // 2
                            q = 2 * (h % 2)
                            v_at = slice(QW + KW + g * HD, QW + KW + (g + 1) * HD)
                            v_of = lambda block: self.qkv_padded[:, ds(block, 1), v_at].rearrange("p o f -> p (o f)")
                            e.matmul(pso[:, g, h, :], pT[:, 2 * g + n, q * P:(q + 1) * P], v_of(u),
                                     start=True, stop=False)
                            mm = e.matmul(pso[:, g, h, :], pT[:, 2 * g + n, (q + 1) * P:(q + 2) * P], v_of(u + 1),
                                          start=False, stop=True)
                        mm.then_inc(o_done, 1)
                    e.wait_ge(o_taken, 2 * (u + 1) + 1)
                    if not last:
                        e.wait_ge(qk_c, 2 * (u + 2))
                    for j in range(4):
                        mm = e.transpose(psq[:, j, :], att[:, j * P:(j + 1) * P], ident[:, :])
                    mm.then_inc(a_t, 1)

                e.sem_inc(a_c, 1)
                e.sem_inc(s_taken, 1)
                e.sem_inc(o_taken, 1)
                e.sem_inc(p_c, 2)
                e.wait_ge(kT_set, 1)
                turn(0, 0)
                blocks(e, block_of)

            @block.scalar
            def _(e):
                def turned(u, s):
                    e.wait_ge(qk_t, u + 2)
                    e.copy(qT[:], psq[:]).then_inc(qk_c, 1)
                    e.copy(kT[:, s, :, :], psk[:, 0:NKV, :]).then_inc(qk_c, 1)

                def block_of(u, s, last):
                    for g in range(NKV):
                        w = 2 * u + g
                        e.wait_ge(neg, w + 1)
                        for h in range(G):
                            e.activation(pr[:, g, h, :], sc[:, g, h, :], ACT.Exp, bias=nmx[:, g, h:h + 1],
                                         accum_out=den[:, g, h:h + 1]).then_inc(expd, 1)
                        e.activation(es[:, g, :], sx[:, g, :], ACT.Exp).then_inc(expd, 1)
                        if g == 0 and not last:
                            turned(u + 1, 1 - s)
                        for n in range(NP):
                            e.wait_ge(p_t, NP * w + n + 1)
                            e.copy(pT[:, 2 * g + n, :], pst[n % 2][:, :]).then_inc(p_c, 1)
                    e.wait_ge(a_t, u + 1)
                    e.copy(attT[:, :, ds(u * P, P)], psq[:]).then_inc(a_c, 1)

                e.wait_ge(kT_set, 1)
                turned(0, 0)
                blocks(e, block_of)
                e.wait_ge(a_c, NBLK + 1)

            @block.vector
            def _(e):
                def masked(u, s, g, mask):
                    w = 2 * u + g
                    ch = Chain(e, vstep, VS * u * 2 + g * (VS - 3))
                    e.wait_ge(s_done, w + 1)
                    ch(e.scalar_tensor_tensor(out=sc[:, g], in0=pss[:], scalar=SCALE,
                                              in1=mask[:].unsqueeze(1).to_broadcast([P, G, 2 * WIN]),
                                              op0=ALU.mult, op1=ALU.add))
                    ch.settle()
                    e.sem_inc(s_taken, 1)
                    ch(e.tensor_reduce(mx[:, g, :], sc[:, g], AX.X, ALU.max))
                    ch.settle()
                    ch(e.tensor_tensor(mx[:, g, :], mx[:, g, :], sink[:, g * G:(g + 1) * G], ALU.max))
                    ch.settle()
                    ch(e.tensor_scalar(nmx[:, g, :], mx[:, g, :], -1.0, None, ALU.mult))
                    ch(e.tensor_tensor(sx[:, g, :], sink[:, g * G:(g + 1) * G], mx[:, g, :], ALU.subtract))
                    ch.settle()
                    e.sem_inc(neg, 1)

                def weighted(u, s, g):
                    w = 2 * u + g
                    ch = Chain(e, vstep, VS * u * 2 + 2 * (VS - 3) + 3 * g)
                    e.wait_ge(expd, (G + 1) * (w + 1))
                    ch(e.tensor_tensor(den[:, g, :], den[:, g, :], es[:, g, :], ALU.add))
                    ch.settle()
                    ch(e.reciprocal(den[:, g, :], den[:, g, :]))
                    ch.settle()
                    e.wait_ge(o_done, w + 1)
                    e.wait_ge(a_c, u + 1)
                    ch(e.tensor_tensor(
                        att[:, g * G * HD:(g + 1) * G * HD].rearrange("p (b a d) -> p a b d", a=2, b=2),
                        pso[:, g, :, :].rearrange("p (a b) d -> p a b d", a=2),
                        den[:, g, :].rearrange("p (a b) -> p a b", a=2).unsqueeze(3).to_broadcast([P, 2, 2, HD]),
                        ALU.mult))
                    ch.settle()
                    e.sem_inc(o_taken, 1)

                def block_of(u, s, last, mask=band):
                    for g in range(NKV):
                        masked(u, s, g, mask)
                    for g in range(NKV):
                        weighted(u, s, g)

                e.memset(kT[:, 1, :, :], 0.0).then_inc(kT_set, 1)
                e.wait_ge(consts2, 48)
                block_of(0, 0, False, band1)
                block_of(1, 1, False)
                with e.Fori(1, LAST // 2) as t:
                    for s in range(2):
                        block_of(2 * t + s, s, False)
                for u in range(LAST, NBLK):
                    block_of(u, u % 2, u == NBLK - 1)
        self.attention_decode()

    def attention_decode(self):
        i = self.i
        qkv, attT, ident = self.qkv, self.attT, self.ident
        G = NQ // NKV
        NKC = NB * WIN
        with self.stage() as (c, block):
            ck = self.sb(c, "ck", [P, NB, KW])
            cv = self.sb(c, "cv", [P, NB, KW])
            mask = self.sb(c, "dmask", [P, T])
            sink = self.sb(c, "dsink", [P, NKV])
            kT = self.sb(c, "dkT", [P, T])
            qT = self.sb(c, "dqT", [P, NKV, P])
            sc = self.sb(c, "dsc", [P, T])
            pr = self.sb(c, "dpr", [P, T])
            pT = self.sb(c, "dpT", [P, TT, P])
            col = self.sb(c, "dcol", [P, 8])
            pss = self.ps(c, "dpss", [P, NC, 512])
            psa = self.ps(c, "dpsa", [P, 4, P])
            psb = self.ps(c, "dpsb", [P, 4, P])
            pso = self.ps(c, "dpso", [P, P])
            dk_in, kt, kc, qt, qc, sdone, vst, ex, ptt, ptc, od, oc = self.sems(
                "dk_in", "dkt", "dkc", "dqt", "dqc", "dsdone", "dvst", "dex", "dptt", "dptc", "dod", "doc")

            @block.sync
            def _(e):
                e.dma_start(ck[:], i["cache_k"].rearrange("b s f -> s b f")).then_inc(dk_in, 16)
                e.dma_start(cv[:], i["cache_v"].rearrange("b s f -> s b f")).then_inc(dk_in, 16)
                e.dma_start(mask[:], i["dmask"]).then_inc(dk_in, 16)
                e.dma_start(sink[:], i["dsink"]).then_inc(dk_in, 16)

            @block.tensor
            def _(e):
                e.wait_ge(dk_in, 64)
                for q in range(3):
                    ps = (psa, psb, psa)[q]
                    if q == 2:
                        e.wait_ge(kc, 1)
                        mm = e.transpose(ps[:, 0, 0:TS], qkv[0:TS, TT - 1, QW:QW + KW], ident[0:TS, 0:TS])
                    else:
                        for b in range(4):
                            mm = e.transpose(ps[:, b, :], ck[:, 4 * q + b, :], ident[:, :])
                    mm.then_inc(kt, 1)
                e.wait_ge(kc, 2)
                for g in range(NKV):
                    for h in range(G):
                        a = (g * G + h) * HD
                        mm = e.matmul(psb[g * HD:(g + 1) * HD, g, h * TS:(h + 1) * TS],
                                      qkv[0:TS, TT - 1, a:a + HD], ident[0:TS, 0:TS], start=True, stop=True)
                mm.then_inc(qt, 1)
                e.wait_ge(qc, 2)
                e.wait_ge(kc, 3)
                for g in range(NKV):
                    rows = slice(g * HD, (g + 1) * HD)
                    if g:
                        e.wait_ge(vst, 1)
                    for n in range(NC):
                        mm = e.matmul(pss[:, n, 0:CW], qT[rows, g, :], kT[rows, n * CW:(n + 1) * CW],
                                      start=True, stop=True)
                    mm.then_inc(sdone, 1)
                    e.wait_ge(vst, 7 * g + 7)
                    for q in range(3):
                        if q or g:
                            e.wait_ge(ptc, 3 * g + q)
                        ps = (psa, psb, psa)[q]
                        if q == 2:
                            mm = e.transpose(ps[0:TS, 0, :], pr[:, NKC:T], ident[:, :])
                        else:
                            for b in range(4):
                                mm = e.transpose(ps[:, b, :], pr[:, (4 * q + b) * P:(4 * q + b + 1) * P], ident[:, :])
                        mm.then_inc(ptt, 1)
                    e.wait_ge(ptc, 3 * g + 3)
                    if g:
                        e.wait_ge(oc, 4)
                    for b in range(NB):
                        e.matmul(pso[0:HD, :], cv[:, b, g * HD:(g + 1) * HD], pT[:, b, :], start=(b == 0), stop=False)
                    a = QW + KW + g * HD
                    e.matmul(pso[0:HD, :], qkv[0:TS, TT - 1, a:a + HD], pT[0:TS, NB, :], start=False, stop=True
                             ).then_inc(od, 1)

            @block.scalar
            def _(e):
                for q in range(3):
                    e.wait_ge(kt, q + 1)
                    ps = (psa, psb, psa)[q]
                    if q == 2:
                        e.copy(kT[:, NKC:T], ps[:, 0, 0:TS]).then_inc(kc, 1)
                    else:
                        e.copy(kT[:, q * 512:(q + 1) * 512], ps[:].rearrange("p a b -> p (a b)")).then_inc(kc, 1)
                e.wait_ge(qt, 1)
                for g in range(NKV):
                    rows = slice(g * HD, (g + 1) * HD)
                    e.copy(qT[rows, g, :], psb[rows, g, :]).then_inc(qc, 1)
                for g in range(NKV):
                    e.wait_ge(vst, 7 * g + 4)
                    e.activation(pr[:, :], sc[:, :], ACT.Exp, bias=col[:, 1:2], accum_out=col[:, 2:3]).then_inc(ex, 1)
                    e.activation(col[:, 3:4], sink[:, g:g + 1], ACT.Exp, bias=col[:, 1:2]).then_inc(ex, 1)
                    for q in range(3):
                        e.wait_ge(ptt, 3 * g + q + 1)
                        ps = (psa, psb, psa)[q]
                        if q == 2:
                            e.copy(pT[0:TS, NB, :], ps[0:TS, 0, :]).then_inc(ptc, 1)
                        else:
                            e.copy(pT[:, 4 * q:4 * q + 4, :], ps[:]).then_inc(ptc, 1)

            @block.vector
            def _(e):
                for g in range(NKV):
                    ch = Chain(e, vst, 7 * g)
                    e.wait_ge(sdone, g + 1)
                    e.wait_ge(ptt, 3 * g)
                    ch(e.scalar_tensor_tensor(out=sc[:].rearrange("p (n w) -> p n w", n=NC), in0=pss[:, :, 0:CW],
                                              scalar=SCALE, in1=mask[:].rearrange("p (n w) -> p n w", n=NC),
                                              op0=ALU.mult, op1=ALU.add))
                    ch.settle()
                    ch(e.tensor_reduce(col[:, 0:1], sc[:], AX.X, ALU.max))
                    ch.settle()
                    ch(e.tensor_tensor(col[:, 0:1], col[:, 0:1], sink[:, g:g + 1], ALU.max))
                    ch.settle()
                    ch(e.tensor_scalar(col[:, 1:2], col[:, 0:1], -1.0, None, ALU.mult))
                    e.wait_ge(ex, 2 * g + 2)
                    ch(e.tensor_tensor(col[:, 4:5], col[:, 2:3], col[:, 3:4], ALU.add))
                    ch.settle()
                    ch(e.reciprocal(col[:, 5:6], col[:, 4:5]))
                    ch.settle()
                    ch(e.tensor_scalar(pr[:, :], pr[:, :], col[:, 5:6], None, ALU.mult))
                    e.wait_ge(od, g + 1)
                    for h in range(G):
                        hh = g * G + h
                        e.tensor_copy(attT[(hh % 2) * HD:(hh % 2 + 1) * HD, hh // 2, TP:T],
                                      pso[0:HD, h * TS:(h + 1) * TS]).then_inc(oc, 1)
                e.wait_ge(oc, NQ)

    def rwkv(self):
        nc = self.nc
        with ExitStack() as c:
            self.dv = {n: self.sb(c, "dec_" + n, [P, NPAIR, TS]) for n in ("alpha", "beta", "kappa", "rho", "v")}
            self.dcum = self.sb(c, "dec_cum", [P, NPAIR, NB])
            self.lmask = self.sb(c, "level_masks", [P, LEVELS, P])
            self.low0 = self.sb(c, "low0", [P, P])
            self.before = self.sb(c, "before", [P, P])
            self.upto = self.sb(c, "upto", [P, 2, CH])
            with ExitStack() as c2:
                al, be, ka, rh, cu = (self.sb(c2, n, [P, T]) for n in ("alpha", "beta", "kappa", "rho", "cum"))
                self.al, self.be, self.ka, self.rh, self.cu = al, be, ka, rh, cu
                self.w2, self.a2 = self.sb(c2, "w2", [LW, P]), self.sb(c2, "a2", [LA, P])
                self.g2 = self.sb(c2, "g2", [LG, P])
                self.par = self.sb(c2, "pair_par", [P, 5])
                self.omka = self.sb(c2, "omka", [P, 1])
                self.work = self.sb(c2, "work", [P, WORK])
                self.banks = self.ps(c2, "banks", [P, 8, 512])
                self.lora_inputs()
                with nc.Fori(0, NPAIR) as j:
                    self.rwkv_elementwise(j)
                    self.rwkv_chunks(j)
            self.rwkv_decode()
        self.rwkv_out()

    def lora_inputs(self):
        i = self.i
        with self.stage() as (c, block):
            m_in, done = self.sems("m_in", "lora_done")

            @block.sync
            def _(e):
                e.dma_start(self.lmask[:], i["level_masks"]).then_inc(m_in, 16)
                e.dma_start(self.low0[:], i["low0"]).then_inc(m_in, 16)
                e.dma_start(self.before[:], i["before"]).then_inc(m_in, 16)
                e.dma_start(self.upto[:], i["upto"]).then_inc(m_in, 16)
                e.wait_ge(m_in, 64)

            @block.scalar
            def _(e):
                e.activation(self.lw[:], self.lw[:], ACT.Tanh).then_inc(done, 1)
                e.activation(self.lg[:], self.lg[:], ACT.Sigmoid).then_inc(done, 1)
                e.wait_ge(done, 2)

    def rwkv_elementwise(self, j):
        i = self.i
        al, be, ka, rh, cu = self.al, self.be, self.ka, self.rh, self.cu
        plane = lambda n: self.mixed[:, ds(j + n, 1), :].rearrange("p o t -> p (o t)")
        r, k, v = plane(0), plane(NPAIR), plane(2 * NPAIR)
        with self.stage() as (c, block):
            w2, a2, g2, par, omka = self.w2, self.a2, self.g2, self.par, self.omka
            carve = Carver(self.work)
            dec, a, kk, t0, t1, first = (carve(T) for _ in range(6))
            wg, gcol, gsig = carve(2, KT, P), carve(2, 2), carve(2, T)
            pg = self.banks[:, 2 * NC:2 * NC + 2, :]
            gw_in, = self.sems("gate_w_in")
            gb_in, gate_p, gate_s, gate_out = self.sems("gate_b_in", "gate_product", "gate_sigmoid", "gate_out")
            pa, pb = self.banks[:, 0:NC, :], self.banks[:, NC:2 * NC, :]
            par_in, pz, az, va, pv, vz, kk_set, sumsq, cum, pool_s, k_used, bonus = self.sems(
                "par_in2", "pz", "az", "va", "pv", "vz", "kk_set", "sum_squares", "c_set", "pool_steps", "k_used",
                "bonus")
            split = lambda x: x.rearrange("p (n w) -> p n w", n=NC)
            used = lambda p: p[:, :, 0:CW]
            starts = lambda x: (x[:, 0:TP].rearrange("p (n w) -> p n w", w=CH)[:, :, 0],
                                x[:, TP:T].rearrange("p (n w) -> p n w", w=NS)[:, :, 0])

            @block.sync
            def _(e):
                for a_, b_ in ((w2, "w2"), (a2, "a2"), (g2, "g2"), (par, "pair_par")):
                    e.dma_start(a_[:], i[b_][ds(j, 1)].rearrange("o p f -> (o p) f")).then_inc(par_in, 16)
                e.dma_start(wg[:], i["w_merge"][ds(2 * j, 2), :, KT:2 * KT, :].rearrange("t p k f -> p t k f")
                            ).then_inc(gw_in, 16)
                e.dma_start(gcol[:], i["b_gate"][:, ds(2 * j, 2), :]).then_inc(gb_in, 16)
                for z in range(2):
                    e.wait_ge(gate_s, NC * (z + 1))
                    e.dma_start(self.gate_d[ds(2 * j + z, 1)].rearrange("o p t -> (o p) t"), gsig[:, z, :]
                                ).then_inc(gate_out, 16)
                e.wait_ge(gate_out, 32)

            @block.tensor
            def _(e):
                def product(ps, lhsT, rhs):
                    for n in range(NC):
                        mm = e.matmul(ps[:, n, 0:CW], lhsT, rhs[:, n * CW:(n + 1) * CW], start=True, stop=True)
                    mm.then_inc(pz, 1)
                e.wait_ge(par_in, 64)
                product(pa, w2[:], self.lw[:])
                e.wait_ge(pv, 1)
                product(pb, self.headones[:], t0[:])
                e.wait_ge(az, 1)
                product(pa, a2[:], self.la[:])
                e.wait_ge(sumsq, 1)
                product(pb, g2[:], self.lg[:])
                e.wait_ge(gw_in, 16)
                for z in range(2):
                    if z:
                        e.wait_ge(az, 4)
                        e.wait_ge(bonus, 1)
                        product(pa, self.headones[:], t1[:])
                    for n in range(NC):
                        part = z * NC + n
                        if part >= 2:
                            e.wait_ge(gate_s, part - 1)
                        for k_ in range(KT):
                            mm = e.matmul(pg[:, part % 2, 0:CW], wg[:, z, k_, :],
                                          self.hT[:, k_, n * CW:(n + 1) * CW], start=(k_ == 0), stop=(k_ == KT - 1))
                        mm.then_inc(gate_p, 1)

            @block.scalar
            def _(e):
                e.wait_ge(pz, 1)
                e.activation(split(dec[:]), used(pa), ACT.Sigmoid, bias=par[:, 0:1]).then_inc(az, 1)
                e.wait_ge(az, 1)
                e.activation(dec[:], dec[:], ACT.Exp, scale=-float(np.exp(-0.5))).then_inc(az, 1)
                e.wait_ge(sumsq, 1)
                e.activation(t0[:], t0[:], ACT.Sqrt).then_inc(az, 1)
                e.wait_ge(pz, 3)
                e.activation(split(a[:]), used(pa), ACT.Sigmoid, bias=par[:, 1:2]).then_inc(az, 1)
                e.wait_ge(gb_in, 16)
                for part in range(2 * NC):
                    z, n = part // NC, part % NC
                    e.wait_ge(gate_p, part + 1)
                    e.activation(gsig[:, z, n * CW:(n + 1) * CW], pg[:, part % 2, 0:CW], ACT.Sigmoid,
                                 bias=gcol[:, z, 1:2]).then_inc(gate_s, 1)
                e.wait_ge(pz, 4)
                e.wait_ge(k_used, 1)
                e.copy(split(k), used(pb)).then_inc(az, 1)

            @block.gpsimd
            def _(e):
                e.wait_ge(kk_set, 1)
                e.tensor_tensor(t0[:], kk[:], kk[:], ALU.mult).then_inc(pv, 1)
                ch = Chain(e, pool_s)
                e.wait_ge(cum, 1)
                ch(e.tensor_copy(dec[:, 1:T], cu[:, 0:T - 1]))
                ch.settle()
                for x in starts(dec[:]):
                    ch(e.memset(x, 1.0))
                ch(e.tensor_tensor(rh[:], cu[:], r, ALU.mult))
                e.wait_ge(az, 4)
                ch(e.tensor_scalar(t1[:], a[:], par[:, 3:4], omka[:, 0:1], ALU.mult, ALU.add))
                ch.settle()
                e.tensor_tensor(ka[:], t1[:], k, ALU.mult).then_inc(k_used, 1)
                e.wait_ge(k_used, 1)
                ch(e.tensor_tensor(t1[:], ka[:], r, ALU.mult))
                ch.settle()
                e.tensor_scalar(t1[:], t1[:], par[:, 4:5], None, ALU.mult).then_inc(bonus, 1)

            @block.vector
            def _(e):
                ch = Chain(e, va)
                e.memset(first[:], 0.0).then_inc(vz, 1)
                e.wait_ge(par_in, 64)
                ch(e.tensor_scalar(omka[:], par[:, 3:4], -1.0, 1.0, ALU.mult, ALU.add))
                ch.settle()
                e.tensor_scalar(kk[:], k, par[:, 2:3], None, ALU.mult).then_inc(kk_set, 1)
                e.wait_ge(pz, 2)
                e.tensor_scalar(split(t0[:]), used(pb), 1e-24, None, ALU.max).then_inc(sumsq, 1)
                e.wait_ge(az, 2)
                e.wait_ge(vz, 1)
                for x, y in zip(starts(first[:]), starts(dec[:])):
                    ch(e.tensor_copy(x, y))
                ch.settle()
                for x in starts(dec[:]):
                    ch(e.memset(x, 0.0))
                ch.settle()
                e.tensor_tensor_scan(cu[:], dec[:], first[:], 0.0, ALU.mult, ALU.add).then_inc(cum, 1)
                e.wait_ge(az, 3)
                ch(e.reciprocal(t0[:], t0[:]))
                ch.settle()
                ch(e.tensor_tensor(kk[:], kk[:], t0[:], ALU.mult))
                e.wait_ge(cum, 1)
                ch(e.reciprocal(be[:], cu[:]))
                ch.settle()
                e.wait_ge(bonus, 1)
                ch(e.tensor_tensor(ka[:], ka[:], be[:], ALU.mult))
                ch(e.tensor_tensor(al[:], dec[:], kk[:], ALU.mult))
                ch(e.tensor_tensor(a[:], a[:], kk[:], ALU.mult))
                ch.settle()
                ch(e.tensor_tensor(be[:], be[:], a[:], ALU.mult))
                e.wait_ge(pz, 5)
                ch(e.tensor_tensor(split(r), used(pa), split(v), ALU.mult))
                ch.settle()
                for n, x in (("alpha", al), ("beta", be), ("kappa", ka), ("rho", rh)):
                    ch(e.tensor_copy(self.dv[n][:, ds(j, 1), :].rearrange("p o t -> p (o t)"), x[:, TP:T]))
                ch(e.tensor_copy(self.dv["v"][:, ds(j, 1), :].rearrange("p o t -> p (o t)"), v[:, TP:T]))
                ch(e.tensor_copy(self.dcum[:, ds(j, 1), :].rearrange("p o t -> p (o t)"),
                                 cu[:, TP:T].rearrange("p (b n) -> p b n", n=NS)[:, :, NS - 1]))
                ch.settle()

    def rwkv_chunks(self, j):
        o = self.o
        ident = self.ident
        v = self.mixed[:, ds(j + 2 * NPAIR, 1), :].rearrange("p o t -> p (o t)")
        L = LANES
        H2 = L // 2
        with self.stage() as (c, block):
            carve = Carver(self.work)
            big = lambda: carve(L, P)
            ab, bb, kb, vb = (big() for _ in range(4))
            cq = carve(2, L)
            araw = big()
            alv = carve(LEVELS - 1, L, P)
            XY = [big(), big()]
            Pm = [carve(H2, P), carve(H2, P)]
            bt = big()
            brk = [carve(L, 2, CH), carve(L, 2, CH)]
            at = big()
            bT, kT, vT, wv, apt = ([big(), big()] for _ in range(5))
            r1 = big()
            st, sc, nsa = carve(2, P), carve(2, P), carve(2, P)
            b = [self.banks[:, n, :].rearrange("p (l w) -> p l w", l=L) for n in range(8)]
            b_p = (b[0], b[3])
            b_xy = (b[1], b[2])
            b_y = self.banks[:, 7, 0:L * CH]
            b_u = self.banks[:, 7, L * CH:].rearrange("p (s w) -> p s w", s=2)
            names = ("built", "cq_set", "gram", "tposed", "araw_c", "t_c", "lvl", "g_v", "xy0", "r1_d", "r1_c", "wa_d",
                     "wa_c", "sa_d", "nsa_v", "u_d", "sc_c", "st_v", "y_c", "wkv_out")
            (built, cq_set, gram, tposed, araw_c, t_c, lvl, g_v, xy0, r1_d, r1_c, wa_d, wa_c, sa_d, nsa_v, u_d, sc_c,
             st_v, y_c, out_s) = self.sems(*names)
            p_d, p_c, xy_d, xy_v = (self.sems(n + "0", n + "1") for n in ("p_d", "p_c", "xy_d", "xy_v"))
            NL = LEVELS - 1
            MASKED = 4
            bc = lambda m: m.unsqueeze(1).to_broadcast([P, L, P])
            cols = lambda q, l=0, n=L: slice((q * L + l) * CH, (q * L + l + n) * CH)
            rho = lambda q, l: self.rh[:, cols(q, l, 1)]
            x_of = lambda l: XY[l // H2][:, l % H2, :]
            y_of = lambda l: XY[l // H2][:, H2 + l % H2, :]

            @block.gpsimd
            def _(e):
                def build(q):
                    if q:
                        e.wait_ge(tposed, 4 * q)
                    for src, dst in ((self.al[:], ab), (self.be[:], bb), (self.ka[:], kb), (v, vb)):
                        for h in range(2):
                            mine = self.headones[:, h * HD:(h + 1) * HD].unsqueeze(1).to_broadcast([P, L, CH])
                            e.tensor_tensor(dst[:, :, h * CH:(h + 1) * CH],
                                            src[:, cols(q)].rearrange("p (l w) -> p l w", l=L),
                                            mine, ALU.mult).then_inc(built, 1)
                    if q >= 2:
                        e.wait_ge(y_c, q - 1)
                    e.tensor_copy(cq[:, q % 2, :], self.cu[:, cols(q)].rearrange("p (l w) -> p l w", l=L)[:, :, CH - 1]
                                  ).then_inc(cq_set, 1)

                build(0)
                for q in range(NQUAD):
                    e.wait_ge(araw_c, q + 1)
                    for n in range(NL):
                        e.tensor_tensor(alv[:, n, :, :], araw[:], bc(self.lmask[:, n + 1, :]), ALU.mult
                                        ).then_inc(lvl, 1)
                    if q + 1 < NQUAD:
                        build(q + 1)

            @block.tensor
            def _(e):
                def step_sa(q, l):
                    if l == 0:
                        e.wait_ge(wa_c, 2 * (q + 1))
                    e.wait_ge(st_v, L * q + l + 1)
                    e.matmul(b[6][:, l, :], apt[q % 2][:, l, :], st[:, l % 2, :], start=True, stop=True
                             ).then_inc(sa_d, 1)

                def step_out(q, l):
                    s, z = l % 2, q % 2
                    if l == 0 and q:
                        e.wait_ge(y_c, q)
                    e.wait_ge(nsa_v, L * q + l + 1)
                    y = b_y[:, l * CH:(l + 1) * CH]
                    e.matmul(b_u[:, s, :], kT[z][:, l, :], vT[z][:, l, :], start=True, stop=False)
                    e.matmul(b_u[:, s, :], bT[z][:, l, :], nsa[:, s, :], start=False, stop=True)
                    e.matmul(y, st[:, s, :], rho(q, l), start=True, stop=False)
                    e.matmul(y, vT[z][:, l, :], brk[z][:, l, 1, :], start=False, stop=False)
                    e.matmul(y, nsa[:, s, :], brk[z][:, l, 0, :], start=False, stop=True).then_inc(u_d, 1)

                def prepare(q, steps):
                    e.wait_ge(built, 8 * (q + 1))
                    for l in range(L):
                        e.matmul(b[0][:, l, :], bb[:, l, :], ab[:, l, :], start=True, stop=True)
                    for l in range(L):
                        mm = e.matmul(b[1][:, l, :], ab[:, l, :], bb[:, l, :], start=True, stop=True)
                    mm.then_inc(gram, 1)
                    for l in range(L):
                        e.matmul(b[2][:, l, :], kb[:, l, :], ab[:, l, :], start=True, stop=True)
                    for l in range(L):
                        e.matmul(b[3][:, l, 0:CH], bb[:, l, :], rho(q, l), start=True, stop=True)
                        mm = e.matmul(b[3][:, l, CH:P], kb[:, l, :], rho(q, l), start=True, stop=True)
                    mm.then_inc(gram, 1)
                    if steps:
                        step_sa(q - 1, 0)
                    for n, m in enumerate((ab, bb, kb, vb)):
                        if n >= 2:
                            e.wait_ge(t_c, 4 * q + n - 1)
                        if n == 2 and steps:
                            step_out(q - 1, 0)
                        for l in range(L):
                            mm = e.transpose(b[4 + n % 2][:, l, :], m[:, l, :], ident[:])
                        mm.then_inc(tposed, 1)
                    for n in range(NL):
                        e.wait_ge(lvl, NL * q + n + 1)
                        if n == 0:
                            e.wait_ge(g_v, MASKED * (q + 1))
                        for h in range(2):
                            if n:
                                e.wait_ge(xy_v[h], NL * q + n)
                            for l in range(H2 * h, H2 * (h + 1)):
                                mm = e.matmul(b_p[h][:, l % H2, :], alv[:, n, l, :], x_of(l), start=True, stop=True)
                            mm.then_inc(p_d[h], 1)
                        if steps and n + 1 < L:
                            step_sa(q - 1, n + 1)
                        for h in range(2):
                            e.wait_ge(p_c[h], NL * q + n + 1)
                            for l in range(H2 * h, H2 * (h + 1)):
                                p_ = Pm[h][:, l % H2, :]
                                if n + 1 < NL:
                                    e.matmul(b_xy[h][:, l % H2, :], y_of(l), p_, start=True, stop=True)
                                mm = e.matmul(b_xy[h][:, H2 + l % H2, :], p_, y_of(l), start=True, stop=True)
                            mm.then_inc(xy_d[h], 1)
                        if steps and n + 1 < L:
                            step_out(q - 1, n + 1)
                    e.wait_ge(t_c, 4 * (q + 1))
                    for l in range(L):
                        mm = e.matmul(b[3][:, l, :], bt[:, l, :], vT[q % 2][:, l, :], start=True, stop=True)
                    mm.then_inc(r1_d, 1)
                    for h in range(2):
                        e.wait_ge(xy_v[h], NL * (q + 1))
                        for l in range(H2 * h, H2 * (h + 1)):
                            mm = e.matmul(b[5][:, l, :], at[:, l, :], y_of(l), start=True, stop=True)
                    mm.then_inc(wa_d, 1)
                    e.wait_ge(r1_c, q + 1)
                    for l in range(L):
                        mm = e.matmul(b[4][:, l, :], y_of(l), r1[:, l, :], start=True, stop=True)
                    mm.then_inc(wa_d, 1)

                for q in range(NQUAD):
                    prepare(q, steps=q > 0)
                for l in range(L):
                    step_sa(NQUAD - 1, l)
                    step_out(NQUAD - 1, l)

            @block.scalar
            def _(e):
                def step_decay(q, l):
                    if l == 0:
                        e.wait_ge(cq_set, q + 1)
                    e.wait_ge(st_v, L * q + l + 1)
                    e.mul(sc[:, l % 2, :], st[:, l % 2, :], cq[:, q % 2, l:l + 1]).then_inc(sc_c, 1)

                def outputs(q):
                    e.wait_ge(u_d, L * (q + 1))
                    e.wait_ge(st_v, L * (q + 1) + 1)
                    e.copy(v[:, cols(q)], b_y).then_inc(y_c, 1)

                def prepare(q, steps):
                    e.wait_ge(gram, 2 * q + 1)
                    e.copy(araw[:], b[0][:]).then_inc(araw_c, 1)
                    if steps:
                        step_decay(q - 1, 0)
                    for n, m in enumerate((at, bT[q % 2], kT[q % 2], vT[q % 2])):
                        e.wait_ge(tposed, 4 * q + n + 1)
                        e.copy(m[:], b[4 + n % 2][:]).then_inc(t_c, 1)
                    for n in range(NL):
                        for h in range(2):
                            e.wait_ge(p_d[h], NL * q + n + 1)
                            e.copy(Pm[h][:], b_p[h][:, 0:H2, :]).then_inc(p_c[h], 1)
                        if steps and n + 1 < L:
                            step_decay(q - 1, n + 1)
                        if steps and n + 1 == L:
                            outputs(q - 1)
                    e.wait_ge(r1_d, q + 1)
                    e.copy(r1[:], b[3][:]).then_inc(r1_c, 1)
                    e.wait_ge(wa_d, 2 * q + 1)
                    e.copy(apt[q % 2][:], b[5][:]).then_inc(wa_c, 1)
                    e.wait_ge(wa_d, 2 * q + 2)
                    e.copy(wv[q % 2][:], b[4][:]).then_inc(wa_c, 1)

                for q in range(NQUAD):
                    prepare(q, steps=q > 0)
                for l in range(L):
                    step_decay(NQUAD - 1, l)
                outputs(NQUAD - 1)

            @block.vector
            def _(e):
                def step_sa(q, l):
                    e.wait_ge(sa_d, L * q + l + 1)
                    e.scalar_tensor_tensor(out=nsa[:, l % 2, :], in0=b[6][:, l, :], scalar=-1.0,
                                           in1=wv[q % 2][:, l, :], op0=ALU.mult, op1=ALU.subtract).then_inc(nsa_v, 1)

                def step_state(q, l):
                    s = l % 2
                    e.wait_ge(u_d, L * q + l + 1)
                    e.wait_ge(sc_c, L * q + l + 1)
                    e.scalar_tensor_tensor(out=st[:, 1 - s, :], in0=b_u[:, s, :], scalar=cq[:, q % 2, l:l + 1],
                                           in1=sc[:, s, :], op0=ALU.mult, op1=ALU.add).then_inc(st_v, 1)

                def prepare(q, steps):
                    ch = Chain(e, g_v, MASKED * q)
                    e.wait_ge(gram, 2 * q + 1)
                    for h in range(2):
                        lanes = slice(H2 * h, H2 * (h + 1))
                        e.tensor_tensor(XY[h][:, 0:H2, :], b[1][:, lanes, :],
                                        self.low0[:].unsqueeze(1).to_broadcast([P, H2, P]), ALU.mult
                                        ).then_inc(xy0, 1)
                    e.wait_ge(araw_c, q + 1)
                    for h in range(2):
                        lanes = slice(H2 * h, H2 * (h + 1))
                        e.tensor_tensor(XY[h][:, H2:L, :], araw[:, lanes, :],
                                        self.lmask[:, 0, :].unsqueeze(1).to_broadcast([P, H2, P]), ALU.mult
                                        ).then_inc(xy0, 1)
                    e.wait_ge(xy0, 4 * (q + 1))
                    for h in range(2):
                        ch(e.tensor_tensor(XY[h][:], bc(ident[:]), XY[h][:], ALU.subtract))
                    if steps:
                        step_sa(q - 1, 0)
                    e.wait_ge(gram, 2 * q + 2)
                    ch(e.tensor_tensor(bt[:], b[2][:], bc(self.before[:]), ALU.mult))
                    ch(e.tensor_tensor(brk[q % 2][:], b[3][:].rearrange("p l (a w) -> p l a w", a=2),
                                       self.upto[:].unsqueeze(1).to_broadcast([P, L, 2, CH]), ALU.mult))
                    assert ch.n == MASKED
                    if steps:
                        step_state(q - 1, 0)
                    for n in range(NL):
                        if steps and n + 1 < L:
                            step_sa(q - 1, n + 1)
                        for h in range(2):
                            e.wait_ge(xy_d[h], NL * q + n + 1)
                            part = slice(0 if n + 1 < NL else H2, L)
                            e.tensor_tensor(XY[h][:, part, :], XY[h][:, part, :], b_xy[h][:, part, :], ALU.subtract
                                            ).then_inc(xy_v[h], 1)
                        if steps and n + 1 < L:
                            step_state(q - 1, n + 1)

                e.memset(st[:, 0, :], 0.0).then_inc(st_v, 1)
                for q in range(NQUAD):
                    prepare(q, steps=q > 0)
                for l in range(L):
                    step_sa(NQUAD - 1, l)
                    step_state(NQUAD - 1, l)
                e.wait_ge(st_v, TP // CH + 1)

            @block.sync
            def _(e):
                e.wait_ge(st_v, TP // CH + 1)
                for h in range(2):
                    rows = slice(h * HD, (h + 1) * HD)
                    e.dma_start(o["prompt_wkv"][ds(2 * j + h, 1)].rearrange("o a b -> (o a) b"), st[rows, 0, rows]
                                ).then_inc(out_s, 16)
                e.wait_ge(out_s, 32)

    def rwkv_decode(self):
        i, o = self.i, self.o
        ident, dv = self.ident, self.dv
        L, Q = NPAIR, 2 * TS
        with self.stage() as (c, block):
            sb = lambda n, *s: self.sb(c, "d_" + n, list(s))
            st0 = sb("state", P, L, NB, P)
            st1 = sb("state_new", P, L, NB, P)
            bd = [sb(f"bd{n}", P, L, 2, TS) for n in range(5)]
            tm = [sb(f"tm{n}", Q, L, P) for n in range(5)]
            mk = sb("masks", Q, 4, Q)
            mu = sb("upto", Q, 2, TS)
            own = sb("own", Q, NB)
            X, Y, Pm, a1, bt = (sb(n, Q, L, Q) for n in ("x", "y", "p", "a1", "bt"))
            yst = sb("yst", Q, L, TS)
            brk = sb("brk", Q, L, 2, TS)
            r1 = sb("r1", Q, L, P)
            apt = sb("apt", P, L, TS)
            vn = sb("vn", Q, 2, 2, NB, P)
            sums = sb("sums", P, 2, 4, P)
            b = [self.ps(c, f"db{n}", [P, 512]) for n in range(8)]
            d_in, bdp, gram, araw, g_v, p_d, p_c, y_d, y_v, r1_d, r1_c, ap_d, ap_c, sa_d, sa_c, bdn, nt_d, nt_c, y_f, \
                y_fc, vnp, u_d, u_v, u_c, out_s = self.sems(*[f"dec{n}" for n in range(25)])
            q4 = lambda m, rows, w: m[0:rows, 0:L * w].rearrange("p (l w) -> p l w", l=L)

            @block.sync
            def _(e):
                e.dma_start(mk[:], i["dec_masks"]).then_inc(d_in, 16)
                e.dma_start(mu[:], i["dec_upto"]).then_inc(d_in, 16)
                e.dma_start(own[:], i["dec_own"]).then_inc(d_in, 16)
                e.dma_start(st0[:], i["state0"]).then_inc(d_in, 16)
                e.wait_ge(u_c, 2 * L)
                for h in range(2):
                    rows = slice(h * HD, (h + 1) * HD)
                    for l in range(L):
                        e.dma_start(o["sample_wkv"][:, 2 * l + h].rearrange("b j i -> j b i"), st1[rows, l, :, rows]
                                    ).then_inc(out_s, 16)
                e.wait_ge(out_s, 32 * L)

            @block.gpsimd
            def _(e):
                for n, name in enumerate(("alpha", "beta", "kappa", "v")):
                    for h in range(2):
                        e.tensor_scalar(bd[n][:, :, h, :], dv[name][:], self.headones[:, h * HD:h * HD + 1], None,
                                        ALU.mult).then_inc(bdp, 1)
                e.wait_ge(nt_c, 1)
                e.wait_ge(d_in, 64)
                for l in range(L):
                    if l >= 2:
                        e.wait_ge(u_d, 2 * (l - 1))
                    for n, m in enumerate((tm[3], tm[4])):
                        e.tensor_tensor(vn[:, l % 2, n, :, :], m[:, l, :].unsqueeze(1).to_broadcast([Q, NB, P]),
                                        own[:].unsqueeze(2).to_broadcast([Q, NB, P]), ALU.mult).then_inc(vnp, 1)

            @block.tensor
            def _(e):
                e.wait_ge(bdp, 8)
                f = lambda m, l: m[:, l, :, :].rearrange("p a b -> p (a b)")
                for k, (x, y) in enumerate(((1, 0), (0, 1), (2, 0))):
                    for l in range(L):
                        mm = e.matmul(q4(b[k], Q, Q)[:, l, :], f(bd[x], l), f(bd[y], l), start=True, stop=True)
                    mm.then_inc(gram, 1)
                for l in range(L):
                    for n in range(2):
                        mm = e.matmul(q4(b[3], Q, Q)[:, l, n * TS:(n + 1) * TS], f(bd[1 + n], l), dv["rho"][:, l, :],
                                      start=True, stop=True)
                mm.then_inc(gram, 1)
                for n in range(4):
                    for l in range(L):
                        mm = e.transpose(q4(b[4 + n], Q, P)[:, l, :], f(bd[n], l), ident[:])
                    mm.then_inc(gram, 1)
                e.wait_ge(g_v, 7)
                for l in range(L):
                    mm = e.matmul(q4(b[0], Q, Q)[:, l, :], a1[:, l, :], X[:, l, :], start=True, stop=True)
                mm.then_inc(p_d, 1)
                e.wait_ge(p_c, 1)
                for l in range(L):
                    mm = e.matmul(q4(b[1], Q, Q)[:, l, :], Pm[:, l, :], Y[:, l, :], start=True, stop=True)
                mm.then_inc(y_d, 1)
                e.wait_ge(r1_c, 4)
                for l in range(L):
                    mm = e.matmul(q4(b[2], Q, P)[:, l, :], bt[:, l, :], tm[3][:, l, :], start=True, stop=True)
                mm.then_inc(r1_d, 1)
                e.wait_ge(y_v, 2)
                for l in range(L):
                    mm = e.matmul(q4(b[3], P, TS)[:, l, :], tm[0][:, l, :], yst[:, l, :], start=True, stop=True)
                mm.then_inc(ap_d, 1)
                e.wait_ge(ap_c, 1)
                e.wait_ge(r1_c, 5)
                e.wait_ge(d_in, 64)
                for l in range(L):
                    y = q4(b[4], P, TS)[:, l, :]
                    for k in range(NB):
                        e.matmul(y[:, k * NS:(k + 1) * NS], st0[:, l, k, :], apt[:, l, k * NS:(k + 1) * NS],
                                 start=(k == 0), stop=False)
                    mm = e.matmul(y, r1[:, l, :], yst[:, l, :], start=False, stop=True)
                mm.then_inc(sa_d, 1)
                e.wait_ge(bdn, 2)
                for l in range(L):
                    mm = e.transpose(q4(b[5], Q, P)[:, l, :], f(bd[4], l), ident[:])
                mm.then_inc(nt_d, 1)
                e.wait_ge(nt_c, 1)
                for l in range(L):
                    y = q4(b[6], P, TS)[:, l, :]
                    for k in range(NB):
                        e.matmul(y[:, k * NS:(k + 1) * NS], st0[:, l, k, :], dv["rho"][:, l, k * NS:(k + 1) * NS],
                                 start=(k == 0), stop=False)
                    e.matmul(y, tm[3][:, l, :], brk[:, l, 1, :], start=False, stop=False)
                    mm = e.matmul(y, tm[4][:, l, :], brk[:, l, 0, :], start=False, stop=True)
                mm.then_inc(y_f, 1)
                for l in range(L):
                    e.wait_ge(vnp, 2 * (l + 1))
                    for half in range(2):
                        n = 2 * l + half
                        if n >= 4:
                            e.wait_ge(u_v, n - 3)
                        for k in range(4):
                            u = q4(b[n % 4], P, P)[:, k, :]
                            e.matmul(u, tm[2][:, l, :], vn[:, l % 2, 0, 4 * half + k, :], start=True, stop=False)
                            mm = e.matmul(u, tm[1][:, l, :], vn[:, l % 2, 1, 4 * half + k, :], start=False, stop=True)
                        mm.then_inc(u_d, 1)

            @block.scalar
            def _(e):
                for n in range(4):
                    e.wait_ge(gram, 5 + n)
                    e.copy(tm[n][:], q4(b[4 + n], Q, P)).then_inc(r1_c, 1)
                e.wait_ge(p_d, 1)
                e.copy(Pm[:], q4(b[0], Q, Q)).then_inc(p_c, 1)
                e.wait_ge(r1_d, 1)
                e.copy(r1[:], q4(b[2], Q, P)).then_inc(r1_c, 1)
                e.wait_ge(ap_d, 1)
                e.copy(apt[:], q4(b[3], P, TS)).then_inc(ap_c, 1)
                e.wait_ge(nt_d, 1)
                e.copy(tm[4][:], q4(b[5], Q, P)).then_inc(nt_c, 1)
                e.wait_ge(y_f, 1)
                e.copy(self.mixed[:, 2 * NPAIR:3 * NPAIR, TP:T], q4(b[6], P, TS)).then_inc(y_fc, 1)
                for n in range(2 * L):
                    l, half = n // 2, n % 2
                    e.wait_ge(u_v, n + 1)
                    for k in range(4):
                        mm = e.mul(st1[:, l, 4 * half + k, :], sums[:, half, k, :],
                                   self.dcum[:, l, 4 * half + k:4 * half + k + 1])
                    mm.then_inc(u_c, 1)
                e.wait_ge(y_fc, 1)

            @block.vector
            def _(e):
                m = lambda k: mk[:, k, :].unsqueeze(1).to_broadcast([Q, L, Q])
                eye = ident[0:Q, 0:Q].unsqueeze(1).to_broadcast([Q, L, Q])
                e.wait_ge(d_in, 64)
                ch = Chain(e, g_v)
                e.wait_ge(gram, 1)
                ch(e.tensor_tensor(Y[:], q4(b[0], Q, Q), m(1), ALU.mult))
                ch(e.tensor_tensor(a1[:], q4(b[0], Q, Q), m(2), ALU.mult))
                e.wait_ge(gram, 2)
                ch(e.tensor_tensor(X[:], q4(b[1], Q, Q), m(3), ALU.mult))
                ch.settle()
                ch(e.tensor_tensor(Y[:], eye, Y[:], ALU.subtract))
                ch(e.tensor_tensor(X[:], eye, X[:], ALU.subtract))
                e.wait_ge(gram, 3)
                ch(e.tensor_tensor(bt[:], q4(b[2], Q, Q), m(0), ALU.mult))
                e.wait_ge(gram, 4)
                ch(e.tensor_tensor(brk[:], q4(b[3], Q, Q).rearrange("p l (a w) -> p l a w", a=2),
                                   mu[:].unsqueeze(1).to_broadcast([Q, L, 2, TS]), ALU.mult))
                e.wait_ge(y_d, 1)
                e.tensor_tensor(Y[:], Y[:], q4(b[1], Q, Q), ALU.subtract).then_inc(y_v, 1)
                e.wait_ge(y_v, 1)
                e.tensor_tensor(yst[:], Y[:, :, 0:TS], Y[:, :, TS:Q], ALU.add).then_inc(y_v, 1)
                e.wait_ge(sa_d, 1)
                e.tensor_scalar(bd[4][:, :, 0, :], q4(b[4], P, TS), self.headones[:, 0:1], -1.0, ALU.mult, ALU.mult
                                ).then_inc(bdn, 1)
                e.tensor_scalar(bd[4][:, :, 1, :], q4(b[4], P, TS), self.headones[:, HD:HD + 1], -1.0, ALU.mult,
                                ALU.mult).then_inc(bdn, 1)
                for n in range(2 * L):
                    l, half = n // 2, n % 2
                    e.wait_ge(u_d, n + 1)
                    if n >= 2:
                        e.wait_ge(u_c, n - 1)
                    e.tensor_tensor(sums[:, half, :, :], st0[:, l, 4 * half:4 * half + 4, :], q4(b[n % 4], P, P),
                                    ALU.add).then_inc(u_v, 1)

    def rwkv_out(self):
        i = self.i
        with self.stage() as (c, block):
            par = self.sb(c, "gn_par", [P, 2, NPAIR])
            epsc = self.sb(c, "gn_eps", [P, 1])
            yc = self.sb(c, "gn_yc", [P, 2, T])
            sq = self.sb(c, "gn_sq", [P, 2, T])
            rs = self.sb(c, "gn_rs", [P, 2, T])
            pm = self.ps(c, "gn_mean", [P, NC, 512])
            pv = self.ps(c, "gn_var", [P, NC, 512])
            par_in, eps_set, mean_d, cen, sqd, var_d, root, vst = self.sems(
                "gn_par_in", "gn_eps_set", "mean_d", "centred", "squared", "var_d", "gn_root", "gn_v")
            gated, = self.sems("gn_gated")
            split = lambda x: x.rearrange("p (n w) -> p n w", n=NC)
            V = 3

            @block.sync
            def _(e):
                e.dma_start(par[:], i["gn_par"]).then_inc(par_in, 16)

            @block.tensor
            def _(e):
                def mean(j):
                    if j:
                        e.wait_ge(cen, j)
                    for n in range(NC):
                        mm = e.matmul(pm[:, n, 0:CW], self.headones[:],
                                      self.mixed[:, 2 * NPAIR + j, n * CW:(n + 1) * CW], start=True, stop=True)
                    mm.then_inc(mean_d, 1)

                mean(0)
                for j in range(NPAIR):
                    if j + 1 < NPAIR:
                        mean(j + 1)
                    e.wait_ge(sqd, j + 1)
                    if j:
                        e.wait_ge(root, j)
                    for n in range(NC):
                        mm = e.matmul(pv[:, n, 0:CW], self.headones[:], sq[:, j % 2, n * CW:(n + 1) * CW],
                                      start=True, stop=True)
                    mm.then_inc(var_d, 1)

            @block.scalar
            def _(e):
                e.wait_ge(eps_set, 1)
                for j in range(NPAIR):
                    e.wait_ge(cen, j + 1)
                    e.activation(sq[:, j % 2, :], yc[:, j % 2, :], ACT.Square).then_inc(sqd, 1)
                    e.wait_ge(var_d, j + 1)
                    if j >= 2:
                        e.wait_ge(vst, V * (j - 1))
                    e.activation(split(rs[:, j % 2, :]), pv[:, :, 0:CW], ACT.Sqrt, bias=epsc[:], scale=1.0 / HD
                                 ).then_inc(root, 1)

            @block.vector
            def _(e):
                def centre(j):
                    e.wait_ge(mean_d, j + 1)
                    if j >= 2:
                        e.wait_ge(gated, 2 * (j - 1))
                    e.scalar_tensor_tensor(out=split(yc[:, j % 2, :]), in0=pm[:, :, 0:CW], scalar=-1.0 / HD,
                                           in1=split(self.mixed[:, 2 * NPAIR + j, :]), op0=ALU.mult, op1=ALU.add
                                           ).then_inc(cen, 1)

                e.memset(epsc[:], GN_EPS).then_inc(eps_set, 1)
                e.wait_ge(par_in, 16)
                centre(0)
                for j in range(NPAIR):
                    if j + 1 < NPAIR:
                        centre(j + 1)
                    ch = Chain(e, vst, V * j)
                    s = j % 2
                    e.wait_ge(root, j + 1)
                    ch(e.reciprocal(rs[:, s, :], rs[:, s, :]))
                    ch.settle()
                    ch(e.tensor_tensor(yc[:, s, :], yc[:, s, :], rs[:, s, :], ALU.mult))
                    ch.settle()
                    ch(e.tensor_scalar(yc[:, s, :], yc[:, s, :], par[:, 0, j:j + 1], par[:, 1, j:j + 1],
                                       ALU.mult, ALU.add))
                    assert ch.n == V

            @block.gpsimd
            def _(e):
                for j in range(NPAIR):
                    yj = yc[:, j % 2, :]
                    e.wait_ge(vst, V * (j + 1))
                    e.tensor_tensor(yj, yj, self.mixed[:, j, :], ALU.add).then_inc(gated, 1)
                    e.wait_ge(gated, 2 * j + 1)
                    e.tensor_tensor(self.mixed[:, j, :], yj, self.mixed[:, NPAIR + j, :], ALU.mult).then_inc(gated, 1)
                e.wait_ge(gated, 2 * NPAIR)

    def merge(self):
        i = self.i
        rwT, outT = self.mixed[:, 0:NPAIR, :], self.mixed[:, NPAIR:NPAIR + KT, :]
        with self.stage() as (c, block):
            WK = KT + 2 * NPAIR
            w = self.sb(c, "w_merge", [P, 2, WK, P])
            gb = self.sb(c, "b_gate", [P, KT, 2])
            bcol = self.sb(c, "b_gate_now", [P, 2, 2])
            sg = self.sb(c, "sig", [P, 2, CW])
            gate_b = self.sb(c, "gate_b", [P, 2, T])
            halves = self.sb(c, "gated", [P, 2, 2, CW])
            ps = self.ps(c, "ps_merge", [P, 2, 3, 512])
            gate_in = self.sems("gate_in0", "gate_in1")
            wo_in, = self.sems("w_o_in")
            b_in, prod, bcp, sgd, gated, summed = self.sems("bg_in", "mprod", "bcp", "sgd", "gated", "summed")
            w_in = self.sems("wm_in0", "wm_in1")

            @block.sync
            def _(e):
                e.dma_start(gb[:], i["b_gate"]).then_inc(b_in, 16)
                with e.Fori(0, KT // 2) as t:
                    for s in range(2):
                        tile = ds(2 * t + s, 1)
                        e.wait_ge(prod, NC * (2 * t + s) + 1)
                        for to, of in ((slice(0, KT), slice(0, KT)), (slice(KT, WK), slice(2 * KT, KT + WK))):
                            e.dma_start(w[:, s, to, :], i["w_merge"][tile, :, of, :].rearrange("o p k f -> (o p) k f")
                                        ).then_inc(w_in[s], 16)
                        e.wait_ge(gated, 2 * NC * (2 * t + s) + 1)
                        e.dma_start(gate_b[:, s, :], self.gate_d[tile].rearrange("o p t -> (o p) t")
                                    ).then_inc(gate_in[s], 16)
                e.dma_start(self.w_o[:], i["w_o"].rearrange("(k p) f -> p k f", p=P)).then_inc(wo_in, 16)
                e.wait_ge(wo_in, 16)

            @block.tensor
            def _(e):
                e.sem_inc(prod, NC + 1)
                with e.Fori(0, KT // 2) as t:
                    for s in range(2):
                        e.wait_ge(w_in[s], 32 * (t + 1))
                        for n in range(NC):
                            u = (2 * t + s) * NC + n
                            z = (s * NC + n) % 2
                            e.wait_ge(gated, 2 * (u + NC - 1) + 1)
                            cols = slice(n * CW, (n + 1) * CW)
                            k0 = 0
                            for m, (rhs, K) in enumerate(((self.hT, KT), (self.attT, NPAIR),
                                                          (rwT, NPAIR))):
                                for k in range(K):
                                    mm = e.matmul(ps[:, z, m, 0:CW], w[:, s, k0 + k, :], rhs[:, k, cols],
                                                  start=(k == 0), stop=(k == K - 1))
                                k0 += K
                            mm.then_inc(prod, 1)

            @block.scalar
            def _(e):
                e.wait_ge(b_in, 16)
                with e.Fori(0, KT // 2) as t:
                    for s in range(2):
                        e.copy(bcol[:, s, :], gb[:, ds(2 * t + s, 1), :].rearrange("p o f -> p (o f)")
                               ).then_inc(bcp, 1)
                        e.wait_ge(bcp, 2 * t + s + 1)
                        for n in range(NC):
                            u = (2 * t + s) * NC + n
                            z = (s * NC + n) % 2
                            e.wait_ge(prod, NC + u + 2)
                            e.wait_ge(gated, 2 * (u + NC - 1) + 1)
                            e.activation(sg[:, z, :], ps[:, z, 0, 0:CW], ACT.Sigmoid, bias=bcol[:, s, 0:1]
                                         ).then_inc(sgd, 1)

            @block.vector
            def _(e):
                e.sem_inc(gated, 2 * NC + 1)
                with e.Fori(0, KT // 2) as t:
                    for s in range(2):
                        for n in range(NC):
                            u = (2 * t + s) * NC + n
                            z = (s * NC + n) % 2
                            if n == 0:
                                e.wait_ge(gate_in[s], 16 * (t + 1))
                            e.wait_ge(sgd, u + 1)
                            e.wait_ge(summed, u + 1)
                            for m, gate in enumerate((sg[:, z, :], gate_b[:, s, n * CW:(n + 1) * CW])):
                                e.tensor_tensor(halves[:, z, m, :], gate, ps[:, z, 1 + m, 0:CW], ALU.mult
                                                ).then_inc(gated, 1)

            @block.gpsimd
            def _(e):
                e.sem_inc(summed, 2)
                with e.Fori(0, KT // 2) as t:
                    for s in range(2):
                        for n in range(NC):
                            u = (2 * t + s) * NC + n
                            z = (s * NC + n) % 2
                            e.wait_ge(gated, 2 * (u + 1 + NC) + 1)
                            e.tensor_tensor(outT[:, ds(2 * t + s, 1), n * CW:(n + 1) * CW].rearrange("p o f -> p (o f)"),
                                            halves[:, z, 0, :], halves[:, z, 1, :], ALU.add).then_inc(summed, 1)

    def output_projection(self):
        i = self.i
        merged = self.mixed[:, NPAIR:NPAIR + KT, :]
        with self.stage() as (c, block):
            w = self.w_o
            g = self.sb(c, "g2row", [P, D])
            epsc = self.sb(c, "eps2", [P, 1])
            x = self.sb(c, "x_rows", [P, 2, D])
            h = self.sb(c, "h_rows", [P, 2, D])
            sq = self.sb(c, "sq2", [P, D])
            col = self.sb(c, "col2", [P, 2, 2])
            ps = self.ps(c, "ps_o", [P, 2, 2, 512])
            g_in, eps_set, prod, x1d, ssd, rootd, vst, hd = self.sems(
                "g2_in", "eps2_set", "oprod", "x1_done", "ssd", "root2", "v2", "h2_done")
            x_in = self.sems("xr_in0", "xr_in1")
            x1_out = self.sems("x1_out0", "x1_out1")
            h2_out = self.sems("h2_out0", "h2_out1")

            @block.sync
            def _(e):
                e.dma_start(g[:], i["norm2_g"].to_broadcast([P, D])).then_inc(g_in, 16)
                for m in range(TT):
                    n, s = tokens_in(m), m % 2
                    if m >= 2:
                        e.wait_ge(x1_out[s], 16 * (m // 2))
                        e.wait_ge(hd, m - 1)
                        e.wait_ge(ssd, m - 1)
                    e.dma_start(x[0:n, s, :], i["x"][m * P:m * P + n, :]).then_inc(x_in[s], 16)

            @block.tensor
            def _(e):
                def product(m):
                    n, s = tokens_in(m), m % 2
                    if m >= 2:
                        e.wait_ge(x1d, m - 1)
                    for k in range(KT):
                        for d in range(2):
                            mm = e.matmul(ps[0:n, s, d, :], merged[:, k, m * P:m * P + n],
                                          w[:, k, d * 512:(d + 1) * 512], start=(k == 0), stop=(k == KT - 1))
                    mm.then_inc(prod, 1)

                for m in range(TT):
                    product(m)

            @block.scalar
            def _(e):
                e.wait_ge(eps_set, 1)
                for m in range(TT):
                    n, s = tokens_in(m), m % 2
                    e.wait_ge(x1d, m + 1)
                    if m:
                        e.wait_ge(ssd, m)
                    e.activation(sq[0:n, :], x[0:n, s, :], ACT.Square, accum_out=col[0:n, s, 0:1]).then_inc(ssd, 1)
                    e.wait_ge(ssd, m + 1)
                    e.activation(col[0:n, s, 1:2], col[0:n, s, 0:1], ACT.Sqrt, bias=epsc[0:n, :], scale=1.0 / D
                                 ).then_inc(rootd, 1)
                    e.dma_start(self.x1_d[m * P:m * P + n, :], x[0:n, s, :]).then_inc(x1_out[s], 16)
                    e.wait_ge(hd, m + 1)
                    e.dma_start(self.h2_d[m * P:m * P + n, :], h[0:n, s, :]).then_inc(h2_out[s], 16)
                for q in (x1_out, h2_out):
                    e.wait_ge(q[0], 16 * ((TT + 1) // 2))
                    e.wait_ge(q[1], 16 * (TT // 2))

            @block.vector
            def _(e):
                e.memset(epsc[:], EPS).then_inc(eps_set, 1)
                e.wait_ge(g_in, 16)
                for m in range(TT):
                    n, s = tokens_in(m), m % 2
                    e.wait_ge(prod, m + 1)
                    e.wait_ge(x_in[s], 16 * (m // 2 + 1))
                    e.tensor_tensor(x[0:n, s, :], ps[0:n, s, :, :].rearrange("p a b -> p (a b)"), x[0:n, s, :], ALU.add
                                    ).then_inc(x1d, 1)
                    e.wait_ge(rootd, m + 1)
                    e.reciprocal(col[0:n, s, 1:2], col[0:n, s, 1:2]).then_inc(vst, 1)
                    e.wait_ge(vst, m + 1)
                    if m >= 2:
                        e.wait_ge(h2_out[s], 16 * (m // 2))
                    e.scalar_tensor_tensor(out=h[0:n, s, :], in0=x[0:n, s, :], scalar=col[0:n, s, 1:2],
                                           in1=g[0:n, :], op0=ALU.mult, op1=ALU.mult).then_inc(hd, 1)

    def experts(self):
        i, o = self.i, self.o
        RING, G = TOPK // 2, 4
        NG = TOPK // G
        PT = TP // P
        HU = P // TS
        DU = PH // HU
        NU = PT * PH + DU
        with self.stage() as (c, block):
            ring = self.sb(c, "ring", [P, RING, 2 * D])
            hrow = self.sb(c, "h2_tile", [P, D])
            hnext = self.sb(c, "h2_next", [P, D])
            xrow = self.sb(c, "x1_tile", [P, D])
            grow = self.sb(c, "gf_row", [P, D])
            epsc = self.sb(c, "eps3", [P, 1])
            wq = self.sb(c, "w_query", [P, KT, PH * 2 * P])
            sk = self.sb(c, "sub_keys", [P, NHALF, NKEY])
            h2T = self.sb(c, "h2T", [P, KT, P])
            q = self.sb(c, "query", [P, 2 * P])
            qT = self.sb(c, "queryT", [P, 2, P])
            fold = self.sb(c, "fold", [P, TS])
            sc = self.sb(c, "s_unit", [P, 2, 2, NKEY])
            sm = self.sb(c, "s_left", [P, 2, NKEY])
            sv = self.sb(c, "top_s", [P, 2, TOPK])
            si = self.sb(c, "top_i", [P, 2, TOPK], U32)
            sif = self.sb(c, "top_if", [P, 2, TOPK])
            cand = self.sb(c, "cand", [P, TOPK * TOPK])
            cleft = self.sb(c, "cand_left", [P, TOPK * TOPK])
            bs = self.sb(c, "best_s", [P, TOPK])
            bp = self.sb(c, "best_pos", [P, TOPK], U32)
            ranks = self.sb(c, "ranks", [P, 2, TOPK], U32)
            ranksf = self.sb(c, "ranks_f", [P, 2, TOPK])
            iota = self.sb(c, "iota", [P, TOPK])
            hot = self.sb(c, "hot", [P, 2, TOPK, TOPK])
            pick = self.sb(c, "pick", [P, 2, TOPK])
            idx = self.sb(c, "expert_id", [P, 2, TOPK], U32)
            nmax = self.sb(c, "neg_max", [P, 1])
            ex = self.sb(c, "exp_s", [P, 2, TOPK])
            den = self.sb(c, "gate_den", [P, 2, 1])
            gate = self.sb(c, "gate", [P, 2, TOPK])
            dot = self.sb(c, "dots", [P, 2, TOPK])
            act = self.sb(c, "acts", [P, 2, TOPK])
            wt = self.sb(c, "weights", [P, 2, TOPK])
            diag = self.sb(c, "diag", [P, 2 * G, P])
            zero = self.sb(c, "zero", [P, P])
            x2 = self.sb(c, "x2", [P, D])
            sq = self.sb(c, "sq3", [P, D])
            col = self.sb(c, "col3", [P, 2])
            yrow = self.sb(c, "y_tile", [P, D])
            acc = self.ps(c, "acc", [P, 2, 512])
            pq = self.ps(c, "ps_query", [P, HU, 2 * P])
            psc = self.ps(c, "ps_score", [P, HU, 2 * NKEY])
            pt = self.ps(c, "ps_turned", [P, 2, 4, P])
            (passed, c_in, const_set, found, idx_d, exp_d, gate_d, dots, gelu, wtd, diagd, pv, accd, x2d, ssd, rootd,
             norm_d, yd, y_out) = self.sems(
                "passed", "c3_in", "const3_set", "topk", "idx_done", "exp_done", "gate_done", "dots_done", "gelu_done",
                "wt_done", "diag_done", "v_used", "acc_done", "x2_done", "ss3", "root3", "norm3", "y_done", "y_out")
            sk_in, h_t, h2T_c, q_d, q_c, q_t, qT_c, s_d, sc_c = self.sems(
                "sk_in", "h2_turned", "h2T_copied", "query_done", "query_copied", "query_turned", "queryT_copied",
                "scores_done", "scores_copied")
            w_in = self.sems("wq_first_in", "wq_rest_in")
            h_in, x_in, h_c = self.sems("hr_in", "x1r_in", "h2_copied")
            uv_in = self.sems(*[f"uv_in{n}" for n in range(RING)])
            KEYS, PAIRS, FOUND = 11, 7, 26

            @block.sync
            def _(e):
                e.dma_start(grow[:], i["final_g"].to_broadcast([P, D])).then_inc(c_in, 16)
                e.dma_start(iota[:], i["iota"].to_broadcast([P, TOPK])).then_inc(c_in, 16)
                e.dma_start(fold[:], i["fold"]).then_inc(c_in, 16)

                def tile_rows(m, first):
                    decode = isinstance(m, int) and m == PT
                    for n in range(HU):
                        row = first + (0 if decode else n * TS)
                        e.dma_start(hnext[n * TS:(n + 1) * TS, :], self.h2_d[ds(row, TS), :]).then_inc(h_in, 16)
                    n = TS if decode else P
                    return lambda: e.dma_start(xrow[0:n, :], self.x1_d[ds(first, n), :]).then_inc(x_in, 16)

                def follow(m, first):
                    e.wait_ge(h_c, m + 1)
                    x_rows = tile_rows(m + 1, first)
                    e.wait_ge(pv, TOPK * (PH * m + 1) + 1)
                    x_rows()

                x_rows = tile_rows(0, 0)
                first = 2 * 2 * P
                e.dma_start(sk[:], i["sub_keys"]).then_inc(sk_in, 16)
                for cols, loaded in ((slice(0, first), w_in[0]), (slice(first, None), w_in[1])):
                    e.dma_start(wq[:, :, cols], i["w_query"][:, cols].rearrange("(k p) f -> p k f", p=P)
                                ).then_inc(loaded, 16)
                x_rows()
                with e.Fori(0, PT - 1) as m:
                    follow(m, (m + 1) * P)
                follow(PT - 1, TP)

            @block.gpsimd
            def _(e):
                with e.Fori(0, NU // 2) as t:
                    for z in range(2):
                        u = 2 * t + z
                        e.wait_ge(idx_d, u + 1)
                        for k in range(TOPK):
                            e.wait_ge(pv, TOPK * u + k + TOPK - RING + 1)
                            e.sem_inc(passed, 1)
                            e.indirect_dma_start(out=ring[:, k % RING, :], out_offset=None, in_=i["uv"],
                                                 in_offset=bass.IndirectOffsetOnAxis(ap=idx[:, z, k:k + 1], axis=0)
                                                 ).then_inc(uv_in[k % RING], 16)

            @block.vector
            def _(e):
                e.memset(epsc[:], EPS).then_inc(const_set, 1)
                e.memset(zero[:], 0.0).then_inc(const_set, 1)

                def find_keys(u, z):
                    ch = Chain(e, found, FOUND * u)
                    e.wait_ge(sc_c, HU * (u + 1))
                    e.sem_inc(passed, 1)
                    for half in range(2):
                        ch(e.max(out=sv[:, half, 0:8], in_=sc[:, z, half, :]))
                    ch.settle()
                    e.sem_inc(passed, 1)
                    for half in range(2):
                        ch(e.max_index(out=si[:, half, 0:8], in_max=sv[:, half, 0:8], in_values=sc[:, z, half, :]))
                        ch(e.match_replace(out=sm[:, half, :], in_to_replace=sv[:, half, 0:8],
                                           in_values=sc[:, z, half, :], imm_value=-3.0e38))
                    ch.settle()
                    e.sem_inc(passed, 1)
                    for half in range(2):
                        ch(e.max(out=sv[:, half, 8:16], in_=sm[:, half, :]))
                    ch.settle()
                    e.sem_inc(passed, 1)
                    for half in range(2):
                        ch(e.max_index(out=si[:, half, 8:16], in_max=sv[:, half, 8:16], in_values=sm[:, half, :]))
                    ch(e.tensor_tensor(cand[:].rearrange("p (a b) -> p a b", a=TOPK),
                                       sv[:, 0, :].unsqueeze(2).to_broadcast([P, TOPK, TOPK]),
                                       sv[:, 1, :].unsqueeze(1).to_broadcast([P, TOPK, TOPK]), ALU.add))
                    assert ch.n == KEYS

                def find_pairs(u):
                    ch = Chain(e, found, FOUND * u + KEYS)
                    ch.settle()
                    ch(e.tensor_copy(sif[:], si[:]))
                    ch(e.max(out=bs[:, 0:8], in_=cand[:]))
                    ch.settle()
                    ch(e.tensor_scalar(nmax[:], bs[:, 0:1], -1.0, None, ALU.mult))
                    ch(e.max_index(out=bp[:, 0:8], in_max=bs[:, 0:8], in_values=cand[:]))
                    ch(e.match_replace(out=cleft[:], in_to_replace=bs[:, 0:8], in_values=cand[:], imm_value=-3.0e38))
                    ch.settle()
                    e.sem_inc(passed, 1)
                    ch(e.max(out=bs[:, 8:16], in_=cleft[:]))
                    ch.settle()
                    e.sem_inc(passed, 1)
                    ch(e.max_index(out=bp[:, 8:16], in_max=bs[:, 8:16], in_values=cleft[:]))
                    assert ch.n == PAIRS

                def find_ids(u, z):
                    ch = Chain(e, found, FOUND * u + KEYS + PAIRS)
                    ch.settle()
                    ch(e.tensor_scalar(ranks[:, 0, :], bp[:], 4, None, ALU.logical_shift_right))
                    ch(e.tensor_scalar(ranks[:, 1, :], bp[:], 15, None, ALU.bitwise_and))
                    ch.settle()
                    ch(e.tensor_copy(ranksf[:], ranks[:]))
                    ch.settle()
                    for half in range(2):
                        ch(e.tensor_tensor(hot[:, half], ranksf[:, half, :].unsqueeze(2).to_broadcast([P, TOPK, TOPK]),
                                           iota[:].unsqueeze(1).to_broadcast([P, TOPK, TOPK]), ALU.is_equal))
                    ch.settle()
                    ch(e.tensor_tensor(hot[:], hot[:], sif[:].unsqueeze(2).to_broadcast([P, 2, TOPK, TOPK]), ALU.mult))
                    ch.settle()
                    ch(e.tensor_reduce(pick[:], hot[:], AX.X, ALU.add))
                    ch.settle()
                    ch(e.scalar_tensor_tensor(out=idx[:, z, :], in0=pick[:, 0, :], scalar=float(NKEY),
                                              in1=pick[:, 1, :], op0=ALU.mult, op1=ALU.add))
                    assert KEYS + PAIRS + ch.n == FOUND
                    ch.settle()
                    e.sem_inc(idx_d, 1)

                def unit(u, z, rows=None, norm=None, last=False):
                    e.wait_ge(exp_d, u + 1)
                    e.reciprocal(den[:, z, :], den[:, z, :]).then_inc(gate_d, 1)
                    e.wait_ge(gate_d, 2 * u + 1)
                    e.tensor_scalar(gate[:, z, :], ex[:, z, :], den[:, z, :], None, ALU.mult).then_inc(gate_d, 1)
                    if rows is not None:
                        e.wait_ge(h_c, rows)
                    for g in range(NG):
                        for k in range(G * g, G * (g + 1)):
                            e.wait_ge(uv_in[k % RING], 16 * (TOPK // RING * u + k // RING + 1))
                            mm = e.tensor_tensor_reduce(ring[:, k % RING, 0:D], ring[:, k % RING, 0:D], hrow[:], 1.0, 0.0,
                                                        ALU.mult, ALU.add, dot[:, z, k:k + 1])
                        mm.then_inc(dots, 1)
                        if g == 0 and norm is not None:
                            last_norm(norm, P)
                        e.wait_ge(gelu, NG * u + g + 1)
                        ks = slice(G * g, G * (g + 1))
                        e.tensor_tensor(wt[:, z, ks], act[:, z, ks], gate[:, z, ks], ALU.mult).then_inc(wtd, 1)
                        if not last:
                            if g == 0:
                                find_keys(u + 1, 1 - z)
                            if g == 1:
                                find_pairs(u + 1)
                            if g == 2:
                                find_ids(u + 1, 1 - z)

                def last_norm(m, n):
                    e.wait_ge(rootd, m + 1)
                    e.reciprocal(col[0:n, 1:2], col[0:n, 1:2]).then_inc(norm_d, 1)
                    e.wait_ge(norm_d, m + 1)
                    e.wait_ge(y_out, 16 * m + 16)
                    e.scalar_tensor_tensor(out=yrow[0:n, :], in0=x2[0:n, :], scalar=col[0:n, 1:2], in1=grow[0:n, :],
                                           op0=ALU.mult, op1=ALU.mult).then_inc(yd, 1)

                e.wait_ge(c_in, 48)
                e.sem_inc(yd, 1)
                find_keys(0, 0)
                find_pairs(0)
                find_ids(0, 0)
                unit(0, 0, rows=1)
                with e.Fori(0, PT) as m:
                    unit(PH * m + 1, 1)
                    with e.Fori(1, PH // 2) as hh:
                        unit(PH * m + 2 * hh, 0)
                        unit(PH * m + 2 * hh + 1, 1)
                    unit(PH * (m + 1), 0, rows=m + 2, norm=m)
                for u in range(PT * PH + 1, NU):
                    unit(u, u % 2, last=u + 1 == NU)
                last_norm(PT, TS)

            @block.scalar
            def _(e):
                e.wait_ge(const_set, 2)
                e.wait_ge(c_in, 48)

                def exps(u, z):
                    e.wait_ge(idx_d, u + 1)
                    e.activation(ex[:, z, :], bs[:], ACT.Exp, bias=nmax[:], accum_out=den[:, z, :]).then_inc(exp_d, 1)

                def turned(m):
                    for d in range(2):
                        e.wait_ge(h_t, 2 * m + d + 1)
                        e.copy(h2T[:, 4 * d:4 * d + 4, :], pt[:, d, :, :]).then_inc(h2T_c, 1)

                def parts(decode):
                    return [(slice(n * TS, (n + 1) * TS), n) for n in range(HU)] if decode else [(slice(0, P), 0)]

                def scores(step, v, z, decode=False):
                    if step == 0:
                        e.wait_ge(q_d, v + 1)
                        for rows, n in parts(decode):
                            e.copy(q[rows, :], pq[rows, n, :]).then_inc(q_c, 1 if decode else HU)
                    if step == 1:
                        e.wait_ge(q_t, v + 1)
                        e.copy(qT[:], pt[:, 0, 0:2, :]).then_inc(qT_c, 1)
                    if step == 2:
                        e.wait_ge(s_d, v + 1)
                        for rows, n in parts(decode):
                            e.copy(sc[rows, z, :, :], psc[rows, n, :].rearrange("p (a k) -> p a k", a=2)
                                   ).then_inc(sc_c, 1 if decode else HU)

                def unit(u, z, places, ahead=True, last=False):
                    n = P if places is self.ident else TS
                    for g in range(NG):
                        ks = slice(G * g, G * (g + 1))
                        e.wait_ge(dots, NG * u + g + 1)
                        e.activation(act[:, z, ks], dot[:, z, ks], ACT.Gelu).then_inc(gelu, 1)
                        e.wait_ge(wtd, NG * u + g + 1)
                        for k in range(G * g, G * (g + 1)):
                            e.wait_ge(pv, TOPK * u + k + TOPK - 2 * G + 1)
                            e.mul(diag[:, k % (2 * G), 0:n], places[:], wt[:, z, k:k + 1]).then_inc(diagd, 1)
                        if ahead:
                            scores(g, u + 2, z, ahead == "decode")
                    if not last:
                        exps(u + 1, 1 - z)

                def root_mean_square(m, n):
                    e.wait_ge(accd, m + 1)
                    e.wait_ge(yd, m + 1)
                    e.copy(x2[0:n, :], acc[0:n, :, :].rearrange("p a b -> p (a b)")).then_inc(x2d, 1)
                    e.wait_ge(x2d, m + 2)
                    e.activation(sq[0:n, :], x2[0:n, :], ACT.Square, accum_out=col[0:n, 0:1]).then_inc(ssd, 1)
                    e.wait_ge(ssd, m + 1)
                    e.activation(col[0:n, 1:2], col[0:n, 0:1], ACT.Sqrt, bias=epsc[0:n], scale=1.0 / D
                                 ).then_inc(rootd, 1)

                def copy_rows(m):
                    e.wait_ge(h_in, 16 * HU * (m + 1))
                    e.copy(hrow[:], hnext[:]).then_inc(h_c, 1)

                def store(m, n, row):
                    e.wait_ge(yd, m + 2)
                    e.dma_start(o["y"][ds(row, n), :], yrow[0:n, :]).then_inc(y_out, 16)

                def tile(m, ahead):
                    with e.Fori(0, PH // 2 - 1) as hh:
                        for z in range(2):
                            unit(m * PH + 2 * hh + z, z, self.ident)
                    turned(m + 1)
                    for z in range(2):
                        unit(m * PH + PH - 2 + z, z, self.ident, ahead)
                    copy_rows(m + 1)
                    root_mean_square(m, P)
                    store(m, P, m * P)

                e.sem_inc(x2d, 1)
                e.sem_inc(y_out, 16)
                turned(0)
                for v in range(2):
                    for step in range(3):
                        scores(step, v, v)
                exps(0, 0)
                copy_rows(0)
                with e.Fori(0, PT - 1) as m:
                    tile(m, True)
                tile(PT - 1, "decode")
                for u in range(PT * PH, NU):
                    unit(u, u % 2, fold, False, u == NU - 1)
                root_mean_square(PT, TS)
                store(PT, TS, TP)
                e.wait_ge(y_out, 16 * (PT + 1) + 16)

            @block.tensor
            def _(e):
                def begin(m, n):
                    e.wait_ge(x_in, 16 * (m + 1))
                    e.wait_ge(x2d, m + 1)
                    for d in range(2):
                        e.matmul(acc[0:n, d, :], self.ident[0:n, 0:n], xrow[0:n, d * 512:(d + 1) * 512],
                                 start=True, stop=False)

                def turn(m):
                    e.wait_ge(h_in, 16 * HU * (m + 1))
                    for d in range(2):
                        for k in range(4):
                            mm = e.transpose(pt[:, d, k, :], hnext[:, (4 * d + k) * P:(4 * d + k + 1) * P],
                                             self.ident[:])
                        mm.then_inc(h_t, 1)

                def scores(step, v, heads):
                    if step == 0:
                        for n, h in enumerate(heads):
                            for k in range(KT):
                                mm = e.matmul(pq[:, n, :], h2T[:, k, :], wq[:, k, ds(h * (2 * P), 2 * P)],
                                              start=(k == 0), stop=(k == KT - 1))
                        mm.then_inc(q_d, 1)
                    if step == 1:
                        e.wait_ge(q_c, HU * (v + 1))
                        for a in range(2):
                            mm = e.transpose(pt[:, 0, a, :], q[:, a * P:(a + 1) * P], self.ident[:])
                        mm.then_inc(q_t, 1)
                    if step == 2:
                        e.wait_ge(qT_c, v + 1)
                        for n, h in enumerate(heads):
                            for a in range(2):
                                mm = e.matmul(psc[:, n, a * NKEY:(a + 1) * NKEY], qT[:, a, :],
                                              sk[:, ds(2 * h + a, 1), :].rearrange("p o k -> p (o k)"),
                                              start=True, stop=True)
                        mm.then_inc(s_d, 1)

                def unit(u, n, heads=None):
                    for k in range(TOPK):
                        if heads is not None and k % G == 0 and k // G < 3:
                            scores(k // G, u + 2, heads)
                        e.wait_ge(diagd, TOPK * u + k + 1)
                        for d in range(2):
                            mm = e.matmul(acc[0:n, d, :], diag[:, k % (2 * G), 0:n],
                                          ring[:, k % RING, D + d * 512:D + (d + 1) * 512], start=False, stop=False)
                        mm.then_inc(pv, 1)

                def end(n):
                    for d in range(2):
                        mm = e.matmul(acc[0:n, d, :], zero[0:n, 0:n], grow[0:n, d * 512:(d + 1) * 512],
                                      start=False, stop=True)
                    mm.then_inc(accd, 1)

                e.wait_ge(const_set, 2)
                e.wait_ge(c_in, 48)
                e.sem_inc(pv, TOPK)
                turn(0)
                e.wait_ge(h2T_c, 2)
                e.wait_ge(w_in[0], 16)
                e.wait_ge(sk_in, 16)
                for v in range(2):
                    for step in range(3):
                        scores(step, v, [v])
                e.wait_ge(w_in[1], 16)

                def tile(m, decode=False):
                    begin(m, P)
                    with e.Fori(0, PH // 2 - 1) as hh:
                        for z in range(2):
                            unit(m * PH + 2 * hh + z, P, [2 * hh + z + 2])
                    e.wait_ge(qT_c, PH * (m + 1))
                    turn(m + 1)
                    e.wait_ge(h2T_c, 2 * (m + 2))
                    for z in range(2):
                        unit(m * PH + PH - 2 + z, P, range(HU * z, HU * (z + 1)) if decode else [z])
                    end(P)

                with e.Fori(0, PT - 1) as m:
                    tile(m)
                tile(PT - 1, decode=True)
                begin(PT, TS)
                for u in range(PT * PH, NU):
                    unit(u, TS)
                end(TS)


def layout(inp):
    a = {k: np.ascontiguousarray(v) for k, v in inp.items()}
    f = np.float32
    eye = np.eye(P, dtype=f)
    head = np.kron(np.eye(2, dtype=f), np.ones((HD, HD), f))
    x = np.concatenate([a["x_prompt"].reshape(TP, D), a["x_sample"].reshape(TS, D)])
    w_in = a["w_in"][0]
    main = slice(OFF_B, OFF_B + 3 * RW)
    lora = slice(OFF_B + 3 * RW, OFF_G)
    tiles = lambda v: v.reshape(-1, P).T

    def loras(v):
        v = np.moveaxis(v, -1, 0)
        out = np.zeros((LG, 3) + v.shape[1:], f)
        for m, (off, n) in enumerate(((0, LW), (LW, LA), (LW + LA, LG))):
            out[:n, m] = v[off:off + n]
        return out

    pos = np.concatenate([np.arange(TP), np.tile(8192 + np.arange(NS), NB)]).astype(f)
    pos = np.concatenate([pos, np.zeros(TT * P - T, f)])
    angle = pos[:, None] * (f(500000.0) ** (-np.arange(RH, dtype=f) / f(RH)))[None, :]
    rope = [fn(angle).astype(f).reshape(TT, P, RH).transpose(1, 0, 2) for fn in (np.cos, np.sin)]
    diff = WIN + np.arange(WIN)[:, None] - np.arange(2 * WIN)[None, :]
    seen = (diff >= 0) & (diff < WIN)
    band = np.where(seen, f(0), f(NEG))
    first = np.where(seen & (np.arange(2 * WIN) >= WIN)[None, :], f(0), f(NEG))
    row_b, row_n = (np.tile(z, NQ // NKV)[:, None] for z in (np.repeat(np.arange(NB), NS), np.tile(np.arange(NS), NB)))
    key_b = np.concatenate([np.repeat(np.arange(NB), WIN), np.repeat(np.arange(NB), NS)])[None, :]
    key_j = np.concatenate([np.tile(np.arange(WIN), NB), WIN + np.tile(np.arange(NS), NB)])[None, :]
    ddiff = WIN + row_n - key_j
    dmask = np.where((row_b == key_b) & (ddiff >= 0) & (ddiff < WIN), f(0), f(NEG))
    ct = np.tile(np.arange(CH), 2)
    levels = []
    for n in range(LEVELS):
        half = 1 << n
        same = ct[:, None] // (2 * half) == ct[None, :] // (2 * half)
        levels.append((head * same * ((ct // half) % 2 == 0)[:, None] * ((ct // half) % 2 == 1)[None, :]).astype(f))
    db, dn = np.tile(np.repeat(np.arange(NB), NS), 2), np.tile(np.arange(NS), 2 * NB)
    dh = np.repeat(np.arange(2), TS)
    dsame = (db[:, None] == db[None, :]) & (dh[:, None] == dh[None, :])
    dl0 = dsame & (dn[:, None] // 2 == dn[None, :] // 2) & (dn[:, None] < dn[None, :])
    dl1 = dsame & (dn[:, None] < 2) & (dn[None, :] >= 2)
    state0 = np.zeros((2, HD, NPAIR, NB, 2, HD), f)
    start = a["state_wkv"][0].reshape(NB, NPAIR, 2, HD, HD)
    for h in range(2):
        state0[h, :, :, :, h, :] = start[:, :, h].transpose(3, 1, 0, 2)
    state0 = state0.reshape(P, NPAIR, NB, P)
    blocks = lambda w: w.reshape(-1, P, w.shape[1] // P, P).transpose(2, 1, 0, 3)
    pairs = lambda w: w.reshape(w.shape[0], NPAIR, P).transpose(1, 0, 2)
    mu, b_in, sh = a["shift_mu"][0], a["b_in"][0], a["state_shift"][0]
    return {
        "ident": eye, "ones": np.ones((P, P), f), "headones": head,
        "xT": x.T, "x": x,
        "norm1_g": tiles(a["norm1_g"][0]),
        "w_in": w_in, "b_qkv": b_in[None, :QKV],
        "w_main": w_in[:, main].reshape(KT, P, NMAIN, P).transpose(2, 1, 0, 3),
        "w_lora": w_in[:, lora].reshape(KT, P, -1).transpose(1, 0, 2),
        "b_main": tiles(b_in[main]), "mu_main": tiles(mu[:3 * RW]),
        "shift_main": sh[:, :3 * RW].reshape(NB, NMAIN, P).transpose(2, 1, 0),
        "lora_b": loras(b_in[lora]), "lora_mu": loras(mu[3 * RW:]),
        "lora_shift": loras(sh[:, 3 * RW:]),
        "cos": rope[0], "sin": rope[1], "band": band, "band_first": first,
        "sinks": a["attn_sinks"].reshape(NKV, 2, 2).transpose(0, 2, 1).reshape(1, NQ),
        "cache_k": a["cache_win_k"].reshape(NB, WIN, KW), "cache_v": a["cache_win_v"].reshape(NB, WIN, KW),
        "w2": pairs(a["w2"][0]), "a2": pairs(a["a2"][0]), "g2": pairs(a["g2"][0]),
        "pair_par": np.stack([a[n][0].reshape(NPAIR, P) for n in ("w0", "a0", "k_k", "k_a", "r_k")], axis=-1),
        "level_masks": np.stack(levels, axis=1), "low0": levels[0].T,
        "before": (head * (ct[:, None] < ct[None, :])).astype(f),
        "upto": np.stack([(ct[:, None] <= np.arange(CH)[None, :])] * 2, axis=1).astype(f),
        "dec_masks": np.stack([dsame * (dn[:, None] < dn[None, :]), dl0, dl1, dl0.T], axis=1).astype(f),
        "dec_upto": np.stack([(db[:, None] == db[None, :TS]) & (dn[:, None] <= dn[None, :TS])] * 2, axis=1).astype(f),
        "dec_own": (db[:, None] == np.arange(NB)[None, :]).astype(f),
        "state0": state0,
        "gn_par": np.stack([tiles(a["ln_x_w"][0]), tiles(a["ln_x_b"][0])], axis=1),
        "w_merge": np.concatenate([blocks(w_in[:, OFF_G:OFF_G + D]), blocks(w_in[:, OFF_G + D:]),
                                   blocks(a["w_up_a"][0]), blocks(a["w_up_b"][0])], axis=2),
        "b_gate": b_in[OFF_G:].reshape(2, KT, P).transpose(2, 1, 0),
        "w_o": a["w_o"][0], "norm2_g": a["norm2_g"], "final_g": a["final_norm_g"][None],
        "w_query": a["w_query"][0],
        "sub_keys": a["sub_keys"][0].reshape(NHALF, NKEY, P).transpose(2, 0, 1),
        "uv": np.concatenate([a["expert_u"][0], a["expert_v"][0]], axis=1),
        "fold": np.tile(np.eye(TS, dtype=f), (P // TS, 1)),
        "iota": np.arange(TOPK, dtype=f)[None],
        "dmask": dmask, "dsink": np.repeat(a["attn_sinks"].reshape(NKV, NQ // NKV), TS, axis=1).T,
    }


OUTS = {"y": (T, D), "prompt_win_k": (WIN, KW), "prompt_win_v": (WIN, KW), "prompt_wkv": (NQ, HD, HD),
        "shift": (1 + NB, OFF_G - OFF_B), "sample_win_k": (NB, WIN, KW), "sample_win_v": (NB, WIN, KW),
        "sample_wkv": (NB, NQ, HD, HD)}


def kernel(**inputs):
    import concourse.bacc as _bacc
    from concourse.bass_utils import run_bass_kernel_spmd as _run

    nc = _bacc.Bacc("TRN2", target_bir_lowering=False, num_devices=1)
    arrays, ins, outs = {}, {}, {}
    for name, array in layout(inputs).items():
        array = np.ascontiguousarray(array)
        arrays[f"in_{name}_dram"] = array
        ins[name] = nc.dram_tensor(f"in_{name}_dram", array.shape, mybir.dt.from_np(array.dtype),
                                   kind="ExternalInput").ap()
    for name, shape in OUTS.items():
        outs[name] = nc.dram_tensor(f"out_{name}_dram", shape, F32, kind="ExternalOutput").ap()
    Program(nc, ins, outs).build()
    r = _run(nc, [arrays], core_ids=[0])
    got = {name: np.asarray(r.results[0][f"out_{name}_dram"]) for name in OUTS}
    win = lambda name, *lead: got[name].reshape(lead + (WIN, NKV, HD))
    wkv = lambda name, *lead: np.ascontiguousarray(got[name].reshape(lead + (NQ, HD, HD)).swapaxes(-1, -2))
    return (got["y"][:TP].reshape(1, TP, D), got["y"][TP:].reshape(NB, NS, D),
            win("prompt_win_k", 1, 1), win("prompt_win_v", 1, 1), wkv("prompt_wkv", 1, 1), got["shift"][None, :1],
            win("sample_win_k", 1, NB), win("sample_win_v", 1, NB), wkv("sample_wkv", 1, NB), got["shift"][None, 1:])
```
